# Optimizing a Trainium2 kernel written in Bass

```python
import jax
import jax.numpy as jnp
from jax import lax
import numpy as np

D_MODEL = 2048
BATCH = 1
SEQ = 512
DEPTH = 2
DEC_BATCH = 8
DEC_SEQ = 1
PAST_LEN = 2048
PAGE_SIZE = 128

N_EVEN = (DEPTH + 1) // 2
N_ODD = DEPTH // 2
EPS = 1e-6
A_WIDTH = D_MODEL // 2
A_HEADS = 8
A_HEAD_DIM = A_WIDTH // A_HEADS
GMLP_CHUNK = 128
B_WIDTH = D_MODEL - A_WIDTH
POOL_WINDOWS = (2, 4, 8, 16)
N_POOL_GROUPS = len(POOL_WINDOWS)
POOL_GROUP = B_WIDTH // N_POOL_GROUPS
POOL_PAD = max(POOL_WINDOWS) - 1
HEAD_DIM = 128
C_HEADS = D_MODEL // HEAD_DIM
C_KV_HEADS = 4
C_REP = C_HEADS // C_KV_HEADS
C_WIDTH = C_HEADS * HEAD_DIM
KV_WIDTH = C_KV_HEADS * HEAD_DIM
CMP_BLOCK = 64
N_SEL = 16
WINDOW = 512
Q_BLOCK = 64
SEL_FORCE = 1e4
NEG_INF = -1e30
ROPE_THETA = 500000.0
ROT_DIM = HEAD_DIM // 4
EVEN_SPLITS = (A_WIDTH, A_WIDTH, A_WIDTH, B_WIDTH, B_WIDTH)
ODD_SPLITS = (C_WIDTH,) + (KV_WIDTH,) * 6 + (3 * C_HEADS, C_WIDTH)
EVEN_IN = sum(EVEN_SPLITS)
ODD_IN = sum(ODD_SPLITS)

kernel_name = 'hybrid_gmlp_pool_nsa_decode_step'

def split_cols(y, sizes):
    idx = np.cumsum(sizes)[:-1].tolist()
    return jnp.split(y, idx, axis=-1)

def rmsnorm(x, g):
    x32 = x.astype(jnp.float32)
    y = x32 * lax.rsqrt(jnp.mean(x32 * x32, axis=-1, keepdims=True) + EPS)
    return (y * g.astype(jnp.float32)).astype(x.dtype)

def rope(x, pos):
    half = ROT_DIM // 2
    inv_freq = ROPE_THETA ** (-jnp.arange(half, dtype=jnp.float32) * (2.0 / ROT_DIM))
    ang = pos.astype(jnp.float32)[:, None] * inv_freq[None, :]
    cos = jnp.cos(ang)[:, None, :]
    sin = jnp.sin(ang)[:, None, :]
    xf = x.astype(jnp.float32)
    x1, x2, rest = xf[..., :half], xf[..., half:ROT_DIM], xf[..., ROT_DIM:]
    return jnp.concatenate([x1 * cos - x2 * sin, x1 * sin + x2 * cos, rest], axis=-1).astype(x.dtype)

def masked_softmax(s, mask):
    p = jax.nn.softmax(jnp.where(mask, s, NEG_INF), axis=-1)
    return p * mask

def gmlp_mix(u, v, w_s, b_s):
    b, t, _ = v.shape
    l = w_s.shape[-1]
    vh = v.reshape(b, t // l, l, A_HEADS, A_HEAD_DIM)
    causal = jnp.tril(jnp.ones((l, l), dtype=bool))
    w = jnp.where(causal, w_s, 0.0)
    s = jnp.einsum('hij,bcjhd->bcihd', w, vh) + b_s.T[None, None, :, :, None]
    return u * s.reshape(b, t, A_WIDTH).astype(u.dtype)

def pool_mix(p, prefix, pos, w_pool, scale):
    b, t, _ = p.shape
    ext = jnp.concatenate([prefix.astype(p.dtype), p], axis=1).astype(jnp.float32)
    cs = jnp.concatenate([jnp.zeros((b, 1, B_WIDTH), jnp.float32), jnp.cumsum(ext, axis=1)], axis=1)
    cur = ext[:, POOL_PAD:]
    groups = []
    for g, w in enumerate(POOL_WINDOWS):
        sl = slice(g * POOL_GROUP, (g + 1) * POOL_GROUP)
        win_sum = cs[:, POOL_PAD + 1:POOL_PAD + 1 + t, sl] - cs[:, POOL_PAD + 1 - w:POOL_PAD + 1 - w + t, sl]
        cnt = jnp.minimum(pos + 1, w).astype(jnp.float32)[None, :, None]
        groups.append(win_sum / cnt - cur[:, :, sl])
    d = jnp.stack(groups, axis=2)
    y = jnp.einsum('btgc,gce->btge', d, w_pool).reshape(b, t, B_WIDTH)
    return (y * scale).astype(p.dtype)

def even_layer(x, pool_prefix, pos, norm_g, w_in, v_gain, w_s, b_s, w_pool, pool_scale, w_out):
    b, t, _ = x.shape
    l = min(t, GMLP_CHUNK)
    h = rmsnorm(x, norm_g)
    u, v, z_a, p, z_b = split_cols(h @ w_in, EVEN_SPLITS)
    v = rmsnorm(v.reshape(b, t, A_HEADS, A_HEAD_DIM), v_gain.reshape(A_HEADS, A_HEAD_DIM)).reshape(b, t, A_WIDTH)
    a = gmlp_mix(u, v, w_s[:, :l, :l], b_s[:, :l]) * jax.nn.silu(z_a)
    m = pool_mix(p, pool_prefix, pos, w_pool, pool_scale) * jax.nn.silu(z_b)
    y = x + (jnp.concatenate([a, m], axis=-1) @ w_out).astype(x.dtype)
    new_pool = jnp.concatenate([pool_prefix.astype(p.dtype), p], axis=1)[:, -POOL_PAD:]
    return y, v, new_pool

def odd_project(x, pos, norm_g, w_in, q_gain, k_gain):
    b, t, _ = x.shape
    h = rmsnorm(x, norm_g)
    q, kc, vc, ks, vs, kw, vw, g, z = split_cols(h @ w_in, ODD_SPLITS)
    q = rope(rmsnorm(q.reshape(b, t, C_HEADS, HEAD_DIM), q_gain), pos)
    q = q.reshape(b, t, C_KV_HEADS, C_REP, HEAD_DIM)
    heads = lambda a: a.reshape(b, t, C_KV_HEADS, HEAD_DIM)
    key = lambda a, i: rope(rmsnorm(heads(a), k_gain[i]), pos)
    kv_cmp = jnp.stack([key(kc, 0), heads(vc)], axis=2)
    kv_sel = jnp.stack([key(ks, 1), heads(vs)], axis=2)
    kv_win = jnp.stack([key(kw, 2), heads(vw)], axis=2)
    gates = jax.nn.sigmoid(g.astype(jnp.float32)).reshape(b, t, C_KV_HEADS, C_REP, 3)
    return q, kv_cmp, kv_sel, kv_win, gates, z

def block_views(kv_cmp, kv_sel):
    b, length = kv_cmp.shape[:2]
    nb = -(-length // CMP_BLOCK)
    pad = nb * CMP_BLOCK - length
    def blocks(a):
        a = jnp.pad(a, ((0, 0), (0, pad), (0, 0), (0, 0), (0, 0)))
        return a.reshape(b, nb, CMP_BLOCK, 2, C_KV_HEADS, HEAD_DIM)
    means = blocks(kv_cmp).astype(jnp.float32).mean(axis=2)
    sel = blocks(kv_sel).transpose(0, 3, 4, 1, 2, 5).reshape(b, 2, C_KV_HEADS, nb, CMP_BLOCK * HEAD_DIM)
    return means[:, :, 0], means[:, :, 1], sel[:, 0], sel[:, 1]

def nsa_core(q, q_pos, kc_blk, vc_blk, ks_g, vs_g, kw, vw, w_pos, gates):
    b, t = q.shape[:2]
    nb = kc_blk.shape[1]
    scale = HEAD_DIM ** -0.5
    blk = jnp.arange(nb)
    s_c = jnp.einsum('btgrd,bngd->bgrtn', q, kc_blk, preferred_element_type=jnp.float32) * scale
    cmp_ok = ((blk + 1) * CMP_BLOCK - 1)[None, :] <= q_pos[:, None]
    p_c = masked_softmax(s_c, cmp_ok)
    o_c = jnp.einsum('bgrtn,bngd->btgrd', p_c, vc_blk)
    cur = q_pos // CMP_BLOCK
    forced = (blk[None, :] == 0) | (blk[None, :] == cur[:, None]) | (blk[None, :] == cur[:, None] - 1)
    imp = jnp.where(blk[None, :] <= cur[:, None], jnp.where(forced, SEL_FORCE, p_c.sum(axis=2)), -1.0)
    n_sel = min(N_SEL, nb)
    top_v, top_i = lax.top_k(imp, n_sel)
    gather = jax.vmap(jax.vmap(lambda a, i: a[i]))
    k_sel = gather(ks_g, top_i).reshape(b, C_KV_HEADS, t, n_sel * CMP_BLOCK, HEAD_DIM)
    v_sel = gather(vs_g, top_i).reshape(b, C_KV_HEADS, t, n_sel * CMP_BLOCK, HEAD_DIM)
    tok = top_i[..., None] * CMP_BLOCK + jnp.arange(CMP_BLOCK)
    sel_ok = (top_v >= 0)[..., None] & (tok <= q_pos[None, None, :, None, None])
    sel_ok = sel_ok.reshape(b, C_KV_HEADS, 1, t, n_sel * CMP_BLOCK)
    s_s = jnp.einsum('btgrd,bgtmd->bgrtm', q, k_sel, preferred_element_type=jnp.float32) * scale
    p_s = masked_softmax(s_s, sel_ok)
    o_s = jnp.einsum('bgrtm,bgtmd->btgrd', p_s, v_sel)
    rel = q_pos[:, None] - w_pos[None, :]
    w_ok = (w_pos[None, :] >= 0) & (rel >= 0) & (rel < WINDOW)
    s_w = jnp.einsum('btgrd,blgd->bgrtl', q, kw, preferred_element_type=jnp.float32) * scale
    p_w = masked_softmax(s_w, w_ok)
    o_w = jnp.einsum('bgrtl,blgd->btgrd', p_w, vw)
    return gates[..., 0:1] * o_c + gates[..., 1:2] * o_s + gates[..., 2:3] * o_w

def nsa_prompt(q, gates, kv_cmp, kv_sel, kv_win):
    b, s = q.shape[:2]
    kc_blk, vc_blk, ks_g, vs_g = block_views(kv_cmp, kv_sel)
    win_pad = jnp.pad(kv_win, ((0, 0), (WINDOW, 0), (0, 0), (0, 0), (0, 0)))
    def one_block(i):
        start = i * Q_BLOCK
        qb = lax.dynamic_slice_in_dim(q, start, Q_BLOCK, axis=1)
        gb = lax.dynamic_slice_in_dim(gates, start, Q_BLOCK, axis=1)
        wb = lax.dynamic_slice_in_dim(win_pad, start, WINDOW + Q_BLOCK, axis=1)
        q_pos = start + jnp.arange(Q_BLOCK)
        w_pos = start - WINDOW + jnp.arange(WINDOW + Q_BLOCK)
        return nsa_core(qb, q_pos, kc_blk, vc_blk, ks_g, vs_g, wb[:, :, 0], wb[:, :, 1], w_pos, gb)
    o = lax.map(one_block, jnp.arange(s // Q_BLOCK))
    return jnp.moveaxis(o, 0, 1).reshape(b, s, C_KV_HEADS, C_REP, HEAD_DIM)

def nsa_sample(q, gates, kv_cmp, kv_sel, kv_win, pool_cmp, pool_sel, win_buf, page_table):
    db, t = q.shape[:2]
    past_len = page_table.shape[1] * PAGE_SIZE
    def past(pool):
        return pool[page_table].reshape(db, past_len, 2, C_KV_HEADS, HEAD_DIM).astype(kv_cmp.dtype)
    full_cmp = jnp.concatenate([past(pool_cmp), kv_cmp], axis=1)
    full_sel = jnp.concatenate([past(pool_sel), kv_sel], axis=1)
    kc_blk, vc_blk, ks_g, vs_g = block_views(full_cmp, full_sel)
    n_buf = win_buf.shape[1]
    win = jnp.concatenate([win_buf.astype(kv_win.dtype), kv_win], axis=1)
    q_pos = past_len + jnp.arange(t)
    w_pos = past_len - n_buf + jnp.arange(n_buf + t)
    o = nsa_core(q, q_pos, kc_blk, vc_blk, ks_g, vs_g, win[:, :, 0], win[:, :, 1], w_pos, gates)
    return o, win[:, -n_buf:]

def odd_output(x, o, z, w_out):
    b, t = x.shape[:2]
    gated = o.reshape(b, t, C_WIDTH).astype(x.dtype) * jax.nn.silu(z)
    return x + (gated @ w_out).astype(x.dtype)

def setup_inputs(seed: int = 0) -> dict:
    key = jax.random.key(seed)
    ks = jax.random.split(key, 24)
    f32 = jnp.float32
    nrm = lambda k, shape, sc: jax.random.normal(k, shape, f32) * sc
    n_pages = PAST_LEN // PAGE_SIZE
    n_phys = (5 * DEC_BATCH * n_pages + 3) // 4
    win_buf = min(WINDOW, PAST_LEN)
    page_table = jax.random.permutation(ks[6], n_phys)[:DEC_BATCH * n_pages]
    page_table = page_table.reshape(DEC_BATCH, n_pages).astype(jnp.int32)
    return {
        'x_prompt': nrm(ks[0], (BATCH, SEQ, D_MODEL), 1.0),
        'x_sample': nrm(ks[1], (DEC_BATCH, DEC_SEQ, D_MODEL), 1.0),
        'cache_cmp_kv': nrm(ks[2], (N_ODD, n_phys, PAGE_SIZE, 2, C_KV_HEADS, HEAD_DIM), 1.0),
        'cache_sel_kv': nrm(ks[3], (N_ODD, n_phys, PAGE_SIZE, 2, C_KV_HEADS, HEAD_DIM), 1.0),
        'state_win_kv': nrm(ks[4], (N_ODD, DEC_BATCH, win_buf, 2, C_KV_HEADS, HEAD_DIM), 1.0),
        'state_pool': nrm(ks[5], (N_EVEN, DEC_BATCH, POOL_PAD, B_WIDTH), 1.0),
        'page_table': page_table,
        'norm_even': 1.0 + nrm(ks[7], (N_EVEN, D_MODEL), 0.02),
        'w_in_even': nrm(ks[8], (N_EVEN, D_MODEL, EVEN_IN), D_MODEL ** -0.5),
        'v_norm': 1.0 + nrm(ks[9], (N_EVEN, A_WIDTH), 0.02),
        'w_spatial': nrm(ks[10], (N_EVEN, A_HEADS, GMLP_CHUNK, GMLP_CHUNK), GMLP_CHUNK ** -0.5),
        'b_spatial': 1.0 + nrm(ks[11], (N_EVEN, A_HEADS, GMLP_CHUNK), 0.02),
        'w_pool': nrm(ks[12], (N_EVEN, N_POOL_GROUPS, POOL_GROUP, POOL_GROUP), POOL_GROUP ** -0.5),
        'pool_scale': 1.0 + nrm(ks[13], (N_EVEN, B_WIDTH), 0.02),
        'w_out_even': nrm(ks[14], (N_EVEN, A_WIDTH + B_WIDTH, D_MODEL), (A_WIDTH + B_WIDTH) ** -0.5),
        'norm_odd': 1.0 + nrm(ks[15], (N_ODD, D_MODEL), 0.02),
        'w_in_odd': nrm(ks[16], (N_ODD, D_MODEL, ODD_IN), D_MODEL ** -0.5),
        'q_norm': 1.0 + nrm(ks[17], (N_ODD, HEAD_DIM), 0.02),
        'k_norm': 1.0 + nrm(ks[18], (N_ODD, 3, HEAD_DIM), 0.02),
        'w_out_odd': nrm(ks[19], (N_ODD, C_WIDTH, D_MODEL), C_WIDTH ** -0.5),
    }

def reference(x_prompt, x_sample, cache_cmp_kv, cache_sel_kv, state_win_kv, state_pool, page_table,
              norm_even, w_in_even, v_norm, w_spatial, b_spatial, w_pool, pool_scale, w_out_even,
              norm_odd, w_in_odd, q_norm, k_norm, w_out_odd):
    bsz, seq, _ = x_prompt.shape
    dec_t = x_sample.shape[1]
    past_len = page_table.shape[1] * PAGE_SIZE
    pos_p = jnp.arange(seq, dtype=jnp.int32)
    pos_s = past_len + jnp.arange(dec_t, dtype=jnp.int32)
    win_keep = min(WINDOW, seq)
    xp, xs = x_prompt, x_sample
    cmp_p, cmp_s, sel_p, sel_s, win_p, win_s = [], [], [], [], [], []
    pool_p, pool_s, gv_s = [], [], []
    for layer in range(DEPTH):
        li = layer // 2
        if layer % 2 == 0:
            ew = (norm_even[li], w_in_even[li], v_norm[li], w_spatial[li], b_spatial[li],
                  w_pool[li], pool_scale[li], w_out_even[li])
            zero_prefix = jnp.zeros((bsz, POOL_PAD, B_WIDTH), xp.dtype)
            xp, _, pp = even_layer(xp, zero_prefix, pos_p, *ew)
            xs, v_rows, ps = even_layer(xs, state_pool[li], pos_s, *ew)
            pool_p.append(pp)
            pool_s.append(ps)
            gv_s.append(v_rows)
        else:
            ow = (norm_odd[li], w_in_odd[li], q_norm[li], k_norm[li])
            q, kvc, kvs, kvw, gates, z = odd_project(xp, pos_p, *ow)
            xp = odd_output(xp, nsa_prompt(q, gates, kvc, kvs, kvw), z, w_out_odd[li])
            cmp_p.append(kvc)
            sel_p.append(kvs)
            win_p.append(kvw[:, seq - win_keep:])
            q, kvc, kvs, kvw, gates, z = odd_project(xs, pos_s, *ow)
            o, win_new = nsa_sample(q, gates, kvc, kvs, kvw, cache_cmp_kv[li], cache_sel_kv[li],
                                    state_win_kv[li], page_table)
            xs = odd_output(xs, o, z, w_out_odd[li])
            cmp_s.append(kvc)
            sel_s.append(kvs)
            win_s.append(win_new)
    return (xp, xs, jnp.stack(cmp_p), jnp.stack(cmp_s), jnp.stack(sel_p), jnp.stack(sel_s),
            jnp.stack(win_p), jnp.stack(win_s), jnp.stack(pool_p), jnp.stack(pool_s), jnp.stack(gv_s))


_drawn_inputs = setup_inputs


def setup_inputs(seed=0):
    import zlib

    import numpy as np

    out = dict(_drawn_inputs(seed))
    spreads = {}
    factors = {'cache_cmp_kv': 4.788,
     'cache_sel_kv': 3.958,
     'norm_even': 2.793,
     'v_norm': 23.52,
     'b_spatial': 21.637,
     'pool_scale': 22.413,
     'norm_odd': 7.443,
     'q_norm': 8.0,
     'k_norm': 13.927}
    for name, (base, spread) in spreads.items():
        noise = np.random.default_rng([zlib.crc32(name.encode()), seed]).standard_normal(out[name].shape)
        drawn = base * np.exp(spread * noise) if base else spread * noise
        out[name] = jnp.asarray(drawn.astype(out[name].dtype))
    for name, factor in factors.items():
        out[name] = (out[name] * factor).astype(out[name].dtype)
    return out
```

```python
from contextlib import ExitStack

import numpy as np
import concourse.bass as bass
from concourse import mybir

F32 = mybir.dt.float32
F32R = mybir.dt.float32r
BF16 = mybir.dt.bfloat16
I32 = mybir.dt.int32
ALU = mybir.AluOpType
ACT = mybir.ActivationFunctionType
AX = mybir.AxisListType

P = 128
D = 2048
KT = D // P
SEQ = 512
NS = 8
T = SEQ + NS
HALF = T // 2
TT = SEQ // P
TP = 5 * P
EPS = 1e-6
AH = 8
PG = 4
PAD = 15
HEADS = 16
KV = 4
REP = HEADS // KV
HD = 128
PAGES = 16
NBLK = 32
NSEL_FREE = 13
NEG = -1e30
SCALE = HD ** -0.5
PAST = 2048
EXT = PAD + SEQ + NS * 16

N_EVEN_IN, N_EVEN_OUT, N_KV, N_QZ, N_GATE, N_ODD_OUT = 0, 40, 56, 80, 112, 113

CONSTS = {}


def _lay_consts():
    parts, at = [], 0

    def put(name, a):
        nonlocal at
        a = np.asarray(a, np.float32).reshape(P, -1)
        CONSTS[name] = (at, a.shape[1])
        parts.append(a)
        at += a.shape[1]

    p = np.arange(P)
    put("ident", np.eye(P))
    put("ones", np.ones((P, P)))
    put("tril_t", p[:, None] <= p[None, :])
    put("diag8", np.eye(P)[:, :NS])
    pos = np.zeros((P, 5), np.float32)
    pos[:, :TT] = p[:, None] + P * np.arange(TT)[None, :]
    pos[:, TT] = PAST
    inv_freq = np.float32(500000.0) ** (-np.arange(16, dtype=np.float32) * np.float32(2.0 / 32))
    ang = (pos[:, :, None] * inv_freq[None, None, :]).astype(np.float32).astype(np.float64)
    cos, sin = np.cos(ang), np.sin(ang)
    put("cos", cos)
    put("sin", sin)
    par = np.zeros((P, PG, 4 + PAD))
    for g, w in enumerate((2, 4, 8, 16)):
        par[:, g, 0:3] = [w >= 4, w >= 8, w >= 16]
        par[:, g, 3] = 1.0 / w
        par[:, g, 4:] = 1.0 / np.minimum(np.arange(PAD) + 1, w)
    put("pool", par)
    bm = np.zeros((P, 8, 32))
    for c in range(8):
        bm[p, c, 2 * c + p // 64] = 1.0 / 64
    put("page_blocks", bm)
    vm = np.zeros((P, TT, REP, 32))
    for j in range(TT):
        vm[p, j, :, 0] = 0
        for h in range(REP):
            vm[p, j, h, 2 * j + p // 64] = 1.0 / 64
    put("prompt_blocks", vm)
    t = p[:, None] + P * np.arange(TT)[None, :]
    ok = ((np.arange(8) + 1) * 64 - 1)[None, None, :] <= t[:, :, None]
    ok4 = np.repeat(ok[:, :, None, :], REP, 2)
    put("cmp_ok", ok4)
    put("cmp_bias", np.where(ok4, 0.0, NEG))
    put("causal", np.where(p[None, :] <= p[:, None], 0.0, NEG))
    gm = np.zeros((P, P))
    for g in range(KV):
        gm[32 * g:32 * g + REP, 32 * g:32 * g + 32] = 1.0
    put("group_sum", gm)
    i30 = np.arange(30)
    put("before", np.broadcast_to((i30[None, :] < i30[:, None]).reshape(1, -1), (P, 900)))
    return np.ascontiguousarray(np.concatenate(parts, 1))


def build(nc, I, O, xT_scr, x1_scr, szT_scr):
    ctx = ExitStack()
    with ctx:
        base = nc.sbuf_base
        base = (base + 127) // 128 * 128
        LIMIT = nc.sbuf_usable_end

        def at(name, off, shape, dt=F32):
            size = int(np.prod(shape[1:])) * (2 if dt == BF16 else 4)
            assert base + off + size <= LIMIT, (name, base + off + size, LIMIT)
            t_ = nc.alloc_sbuf_tensor_at(name, shape, dt, offset=base + off)
            return t_, off + (size + 31) // 32 * 32

        o = 0
        H_OFF = o
        HH, o = at("act_hi", o, [P, KT, T], F32R)
        HL, o = at("act_lo", o, [P, KT, T], F32R)
        WHL_OFF = o
        WH, o = at("w_hi", o, [P, 2, KT, P], F32R)
        WL, o = at("w_lo", o, [P, 2, KT, P], F32R)
        RAW, o = at("w_raw", o, [P, 2, KT, P])
        A, o = at("act", o, [P, KT, T])
        ident, o = at("ident", o, [P, P])
        ones, o = at("ones", o, [P, P])
        g_even, o = at("gain_even", o, [P, KT])
        g_odd, o = at("gain_odd", o, [P, KT])
        eps_t, o = at("eps", o, [P, 1])
        mhalf, o = at("minus_half", o, [P, 8])
        R_OFF = o

        o = R_OFF
        VG, o = at("v_gain", o, [P, AH * P])
        BS, o = at("b_spatial", o, [P, AH * P])
        WST, o = at("w_spatial_t", o, [P, AH, P])
        DG, o = at("w00_diag", o, [P, AH, NS])
        W00, o = at("w00", o, [P, AH])
        WP, o = at("w_pool", o, [P, PG, 2, 256])
        WPG, o = at("w_pool_group", o, [P, 2, 256])
        PSC, o = at("pool_scale", o, [P, PG, 2])
        PAR, o = at("pool_par", o, [P, PG, 4 + PAD])
        PARG, o = at("pool_par_group", o, [P, 4 + PAD])
        PSG, o = at("pool_scale_group", o, [P, 2])
        STP, o = at("pool_state_t", o, [P, AH, NS * PAD])
        E_OFF = o
        VT, o = at("v_t", o, [P, TP])
        VN, o = at("v_norm", o, [P, 5, P])
        C1, o = at("chain1", o, [P, EXT])
        C2, o = at("chain2", o, [P, EXT])
        UT, o = at("u_t", o, [P, T])
        SZ, o = at("silu_z", o, [P, T])
        EX0, o = at("pool_in0", o, [P, EXT])
        EX1, o = at("pool_in1", o, [P, EXT])
        PD, o = at("pool_diff", o, [P, 2, T])
        TLP, o = at("pool_tail", o, [PAD, P])
        TLS, o = at("pool_tail_s", o, [NS, P])
        SS, o = at("v_sumsq", o, [P, 5])
        SR, o = at("v_rstd", o, [P, 5])
        FIX, o = at("pool_fix", o, [P, PAD])
        EX = [EX0, EX1]
        o = E_OFF
        XS, o = at("x_stage", o, [P, 2, D])
        WSR, o = at("w_spatial_raw", o, [P, AH, P])
        STR, o = at("pool_state_raw", o, [NS * PAD, AH * P])
        TRIL, o = at("tril_t", o, [P, P])
        DI8, o = at("diag8", o, [P, NS])
        o = E_OFF
        SQ, o = at("sq", o, [P, 2, T])
        RS, o = at("rstd", o, [P, T])
        TM, o = at("norm_tmp", o, [P, 2, T])
        o = R_OFF
        XR, o = at("residual", o, [P, 2, T])
        YT, o = at("y_t", o, [P, 2, T])
        YS, o = at("y_rows", o, [P, 2, 5, P])

        o = R_OFF
        KTS, o = at("k_t", o, [P, 2, KV, SEQ])
        VS, o = at("v_rows", o, [P, 2, KV, TT, P])
        VM4, o = at("v_cmp_mean", o, [P, KV, P])
        KM, o = at("k_cmp_mean", o, [P, KV, 32])
        GT, o = at("gate_rows", o, [P, TT, P])
        GS, o = at("gate_sample", o, [P, 3, NS])
        QP, o = at("q_sample", o, [P, NS, KV, 32])
        L1_OFF = o
        KTT, o = at("head_t", o, [P, 2, TP])
        KN, o = at("head_rows", o, [P, 2, 5, P])
        SQ1, o = at("head_sq", o, [P, 5, P])
        GQ, o = at("qk_gain", o, [P, 4, P])
        COS, o = at("cos", o, [P, 5, 16])
        SIN, o = at("sin", o, [P, 5, 16])
        RA, o = at("rope_a", o, [P, 5, 32])
        RB, o = at("rope_b", o, [P, 5, 32])
        HS, o = at("head_ss", o, [P, 5])
        HR, o = at("head_rstd", o, [P, 5])
        VMASK, _ = at("prompt_blocks", o, [P, TT, P])
        ZT, o = at("z_t", o, [P, 2, T])
        KSUM, o = at("k_block_sum", o, [P, 8])
        o = L1_OFF
        PTAB, o = at("page_table", o, [1, P], I32)
        SBIAS, o = at("sel_bias", o, [P, NS, NBLK])
        OC, o = at("o_cmp", o, [P, NS, P])
        o = H_OFF
        PGT, o = at("cmp_pages", o, [P, 2, 4, 1024])
        KMS, o = at("cmp_means", o, [P, 4, 1024])
        KMT, o = at("cmp_k_t", o, [P, KV, NS, 32])
        o2 = WHL_OFF
        BM, o2 = at("page_blocks", o2, [P, 8, 32])
        CE, o2 = at("cmp_e", o2, [P, NS, 32])
        CP, o2 = at("cmp_p_pad", o2, [P, 4, 4, 32])
        CPT, o2 = at("cmp_p_t", o2, [P, 4, P])
        CM, o2 = at("cmp_max", o2, [P, NS])
        CR, o2 = at("cmp_sum", o2, [P, NS])
        GMT, o2 = at("group_sum", o2, [P, P])
        IMP, o2 = at("importance", o2, [P, NS, 32])
        BEF, o2 = at("before", o2, [P, 900])
        RK1, o2 = at("rank1", o2, [P, 30, 30])
        RK2, o2 = at("rank2", o2, [P, 30, 30])
        RNK, o2 = at("rank", o2, [P, 30])
        GTT, o2 = at("gate_t", o2, [P, T])
        G8, o2 = at("gate8", o2, [NS, 3, P])
        assert o2 <= WHL_OFF + 32768
        o = H_OFF
        SK, o = at("sel_k", o, [P, 4, 512])
        SV, o = at("sel_v", o, [P, PAGES, 512])
        NR, o = at("new_row", o, [1, 1024])
        KW, o = at("win_rows", o, [P, 4, 1024])
        assert o <= WHL_OFF
        o = WHL_OFF
        SC, o = at("scores", o, [P, PAGES * P + 1])
        SKT, o = at("sel_k_t", o, [P, KV, 512])
        SPT, o = at("p_t", o, [P, 17, P])
        QS, o = at("q_static", o, [P, KV, 32])
        KNT, o = at("new_k_t", o, [P, KV])
        SWP, o = at("win_p", o, [P, SEQ])
        assert o <= WHL_OFF + 32768
        o = L1_OFF + 8 * 1024
        WPT, o = at("win_p_t", o, [P, 4, P])
        SST, o = at("s_stat", o, [P, 8])
        OSM, o = at("o_sample", o, [P, 2, P])
        o = H_OFF
        VB, o = at("v_static", o, [P, 2, TT, P])
        QC, o = at("q_cmp", o, [P, REP, SEQ])
        PR, o = at("probs", o, [P, 4, SEQ])
        PT_, o = at("probs_t", o, [P, 2, TT, SEQ])
        CS, o = at("cmp_s_t", o, [P, SEQ])
        KMG, o = at("k_mean_static", o, [P, 32])
        VMG, o = at("v_mean_static", o, [P, P])
        o = WHL_OFF
        CPP, o = at("cmp_probs", o, [P, TT, REP, 32])
        CPX, o = at("cmp_probs_t", o, [P, SEQ])
        COK, o = at("cmp_ok", o, [P, TT, REP, 8])
        CBI, o = at("cmp_bias", o, [P, TT, REP, 8])
        CX, o = at("cmp_x", o, [P, TT, REP, 8])
        CMX, o = at("cmp_mx", o, [P, TT, REP])
        CSM, o = at("cmp_sm", o, [P, TT, REP])
        CAU, o = at("causal", o, [P, P])
        CAB, o = at("causal_bf", o, [P, P], BF16)
        IDB, o = at("ident_bf", o, [P, P], BF16)
        AMX, o = at("a_max", o, [P, 8])
        ASM, o = at("a_sum", o, [P, 8])
        AW, o = at("a_w", o, [P, 8])
        SZH, o = at("sz_head", o, [P, 2, T])
        AW2, o = at("a_w2", o, [P, 8])
        assert o <= WHL_OFF + 32768

        MP = ctx.enter_context(nc.psum_tensor("main", [P, 2, 2, 512], F32))
        X = ctx.enter_context(nc.psum_tensor("aux", [P, 4, 512], F32))

        sems = {}

        def sem(name):
            if name not in sems:
                sems[name] = ctx.enter_context(nc.semaphore(name))
            return sems[name]

        w_landed = [sem("w_landed0"), sem("w_landed1")]
        w_hi, w_split, mm_done = sem("w_hi"), sem("w_split"), sem("mm_done")
        evac = [sem("evac0"), sem("evac1")]
        held = sem("held")

        def wait(eng, s, v):
            eng.wait_ge(s, v)
            if not isinstance(v, int):
                eng.sem_inc(held, 1)

        class Seq:

            def __init__(self, eng, name, base=0):
                self.eng, self.s, self.n, self.base = eng, sem(name), 0, base

            def loop(self, i, per, start):
                self.base, self.n = start + per * i, 0

            def do(self, ins):
                self.n += 1
                ins.then_inc(self.s, 1)
                wait(self.eng, self.s, self.base + self.n)

        def load_w(sp, n, half, src, width=P):
            slot = half[1]
            wait(sp, w_split, n + 1)
            nc.sync.dma_start(RAW[:, slot, :, 0:width], src).then_inc(w_landed[slot], 16)

        def split_hi(act, n, half):
            h, slot = half
            wait(act, w_landed[slot], 16 * h + 16)
            wait(act, mm_done, n + 1)
            nc.scalar.copy(WH[:, slot], RAW[:, slot]).then_inc(w_hi, 1)

        def split_lo(dve, n, half):
            slot = half[1]
            wait(dve, w_hi, n + 1)
            nc.vector.tensor_tensor(WL[:, slot], RAW[:, slot], WH[:, slot].bitcast(F32),
                                    ALU.subtract).then_inc(w_split, 1)

        def main(pe, n, half, first=False):
            h, slot = half
            wait(pe, w_split, n + 3)
            wait(pe, evac[slot], h + 1)
            for k in range(KT):
                if first is not False:
                    wait(pe, first, k + 1)
                for q, (w_, x_) in enumerate(((WH, HH), (WH, HL), (WL, HH))):
                    for b in range(2):
                        ins = nc.tensor.matmul(MP[:, slot, b, 0:HALF], w_[:, slot, k, :],
                                               x_[:, k, b * HALF:(b + 1) * HALF],
                                               start=(k == 0 and q == 0), stop=(k == KT - 1 and q == 2))
            ins.then_inc(mm_done, 1)

        def tile_no(n0, per, i, c):
            return n0 + per * i + c, ((n0 + c) // 2 + (per // 2) * i, (n0 + c) % 2)

        def mp(slot):
            return MP[:, slot, :, 0:HALF]

        def two(ap):
            return ap.rearrange("p (b t) -> p b t", b=2)

        w_even = I["w_in_even"].rearrange("(k p) n -> p k n", p=P)
        w_eout = I["w_out_even"].rearrange("(k p) n -> p k n", p=P)
        w_odd = I["w_in_odd"].rearrange("(k p) n -> p k n", p=P)
        w_oout = I["w_out_odd"].rearrange("(k p) n -> p k n", p=P)

        EV = [("v", 0), ("u", 0), ("za", 0), ("v", 1), ("u", 1), ("za", 1), ("p", 0), ("p", 1), ("zb", 0), ("zb", 1)]
        EV_COL = {"u": 0, "v": 1024, "za": 2048, "p": 3072, "zb": 4096}
        KVT = [("k", 2048, 0), ("k", 3072, 1), ("k", 4096, 2), ("v", 2560, 0), ("v", 3584, 1), ("v", 4608, 2)]
        kv_p = [O.get(b + "_kv_prompt") for b in ("cmp", "sel", "win")]
        kv_s = [O.get(b + "_kv_sample") for b in ("cmp", "sel", "win")]
        QKV_Z, QKV_G = 5168, 5120

        def cst(name):
            a, n_ = CONSTS[name]
            return I["consts"][:, a:a + n_]

        block = ctx.enter_context(nc.Block())

        def pad5(bank):
            return X[:, bank:bank + 2, :].rearrange("p b n -> p (b n)")[:, 0:TP].rearrange("p (j d) -> p j d", d=P)

        def over(ap, n):
            return ap.unsqueeze(2).to_broadcast([ap.shape[0], ap.shape[1], n])

        def act_tile(idx):
            if isinstance(idx, int):
                return A[:, idx, :]
            return A[:, bass.ds(idx, 1), :].rearrange("p a t -> p (a t)")

        @block.sync
        def _(sp):
            nc.sync.dma_start(ident[:], cst("ident")).then_inc(sem("ident_landed"), 16)
            xp = I["x_prompt"].rearrange("(j p) d -> j p d", p=P)
            for j in range(2):
                nc.sync.dma_start(XS[:, j], xp[j]).then_inc(sem(f"x_landed{j}"), 16)
            for j in range(2, 5):
                sp.wait_ge(sem("x_turned"), 4 * (j - 1))
                if j < 4:
                    nc.sync.dma_start(XS[:, j % 2], xp[j]).then_inc(sem(f"x_landed{j % 2}"), 16)
                else:
                    nc.sync.dma_start(XS[0:NS, 0], I["x_sample"]).then_inc(sem("x_landed0"), 16)
            with sp.Fori(0, PG) as i:
                for c, (kind, e) in enumerate(EV):
                    n, half = tile_no(N_EVEN_IN, 10, i, c)
                    col = nc.sync.snap(EV_COL[kind] + (2 * i + e) * P, min_val=0, max_val=4992)
                    load_w(sp, n, half, w_even[:, :, bass.ds(col, P)])
            sp.wait_ge(sem("xT_out"), 16)
            with sp.Fori(0, 8) as i:
                for c in range(2):
                    n, half = tile_no(N_EVEN_OUT, 2, i, c)
                    col = nc.sync.snap((2 * i + c) * P, min_val=0, max_val=D - P)
                    kt = nc.sync.snap(2 * i + c, min_val=0, max_val=KT - 1)
                    load_w(sp, n, half, w_eout[:, :, bass.ds(col, P)])
                    wait(sp, evac[c], half[0] + 1)
                    nc.sync.dma_start(XR[:, c], xT_scr[bass.ds(kt, 1)].rearrange("a p t -> p (a t)")).then_inc(
                        sem(f"res_landed{c}"), 16)
            with sp.Fori(0, KV) as i:
                for c, (kind, col0, br) in enumerate(KVT):
                    n, half = tile_no(N_KV, 6, i, c)
                    col = nc.sync.snap(col0 + i * P, min_val=0, max_val=7216 - P)
                    load_w(sp, n, half, w_odd[:, :, bass.ds(col, P)])
                    if c in (1, 4):
                        smp = nc.sync.snap(2 * i + c // 4, min_val=0, max_val=NS - 1)
                        nc.sync.dma_start(O["win_kv_sample"][bass.ds(smp, 1), 0:511, :].rearrange("a r c -> a (r c)"),
                                          I["state_win_kv"][bass.ds(smp, 1), 1:512, :].rearrange("a r c -> a (r c)")
                                          ).then_inc(sem("win_moved"), 16)
            with sp.Fori(0, KV) as i:
                for c in range(8):
                    n, half = tile_no(N_QZ, 8, i, c)
                    col0 = 0 if c < 4 else QKV_Z
                    col = nc.sync.snap(col0 + (4 * i + c % 4) * P, min_val=0, max_val=7216 - P)
                    load_w(sp, n, half, w_odd[:, :, bass.ds(col, P)])
            load_w(sp, N_GATE, (N_GATE // 2, 0), w_odd[:, :, QKV_G:QKV_G + 48], 48)

            sp.wait_ge(mm_done, N_GATE + 3)
            sp.wait_ge(sem("head_turned"), 42)
            nc.sync.dma_start(PTAB[:], I["page_table"]).then_inc(sem("table_landed"), 16)
            for dst, name in ((BM[:].rearrange("p c n -> p (c n)"), "page_blocks"), (GMT[:], "group_sum"),
                              (BEF[:], "before")):
                nc.sync.dma_start(dst, cst(name)).then_inc(sem("cmp_consts"), 16)
            sp.wait_ge(sem("table_landed"), 16)
            with sp.Fori(0, 2) as r:
                for hf in range(2):
                    for c in range(8):
                        for s4 in range(4):
                            pg = nc.sync.value_load(PTAB[0:1, bass.ds(64 * r + 16 * s4 + 8 * hf + c, 1)],
                                                    min_val=0, max_val=NPHYS - 1)
                            if s4 == 0:
                                wait(sp, sem("pages_used"), 16 * r + 8 * hf + c + 1)
                            nc.sync.dma_start(PGT[:, c % 2, s4], I["cache_cmp_kv"][bass.ds(pg, 1)].rearrange(
                                "a t c -> t (a c)")).then_inc(sem(f"pages_landed{c % 2}"), 16)

            sp.wait_ge(sem("oc_ready"), 4)
            for b in range(2):
                sp.wait_ge(sem(f"rows_out{b}"), 32 * 12 + 32)
            with sp.Fori(0, NS) as i:
                smp = nc.sync.snap(i, min_val=0, max_val=NS - 1)
                wait(sp, sem("pv_done"), i + 1)
                nc.sync.dma_start(KW[:], I["state_win_kv"][bass.ds(smp, 1)].rearrange("a (p j) c -> p (a j) c", j=4)
                                  ).then_inc(sem("win_landed"), 16)
                nc.sync.dma_start(NR[:], O["sel_kv_sample"][bass.ds(smp, 1), :]).then_inc(sem("new_landed"), 16)
                wait(sp, sem("win_landed"), 16 * i + 16)
                nc.sync.dma_start(KW[0:1, 0, :], O["win_kv_sample"][bass.ds(smp, 1), 511, :]).then_inc(
                    sem("new_landed"), 16)
                for j in range(PAGES):
                    pg = nc.sync.value_load(PTAB[0:1, bass.ds(16 * i + j, 1)], min_val=0, max_val=NPHYS - 1)
                    page = I["cache_sel_kv"][bass.ds(pg, 1)].rearrange("a t c -> t (a c)")
                    wait(sp, sem("k_turned"), 20 * i + j + 2)
                    nc.sync.dma_start(SK[:, j % 4], page[:, 0:512]).then_inc(sem(f"sk_landed{j % 4}"), 16)
                    nc.sync.dma_start(SV[:, j], page[:, 512:1024]).then_inc(sem("sv_landed"), 16)

            sp.wait_ge(sem("os_done"), NS + 1)
            for dst, name in ((COK[:], "cmp_ok"), (CBI[:], "cmp_bias")):
                nc.sync.dma_start(dst.rearrange("p j e n -> p (j e n)"), cst(name)).then_inc(sem("attn_consts"), 16)
            nc.sync.dma_start(CAU[:], cst("causal")).then_inc(sem("attn_consts"), 16)
            for b in range(2):
                sp.wait_ge(sem(f"z_out{b}"), 16 * 8 + 16)
            with sp.Fori(0, KV) as i:
                for e in range(REP):
                    head = nc.sync.snap(4 * i + e, min_val=0, max_val=HEADS - 1)
                    wait(sp, sem("o_used"), 4 * i + e + 1)
                    nc.sync.dma_start(SZH[:, e % 2], szT_scr[bass.ds(head, 1)].rearrange("a p t -> p (a t)")).then_inc(
                        sem(f"sz_landed{e % 2}"), 16)

            sp.wait_ge(sem("x1_out"), 256)
            with sp.Fori(0, 8) as i:
                for c in range(2):
                    n, half = tile_no(N_ODD_OUT, 2, i, c)
                    h, slot = half
                    col = nc.sync.snap((2 * i + c) * P, min_val=0, max_val=D - P)
                    kt = nc.sync.snap(2 * i + c, min_val=0, max_val=KT - 1)
                    load_w(sp, n, half, w_oout[:, :, bass.ds(col, P)])
                    wait(sp, evac[slot], h + 1)
                    nc.sync.dma_start(XR[:, slot], x1_scr[bass.ds(kt, 1)].rearrange("a p t -> p (a t)")).then_inc(
                        sem(f"res_landed{slot}"), 16)
            for b in range(2):
                sp.wait_ge(sem(f"y_out{b}"), 32 * 8 + 32)
            sp.wait_ge(sem("win_moved"), 16 * NS)
            sp.wait_ge(sem("gv_out"), 16 + 16 * AH)
            sp.wait_ge(sem("tail_out"), 32 + 32 * AH)

        def norm_act(act, r):
            for k in range(KT):
                if k >= 2:
                    act.wait_ge(sem("norm_summed"), KT * r + k - 1)
                nc.scalar.activation(SQ[:, k % 2], A[:, k, :], ACT.Square).then_inc(sem("norm_sq"), 1)
            act.wait_ge(sem("norm_summed"), KT * (r + 1))
            nc.scalar.activation(two(RS[:]), X[:, 2:4, 0:HALF], ACT.Sqrt, bias=eps_t[:, 0:1],
                                 scale=1.0 / D).then_inc(sem("norm_root"), 1)
            for k in range(KT):
                act.wait_ge(sem("norm_scaled"), KT * r + k + 1)
                nc.scalar.copy(HH[:, k], TM[:, k % 2]).then_inc(sem("hi_done"), 1)

        def norm_dve(dve, r, gain, q):
            dve.wait_ge(sem("norm_root"), r + 1)
            nc.vector.reciprocal(RS[:], RS[:]).then_inc(sem("norm_rstd"), 1)
            dve.wait_ge(sem("norm_rstd"), r + 1)

            def scaled(k):
                if k >= 2:
                    dve.wait_ge(sem("lo_done"), KT * q + k - 1)
                nc.vector.scalar_tensor_tensor(out=TM[:, k % 2], in0=A[:, k, :], scalar=gain[:, k:k + 1],
                                               in1=RS[:], op0=ALU.mult, op1=ALU.mult).then_inc(sem("norm_scaled"), 1)

            scaled(0)
            for k in range(KT):
                if k + 1 < KT:
                    scaled(k + 1)
                dve.wait_ge(sem("norm_scaled"), KT * r + k + 1)
                dve.wait_ge(sem("hi_done"), KT * q + k + 1)
                nc.vector.tensor_tensor(HL[:, k], TM[:, k % 2], HH[:, k].bitcast(F32),
                                        ALU.subtract).then_inc(sem("lo_done"), 1)

        def norm_pe(pe, r):
            for k in range(KT):
                pe.wait_ge(sem("norm_sq"), KT * r + k + 1)
                for b in range(2):
                    ins = nc.tensor.matmul(X[:, 2 + b, 0:HALF], ones[:], SQ[:, k % 2, b * HALF:(b + 1) * HALF],
                                           start=(k == 0), stop=(k == KT - 1))
                ins.then_inc(sem("norm_summed"), 1)

        def split_act_act(act, q):
            for k in range(KT):
                nc.scalar.copy(HH[:, k], A[:, k, :]).then_inc(sem("hi_done"), 1)

        def split_act_dve(dve, q):
            for k in range(KT):
                dve.wait_ge(sem("hi_done"), KT * q + k + 1)
                nc.vector.tensor_tensor(HL[:, k], A[:, k, :], HH[:, k].bitcast(F32),
                                        ALU.subtract).then_inc(sem("lo_done"), 1)

        @block.tensor
        def _(pe):
            pe.sem_inc(mm_done, 2)
            pe.sem_inc(sem("v_turned"), 1)
            pe.sem_inc(sem("s_ready"), 1)
            pe.sem_inc(sem("y_ready"), 1)
            pe.sem_inc(sem("tail_turned"), 2)

            def main_split(pe, n, half, q):
                h, slot = half
                wait(pe, w_split, n + 3)
                wait(pe, evac[slot], h + 1)
                for k in range(KT):
                    pe.wait_ge(sem("lo_done"), KT * q + k + 1)
                    for qq, (w_, x_) in enumerate(((WH, HH), (WH, HL), (WL, HH))):
                        for b in range(2):
                            ins = nc.tensor.matmul(MP[:, slot, b, 0:HALF], w_[:, slot, k, :],
                                                   x_[:, k, b * HALF:(b + 1) * HALF],
                                                   start=(k == 0 and qq == 0), stop=(k == KT - 1 and qq == 2))
                ins.then_inc(mm_done, 1)

            x_ev = [sem("x_evac0"), sem("x_evac1")]
            pe.wait_ge(sem("ident_landed"), 16)
            for j in range(4):
                pe.wait_ge(sem(f"x_landed{j % 2}"), 16 * (j // 2) + 16)
                for c in range(4):
                    q = 4 * j + c
                    if q >= 4:
                        pe.wait_ge(x_ev[q % 2], (q - 4) // 2 + 1)
                    for kk in range(4):
                        ins = nc.tensor.transpose(X[:, q % 4, kk * P:(kk + 1) * P],
                                                  XS[:, j % 2, (4 * c + kk) * P:(4 * c + kk + 1) * P], ident[:])
                    ins.then_inc(sem("x_turned"), 1)
            pe.wait_ge(sem("x_landed0"), 48)
            pe.wait_ge(x_ev[0], 7)
            for k in range(KT):
                ins = nc.tensor.transpose(X[:, 0, k * NS:(k + 1) * NS], XS[0:NS, 0, k * P:(k + 1) * P],
                                          ident[0:NS, 0:NS])
            ins.then_inc(sem("x_turned"), 1)
            pe.wait_ge(sem("raw_landed"), 32)
            for b in range(2):
                pe.wait_ge(x_ev[1 - b], 7 + b)
                for t_ in range(4):
                    ins = nc.tensor.transpose(X[:, 1 + b, t_ * 120:(t_ + 1) * 120],
                                              STR[:, (4 * b + t_) * P:(4 * b + t_ + 1) * P], ident[0:120, 0:120])
                ins.then_inc(sem("x_turned"), 1)
            pe.wait_ge(sem("raw_landed"), 32)
            for b in range(2):
                pe.wait_ge(x_ev[1 - b], 8 + b)
                for t_ in range(4):
                    ins = nc.tensor.transpose(X[:, 3 * (1 - b), t_ * P:(t_ + 1) * P], WSR[:, 4 * b + t_, :], ident[:])
                ins.then_inc(sem("x_turned"), 1)
            pe.wait_ge(sem("setup"), SETUP)
            pe.wait_ge(x_ev[0], 12)
            norm_pe(pe, 0)
            pe.wait_ge(sem("pads"), 3)
            pe.wait_ge(sem("diag_ready"), 1)

            def turn_v(i, e):
                n, (h, slot) = tile_no(N_EVEN_IN, 10, i, 3 * e)
                wait(pe, evac[slot], h + 2)
                if e == 0:
                    wait(pe, sem("tail_copied"), 2 * i + 1)
                else:
                    wait(pe, sem("v_mul"), 2 * i + 1)
                for j in range(5):
                    ins = nc.tensor.transpose(pad5(0)[:, j, :], VT[:, j * P:(j + 1) * P], ident[:])
                ins.then_inc(sem("v_turned"), 1)

            def spatial(i, e):
                wait(pe, sem("v_ready"), 2 * i + e + 1)
                if e == 0:
                    wait(pe, sem("y_used"), 2 * i + 1)
                else:
                    wait(pe, sem("s_used"), 2 * i + 1)
                wst = WST[:, bass.ds(2 * i + e, 1), :].rearrange("p a t -> p (a t)")
                dg = DG[:, bass.ds(2 * i + e, 1), :].rearrange("p a t -> p (a t)")
                for j in range(TT):
                    nc.tensor.matmul(X[:, 2, j * P:(j + 1) * P], VN[:, j, :], wst, start=True, stop=True)
                nc.tensor.matmul(X[:, 3, 0:NS], VN[:, 4, :], dg, start=True, stop=True).then_inc(sem("s_ready"), 1)

            def turn_tail(i, e):
                n, (h, slot) = tile_no(N_EVEN_IN, 10, i, 6 + e)
                wait(pe, evac[slot], h + 2)
                if e == 0:
                    wait(pe, sem("v_mul"), 2 * i + 2)
                else:
                    wait(pe, sem("tail_copied"), 2 * i + 2)
                nc.tensor.transpose(X[0:PAD, 0, 0:P], EX[e][:, SEQ:SEQ + PAD], ident[:])
                nc.tensor.transpose(X[0:NS, 1, 0:P], EX[e][:, PAD + SEQ + 15::16], ident[:]).then_inc(
                    sem("tail_turned"), 1)

            def pool_y(i, e):
                wait(pe, sem("pool_d"), 2 * i + 4)
                wait(pe, sem("group_ready"), 3 * i + 3)
                if e == 0:
                    wait(pe, sem("s_used"), 2 * i + 2)
                else:
                    wait(pe, sem("y_used"), 2 * i + 2)
                for b in range(2):
                    for c in range(2):
                        ins = nc.tensor.matmul(X[:, 2 + b, 0:HALF], WPG[:, c, e * P:(e + 1) * P],
                                               PD[:, c, b * HALF:(b + 1) * HALF], start=(c == 0), stop=(c == 1))
                ins.then_inc(sem("y_ready"), 1)

            with pe.Fori(0, PG) as i:
                for c, (kind, e) in enumerate(EV):
                    n, half = tile_no(N_EVEN_IN, 10, i, c)
                    if c == 0:
                        main_split(pe, n, half, 0)
                    else:
                        main(pe, n, half)
                    if kind == "u":
                        turn_v(i, e)
                    if kind == "za":
                        spatial(i, e)
                    if c == 7:
                        turn_tail(i, 0)
                    if c == 8:
                        turn_tail(i, 1)
                        pool_y(i, 0)
                    if c == 9:
                        pool_y(i, 1)
            with pe.Fori(0, 8) as i:
                for c in range(2):
                    n, half = tile_no(N_EVEN_OUT, 2, i, c)
                    if c == 0:
                        main_split(pe, n, half, 1)
                    else:
                        main(pe, n, half)

            pe.wait_ge(sem("y_used"), 9)
            norm_pe(pe, 1)
            pe.sem_inc(sem("head_turned"), 2)
            pe.wait_ge(sem("tail_copied"), 9)
            pe.wait_ge(sem("head_pads"), 4)

            def turn_head(i, m, n, h, slot):
                wait(pe, evac[slot], h + 2)
                wait(pe, sem("rows_read"), m + 1)
                for j in range(5):
                    ins = nc.tensor.transpose(pad5(0)[:, j, :], KTT[:, slot, j * P:(j + 1) * P], ident[:])
                ins.then_inc(sem("head_turned"), 1)

            def turn_back(kq, slot, tiles):
                wait(pe, sem("rows_ready"), kq + 1)
                wait(pe, sem("back_used"), kq + 1)
                for j in range(tiles):
                    ins = nc.tensor.transpose(pad5(2)[:, j, :], KN[:, slot, j, :], ident[:])
                ins.then_inc(sem("back_turned"), 1)

            with pe.Fori(0, KV) as i:
                for c, (kind, col0, br) in enumerate(KVT):
                    n, half = tile_no(N_KV, 6, i, c)
                    if c == 0:
                        main_split(pe, n, half, 2)
                    else:
                        main(pe, n, half)
                    for t_ in ([c - 1, 5] if c == 5 else [c - 1] if c else []):
                        m_n, (mh, ms) = tile_no(N_KV, 6, i, t_)
                        turn_head(i, 6 * i + t_, m_n, mh, ms)
                        if t_ == 4:
                            wait(pe, sem("vc_rows"), i + 1)
                            wait(pe, sem("vm_used"), i + 1)
                            for j in range(TT):
                                ins = nc.tensor.matmul(X[:, 3, 0:P], VMASK[:, j, :], KN[:, 1, j, :],
                                                       start=(j == 0), stop=(j == TT - 1))
                            ins.then_inc(sem("vm_done"), 1)
                    if 2 <= c <= 4:
                        turn_back(3 * i + c - 2, (c - 2) % 2, TT)
            with pe.Fori(0, KV) as i:
                for c in range(8):
                    n, half = tile_no(N_QZ, 8, i, c)
                    main(pe, n, half)
                    if 1 <= c <= 4:
                        m_n, (mh, ms) = tile_no(N_QZ, 8, i, c - 1)
                        turn_head(i, 24 + 4 * i + c - 1, m_n, mh, ms)
                    if 2 <= c <= 5:
                        turn_back(12 + 4 * i + c - 2, (c - 2) % 2, 5)
            main(pe, N_GATE, (N_GATE // 2, 0))
            pe.wait_ge(evac[0], N_GATE // 2 + 2)
            pe.wait_ge(sem("rows_read"), 41)
            for j in range(TT):
                nc.tensor.transpose(X[:, 0, j * P:(j + 1) * P], GTT[:, j * P:(j + 1) * P], ident[:])
            nc.tensor.transpose(X[0:NS, 1, 0:P], GTT[:, SEQ:T], ident[:]).then_inc(sem("gates_turned"), 1)
            pe.wait_ge(sem("gate8_ready"), 3)
            for b in range(3):
                ins = nc.tensor.transpose(X[:, 1, P + b * NS:P + (b + 1) * NS], G8[:, b, :], ident[0:NS, 0:NS])
            ins.then_inc(sem("gates_turned"), 1)

            pe.wait_ge(sem("cmp_consts"), 48)
            pe.wait_ge(sem("gates_copied"), 2)
            pe.wait_ge(sem("back_used"), 29)
            pe.sem_inc(sem("pages_used"), 2)
            with pe.Fori(0, 2) as r:
                for hf in range(2):
                    wait(pe, sem("means_used_a"), r + 1) if hf == 0 else wait(pe, sem("means_used_b"), r + 1)
                    for c in range(8):
                        wait(pe, sem(f"pages_landed{c % 2}"), 512 * r + 256 * hf + 64 * (c // 2) + 64)
                        for kv in range(2):
                            for s4 in range(4):
                                ins = nc.tensor.matmul(X[32 * s4:32 * s4 + 32, 2 * hf + kv, :], BM[:, c, :],
                                                       PGT[:, c % 2, s4, kv * 512:(kv + 1) * 512],
                                                       start=(c == 0), stop=(c == 7))
                        ins.then_inc(sem("pages_used"), 1)
            pe.wait_ge(sem("means_used_a"), 3)
            pe.wait_ge(sem("means_used_b"), 3)
            for it in range(4):
                for g in range(KV):
                    ins = nc.tensor.transpose(X[:, it, g * P:(g + 1) * P], KMS[:, it, g * P:(g + 1) * P], ident[:])
                ins.then_inc(sem("km_turned"), 1)
            pe.wait_ge(sem("kmt_ready"), 4)
            pe.wait_ge(sem("qp_ready"), 1)
            for s_ in range(NS):
                for g in range(KV):
                    ins = nc.tensor.matmul(X[32 * g:32 * g + 32, 0, s_ * 32:(s_ + 1) * 32], QP[:, s_, g, :],
                                           KMT[:, g, s_, :], start=True, stop=True)
            ins.then_inc(sem("cs_done"), 1)
            pe.wait_ge(sem("cp_ready"), 1)
            nc.tensor.matmul(X[:, 1, 0:NS * 32], GMT[:], CE[:].rearrange("p s n -> p (s n)"), start=True,
                             stop=True).then_inc(sem("imp_done"), 1)
            pe.wait_ge(sem("cpad_ready"), 5)
            for it in range(4):
                ins = nc.tensor.transpose(X[:, 2, it * P:(it + 1) * P], CP[:, it].rearrange("p s n -> p (s n)"),
                                          ident[:])
            ins.then_inc(sem("cpt_turned"), 1)
            pe.wait_ge(sem("cpt_ready"), 1)
            pe.wait_ge(sem("imp_copied"), 1)
            for s4 in range(4):
                for r in range(2):
                    for g in range(KV):
                        for hf in range(2):
                            ins = nc.tensor.matmul(
                                X[32 * g:32 * g + 32, s4, r * P:(r + 1) * P],
                                CPT[32 * s4:32 * s4 + 32, 2 * r + hf, 32 * g:32 * g + 32],
                                KMS[32 * s4:32 * s4 + 32, 2 * r + hf, 512 + g * P:512 + (g + 1) * P],
                                start=(hf == 0), stop=(hf == 1))
            ins.then_inc(sem("oc_done"), 1)

            pe.wait_ge(sem("oc_ready"), 4)
            pe.sem_inc(sem("k_turned"), 1)
            pe.sem_inc(sem("sc_done"), 1)
            pe.sem_inc(sem("pv_done"), 1)
            with pe.Fori(0, NS) as i:
                for b in range(5):
                    for t_ in range(4):
                        if b == 0 and t_ == 0:
                            wait(pe, sem("new_landed"), 32 * i + 32)
                            wait(pe, sem("os_done"), i + 1)
                            wait(pe, sem("q_static"), i + 1)
                        if b > 0:
                            wait(pe, sem(f"sk_landed{t_}"), 64 * i + 16 * b)
                        wait(pe, sem("k_evac"), 20 * i + 4 * b + t_ + 1)
                        src = KW if b == 0 else SK
                        for g in range(KV):
                            ins = nc.tensor.transpose(X[:, t_ % 2, g * P:(g + 1) * P], src[:, t_, g * P:(g + 1) * P],
                                                      ident[:])
                        ins.then_inc(sem("k_turned"), 1)
                    wait(pe, sem("k_evac"), 20 * i + 4 * b + 6)
                    if b == 0:
                        wait(pe, sem("sel_read"), 4 * i + 4)
                    elif b == 1:
                        wait(pe, sem("sel_read"), 4 * i + 3)
                    elif b == 2:
                        wait(pe, sem("win_exp"), i + 1)
                    else:
                        wait(pe, sem("sel_read"), 4 * i + 2 + b)
                    for g in range(KV):
                        ins = nc.tensor.matmul(X[32 * g:32 * g + 32, 2 + b % 2, :], QS[:, g, :], SKT[:, g, :],
                                               start=True, stop=True)
                    ins.then_inc(sem("sc_done"), 1)
                wait(pe, sem("k_evac"), 20 * i + 22)
                for g in range(KV):
                    ins = nc.tensor.transpose(X[:, 0, g:g + 1], NR[0:1, g * P:(g + 1) * P], ident[0:1, 0:1])
                ins.then_inc(sem("new_turned"), 1)
                wait(pe, sem("new_evac"), i + 1)
                for g in range(KV):
                    ins = nc.tensor.matmul(X[32 * g:32 * g + 32, 0, 8:9], QS[:, g, :], KNT[:, g:g + 1], start=True,
                                           stop=True)
                ins.then_inc(sem("new_scored"), 1)
                wait(pe, sem("win_exp"), i + 1)
                wait(pe, sem("sel_read"), 4 * i + 8)
                for t_ in range(4):
                    ins = nc.tensor.transpose(X[:, 3, t_ * P:(t_ + 1) * P], SWP[:, t_ * P:(t_ + 1) * P], ident[:])
                ins.then_inc(sem("p_turned"), 1)
                wait(pe, sem("sel_exp"), i + 1)
                for q in range(4):
                    if q >= 1:
                        wait(pe, sem("p_evac"), 6 * i + q)
                    for t_ in range(4):
                        ins = nc.tensor.transpose(X[:, 2 + q % 2, t_ * P:(t_ + 1) * P],
                                                  SC[:, (4 * q + t_) * P:(4 * q + t_ + 1) * P], ident[:])
                    ins.then_inc(sem("p_turned"), 1)
                nc.tensor.transpose(X[0:1, 0, P:2 * P], SC[:, PAGES * P:PAGES * P + 1], ident[:]).then_inc(
                    sem("p_turned"), 1)
                wait(pe, sem("p_evac"), 6 * i + 6)
                wait(pe, sem("sv_landed"), 256 * i + 256)
                for j in range(PAGES):
                    for g in range(KV):
                        nc.tensor.matmul(X[32 * g:32 * g + 32, 1, 0:P], SPT[:, j, 32 * g:32 * g + 32],
                                         SV[:, j, g * P:(g + 1) * P], start=(j == 0), stop=False)
                for g in range(KV):
                    nc.tensor.matmul(X[32 * g:32 * g + 32, 1, 0:P], SPT[0:1, PAGES, 32 * g:32 * g + 32],
                                     NR[0:1, 512 + g * P:512 + (g + 1) * P], start=False, stop=True)
                for t_ in range(4):
                    for g in range(KV):
                        ins = nc.tensor.matmul(X[32 * g:32 * g + 32, 1, P:2 * P], WPT[:, t_, 32 * g:32 * g + 32],
                                               KW[:, t_, 512 + g * P:512 + (g + 1) * P], start=(t_ == 0),
                                               stop=(t_ == 3))
                ins.then_inc(sem("pv_done"), 1)
                wait(pe, sem("o_rows"), i + 1)
                nc.tensor.transpose(X[:, 0, 2 * P:3 * P], OSM[:, 1, :], ident[:]).then_inc(sem("o_turned"), 1)

            pe.wait_ge(sem("os_done"), NS + 1)
            pe.wait_ge(sem("attn_ready"), 2)
            pe.sem_inc(sem("p4_turned"), 4)
            pe.sem_inc(sem("pv4"), 2)

            def unit(w):
                return w // 8, (w // 4) % 2, w % 4

            with pe.Fori(0, KV) as i:
                def score(w):
                    e, br, j = unit(w)
                    wait(pe, sem("p4_exp"), 32 * i + w + 1)
                    nc.tensor.matmul(X[:, w % 4, 0:(j + 1) * P], QC[:, e, j * P:(j + 1) * P],
                                     KTS[:, br, bass.ds(i, 1), 0:(j + 1) * P].rearrange("p a t -> p (a t)"),
                                     start=True, stop=False)
                    nc.tensor.matmul(X[:, w % 4, j * P:(j + 1) * P], IDB[:], CAB[:], start=False,
                                     stop=True).then_inc(sem("s4_done"), 1)

                wait(pe, sem("group_static"), i + 1)
                wait(pe, sem("qc_ready"), i + 1)
                wait(pe, sem("p4_exp"), 32 * i + 4)
                for e in range(REP):
                    ins = nc.tensor.matmul(X[32 * e:32 * e + 32, 0, :], KMG[:], QC[:, e, :], start=True, stop=True)
                ins.then_inc(sem("c4_scored"), 1)
                wait(pe, sem("c4_rows"), i + 1)
                for j in range(TT):
                    ins = nc.tensor.transpose(X[:, 1, j * P:(j + 1) * P], CS[:, j * P:(j + 1) * P], ident[:])
                ins.then_inc(sem("c4_turned"), 1)
                wait(pe, sem("c4_probs"), i + 1)
                for j in range(TT):
                    ins = nc.tensor.transpose(X[:, 0, j * P:(j + 1) * P], CPP[:, j].rearrange("p e n -> p (e n)"),
                                              ident[:])
                ins.then_inc(sem("c4_back"), 1)
                wait(pe, sem("c4_probs_t"), i + 1)
                for w in range(3):
                    score(w)
                for w in range(32):
                    e, br, j = unit(w)
                    if w + 3 < 32:
                        score(w + 3)
                    wait(pe, sem("p4_scaled"), 32 * i + w + 1)
                    wait(pe, sem("pt4_evac"), 32 * i + w + 1)
                    for m in range(j + 1):
                        ins = nc.tensor.transpose(MP[:, 0, w % 2, m * P:(m + 1) * P],
                                                  PR[:, w % 4, m * P:(m + 1) * P], ident[:])
                    ins.then_inc(sem("p4_turned"), 1)
                    if j == 3:
                        o_ = MP[:, 1, e % 2, :]
                        if br == 0:
                            wait(pe, sem("o_used"), 4 * i + e + 1)
                            nc.tensor.matmul(o_, VMG[32 * e:32 * e + 32, :], CPX[32 * e:32 * e + 32, :], start=True,
                                             stop=False)
                        wait(pe, sem("pt4_evac"), 32 * i + w + 3)
                        for m in range(TT):
                            ins = nc.tensor.matmul(o_[:, m * P:SEQ], VB[:, br, m, :], PT_[:, br, m, m * P:SEQ],
                                                   start=False, stop=(br == 1 and m == 3))
                        ins.then_inc(sem("pv4"), 1)

            pe.wait_ge(sem("o_used"), HEADS + 2)
            pe.wait_ge(sem("c4_probs_t"), KV)

            def turn_y(k, slot, n, h):
                bank = 2 * (1 - slot)
                wait(pe, evac[slot], h + 2)
                wait(pe, sem("y_read"), k + 1)
                for j in range(TT):
                    nc.tensor.transpose(pad5(bank)[:, j, :], YT[:, slot, j * P:(j + 1) * P], ident[:])
                nc.tensor.transpose(X[0:NS, bank + 1, 0:P], YT[:, slot, SEQ:T], ident[:]).then_inc(sem("y_turned"), 1)

            pe.sem_inc(sem("y_turned"), 2)

            def out_pass(i, first):
                for c in range(2):
                    n, half = tile_no(N_ODD_OUT, 2, i, c)
                    if first and c == 0:
                        main_split(pe, n, half, 3)
                    else:
                        main(pe, n, half)
                    if not (first and c == 0):
                        pn, (ph, ps_) = tile_no(N_ODD_OUT - 1, 2, i, c)
                        turn_y(2 * i + c - 1, ps_, pn, ph)

            out_pass(0, True)
            with pe.Fori(1, 8) as i:
                out_pass(i, False)
            turn_y(15, (N_ODD_OUT + 15) % 2, N_ODD_OUT + 15, (N_ODD_OUT + 15) // 2)

        @block.scalar
        def _(act):
            act.sem_inc(sem("tail_copied"), 1)
            for q in range(1, 16, 2):
                act.wait_ge(sem("x_turned"), q + 1)
                j, c = q // 4, q % 4
                nc.scalar.copy(A[:, 4 * c:4 * c + 4, j * P:(j + 1) * P],
                               X[:, q % 4, :].rearrange("p (k t) -> p k t", k=4)).then_inc(sem("x_evac1"), 1)
            act.wait_ge(sem("x_turned"), 18)
            nc.scalar.copy(STP[:, 0:4, :], X[:, 1, 0:480].rearrange("p (k t) -> p k t", k=4)).then_inc(
                sem("x_evac1"), 1)
            act.wait_ge(sem("x_evac0"), 9)
            act.wait_ge(sem("x_evac1"), 9)
            act.wait_ge(sem("setup"), SETUP)
            act.wait_ge(sem("setup_set"), 2)
            norm_act(act, 0)
            split_hi(act, 0, (0, 0))

            def evac_p(i, e, slot):
                wait(act, sem("pool_d"), 2 * i + e + 1)
                wait(act, sem("tail_turned"), 2 * i + e + 1)
                nc.scalar.copy(EX[e][:, PAD:PAD + HALF], MP[:, slot, 0, 0:HALF])
                nc.scalar.copy(EX[e][:, PAD + HALF:PAD + SEQ], MP[:, slot, 1, 0:SEQ - HALF])
                nc.scalar.copy(EX[e][:, PAD + SEQ + 15::16], MP[:, slot, 1, SEQ - HALF:HALF]).then_inc(evac[slot], 1)

            def square_v(i, e):
                wait(act, sem("v_turned"), 2 * i + e + 2)
                wait(act, sem("v_ss"), 2 * i + e + 1)
                wait(act, sem("pool_d"), 2 * i + 2)
                nc.scalar.activation(C1[:, 0:TP].rearrange("p (j d) -> p j d", d=P), pad5(0),
                                     ACT.Square).then_inc(sem("v_sq"), 1)

            def copy_tail(i, e):
                wait(act, sem("tail_turned"), 2 * i + e + 3)
                wait(act, sem("tail_out"), 32 * (2 * i + e) + 32)
                nc.scalar.copy(TLP[:], X[0:PAD, 0, 0:P]).then_inc(sem("tail_first"), 1)
                nc.scalar.copy(TLS[:], X[0:NS, 1, 0:P]).then_inc(sem("tail_copied"), 1)

            with act.Fori(0, PG) as i:
                for c, (kind, e) in enumerate(EV):
                    n, half = tile_no(N_EVEN_IN, 10, i, c)
                    nn, nhalf = tile_no(N_EVEN_IN, 10, i, c + 1)
                    slot = half[1]
                    split_hi(act, nn, nhalf)
                    wait(act, mm_done, n + 3)
                    if kind == "v":
                        wait(act, sem("v_turned"), 2 * i + e + 1)
                        nc.scalar.copy(two(VT[:, 0:T]), mp(slot)).then_inc(evac[slot], 1)
                    elif kind == "u":
                        wait(act, sem("u_used"), 2 * i + e + 1)
                        nc.scalar.copy(two(UT[:]), mp(slot)).then_inc(evac[slot], 1)
                        square_v(i, e)
                    elif kind in ("za", "zb"):
                        wait(act, sem("z_used"), 4 * i + (0 if kind == "za" else 2) + e + 1)
                        nc.scalar.activation(two(SZ[:]), mp(slot), ACT.Silu).then_inc(evac[slot], 1)
                    else:
                        evac_p(i, e, slot)
                    if c == 7:
                        copy_tail(i, 0)
                    if c == 8:
                        copy_tail(i, 1)
            act.wait_ge(sem("z_used"), 17)
            act.wait_ge(mm_done, N_EVEN_OUT + 2)
            split_act_act(act, 1)
            with act.Fori(0, 8) as i:
                for c in range(2):
                    n, half = tile_no(N_EVEN_OUT, 2, i, c + 1)
                    split_hi(act, n, half)

            act.wait_ge(evac[0], 29)
            act.wait_ge(evac[1], 29)
            norm_act(act, 1)
            for b in range(2):
                act.sem_inc(sem(f"z_out{b}"), 16)
            act.sem_inc(sem("back_used"), 1)
            act.wait_ge(sem("head_pads"), 4)

            def square_head(m, kq):
                wait(act, sem("head_turned"), m + 3)
                wait(act, sem("h_ss"), kq + 1)
                nc.scalar.activation(SQ1[:], pad5(0), ACT.Square).then_inc(sem("h_sq"), 1)

            with act.Fori(0, KV) as i:
                for c, (kind, col0, br) in enumerate(KVT):
                    n, (h, slot) = tile_no(N_KV, 6, i, c)
                    nn, nhalf = tile_no(N_KV, 6, i, c + 1)
                    split_hi(act, nn, nhalf)
                    wait(act, mm_done, n + 3)
                    wait(act, sem("head_turned"), 6 * i + c + 1)
                    nc.scalar.copy(two(KTT[:, slot, 0:T]), mp(slot)).then_inc(evac[slot], 1)
                    if 1 <= c <= 3:
                        square_head(6 * i + c - 1, 3 * i + c - 1)
                    if c in (3, 4):
                        wait(act, sem("back_turned"), 3 * i + c - 1)
                        nc.scalar.copy(KTS[:, c - 3, bass.ds(i, 1), :].rearrange("p a t -> p (a t)"),
                                       X[:, 2, :]).then_inc(sem("back_used"), 1)
            act.wait_ge(sem("x1_out"), 256)
            with act.Fori(0, KV) as i:
                for c in range(8):
                    n, (h, slot) = tile_no(N_QZ, 8, i, c)
                    nn, nhalf = tile_no(N_QZ, 8, i, c + 1)
                    split_hi(act, nn, nhalf)
                    wait(act, mm_done, n + 3)
                    if c < 4:
                        wait(act, sem("head_turned"), 24 + 4 * i + c + 1)
                        nc.scalar.copy(two(KTT[:, slot, 0:T]), mp(slot)).then_inc(evac[slot], 1)
                    else:
                        wait(act, sem(f"z_out{slot}"), 32 * i + 16 * (c // 2 - 2) + 16)
                        nc.scalar.activation(two(ZT[:, slot]), mp(slot), ACT.Silu).then_inc(evac[slot], 1)
                    if 1 <= c <= 4:
                        square_head(24 + 4 * i + c - 1, 12 + 4 * i + c - 1)
                    if 2 <= c <= 5:
                        kq = 12 + 4 * i + c - 2
                        wait(act, sem("back_turned"), kq + 1)
                        nc.scalar.copy(act_tile(4 * i + c - 2), X[:, 2:4, :].rearrange("p b n -> p (b n)")[:, 0:T]
                                       ).then_inc(sem("back_used"), 1)
                    if c >= 4:
                        head = nc.scalar.snap(4 * i + c - 4, min_val=0, max_val=HEADS - 1)
                        wait(act, evac[slot], h + 2)
                        nc.scalar.dma_start(szT_scr[bass.ds(head, 1)].rearrange("a p t -> p (a t)"), ZT[:, slot]
                                            ).then_inc(sem(f"z_out{slot}"), 16)
            act.wait_ge(mm_done, N_GATE + 3)
            nc.scalar.activation(two(GTT[:]), mp(0), ACT.Sigmoid).then_inc(evac[0], 1)
            act.wait_ge(sem("gates_turned"), 1)
            nc.scalar.copy(GT[:].rearrange("p j n -> p (j n)"), X[:, 0, :]).then_inc(sem("gates_copied"), 1)

            act.sem_inc(sem("means_used_a"), 1)
            act.sem_inc(sem("means_used_b"), 1)
            with act.Fori(0, 2) as r:
                for hf in range(2):
                    wait(act, sem("pages_used"), 16 * r + 8 * hf + 8 + 2)
                    it = bass.ds(2 * r + hf, 1)
                    nc.scalar.copy(KMS[:, it, 0:512].rearrange("p a n -> p (a n)"), X[:, 2 * hf, :]).then_inc(
                        sem("k_means"), 1)
                    wait(act, sem("k_means"), 2 * r + hf + 1)
                    wait(act, sem("v_means"), 2 * r + hf + 1)
                    act.sem_inc(sem("means_used_a" if hf == 0 else "means_used_b"), 1)
            for it in range(4):
                r, hf = it // 2, it % 2
                act.wait_ge(sem("km_turned"), it + 1)
                nc.scalar.copy(KMT[:, :, 4 * r:4 * r + 4, 16 * hf:16 * hf + 16],
                               X[:, it, :].rearrange("p (g s n) -> p g s n", g=KV, s=4)[:, :, :, 0:16]).then_inc(
                    sem("kmt_ready"), 1)
            act.wait_ge(sem("cs_shifted"), 1)
            nc.scalar.activation(CE[:], CE[:], ACT.Exp).then_inc(sem("cs_exp"), 1)

            act.wait_ge(sem("oc_ready"), 4)
            act.sem_inc(sem("k_evac"), 2)
            with act.Fori(0, NS) as i:
                for b in range(5):
                    for t_ in range(4):
                        if t_ == 0:
                            wait(act, sem("sc_done"), 5 * i + b + 1)
                        wait(act, sem("k_turned"), 20 * i + 4 * b + t_ + 2)
                        nc.scalar.copy(SKT[:, :, t_ * P:(t_ + 1) * P],
                                       X[:, t_ % 2, :].rearrange("p (g t) -> p g t", g=KV)).then_inc(
                            sem("k_evac"), 1)
                    if b == 1:
                        wait(act, sem("win_max"), i + 1)
                        nc.scalar.activation(SWP[:], X[:, 2, :], ACT.Exp, bias=SST[:, 0:1],
                                             accum_out=SST[:, 1:2]).then_inc(sem("win_exp"), 1)
                wait(act, sem("new_turned"), i + 1)
                nc.scalar.copy(KNT[:], X[:, 0, 0:KV]).then_inc(sem("new_evac"), 1)
                wait(act, sem("sel_max"), i + 1)
                nc.scalar.activation(SC[:], SC[:], ACT.Exp, bias=SST[:, 2:3], accum_out=SST[:, 3:4]).then_inc(
                    sem("sel_exp"), 1)

            act.wait_ge(sem("os_done"), NS + 1)
            act.sem_inc(sem("p4_exp"), 4)
            act.sem_inc(sem("pt4_evac"), 2)
            with act.Fori(0, KV) as i:
                def exp4(w):
                    j = w % 4
                    wait(act, sem("max4"), 32 * i + w + 1)
                    wait(act, sem("p4_turned"), 32 * i + w + 1)
                    wait(act, sem("p4_scaled_sum"), 32 * i + w + 1)
                    nc.scalar.activation(PR[:, w % 4, 0:(j + 1) * P], X[:, w % 4, 0:(j + 1) * P], ACT.Exp,
                                         bias=AMX[:, w % 8:w % 8 + 1], accum_out=ASM[:, w % 8:w % 8 + 1]).then_inc(
                        sem("p4_exp"), 1)

                wait(act, sem("c4_shifted"), i + 1)
                nc.scalar.activation(CX[:], CX[:], ACT.Exp).then_inc(sem("c4_exp"), 1)
                exp4(0)
                for w in range(32):
                    e, br, j = w // 8, (w // 4) % 2, w % 4
                    if w + 1 < 32:
                        exp4(w + 1)
                    wait(act, sem("p4_turned"), 32 * i + w + 5)
                    if j == 0:
                        wait(act, sem("pv4"), 8 * i + 2 * e + br + 1)
                    nc.scalar.copy(PT_[:, br, 0:j + 1, j * P:(j + 1) * P],
                                   MP[:, 0, w % 2, 0:(j + 1) * P].rearrange("p (m t) -> p m t", t=P)).then_inc(
                        sem("pt4_evac"), 1)

            act.wait_ge(sem("o_used"), HEADS + 2)
            for b in range(2):
                act.sem_inc(sem(f"y_out{b}"), 32)
            split_hi(act, N_ODD_OUT, (N_ODD_OUT // 2, N_ODD_OUT % 2))
            split_act_act(act, 3)
            act.sem_inc(sem("y_read"), 1)
            act.sem_inc(sem("y_read"), 1)
            y_p = O["y_prompt"].rearrange("(j p) c -> p j c", p=P)

            def rows_y(k, slot, uses):
                bank = 2 * (1 - slot)
                wait(act, sem("y_turned"), k + 3)
                wait(act, sem(f"y_out{slot}"), 32 * uses + 32)
                nc.scalar.copy(YS[:, slot, 0:TT, :], pad5(bank)[:, 0:TT, :]).then_inc(sem("y_rows"), 1)
                nc.scalar.copy(YS[0:NS, slot, 4, :], X[0:NS, bank + 1, 0:P]).then_inc(sem("y_read"), 1)
                col = k * P if isinstance(k, int) else nc.scalar.snap(k * P, min_val=0, max_val=D - P)
                wait(act, sem("y_rows"), k + 1)
                wait(act, sem("y_read"), k + 3)
                cols = bass.ds(col, P)
                nc.scalar.dma_start(y_p[:, :, cols], YS[:, slot, 0:TT, :]).then_inc(sem(f"y_out{slot}"), 16)
                nc.scalar.dma_start(O["y_sample"][:, cols], YS[0:NS, slot, 4, :]).then_inc(sem(f"y_out{slot}"), 16)

            def out_act(i, first, last):
                for c in range(2):
                    nn, nhalf = tile_no(N_ODD_OUT, 2, i, c + 1)
                    if not (last and c == 1):
                        split_hi(act, nn, nhalf)
                    if not (first and c == 0):
                        rows_y(2 * i + c - 1, (N_ODD_OUT + c - 1) % 2, i - 1 if c == 0 else i)

            out_act(0, True, False)
            with act.Fori(1, 7) as i:
                out_act(i, False, False)
            out_act(7, False, True)
            rows_y(15, (N_ODD_OUT + 15) % 2, 7)

        @block.vector
        def _(dve):
            dve.sem_inc(w_split, 2)
            dve.sem_inc(evac[0], 1)
            dve.sem_inc(evac[1], 1)
            for name, k in (("v_ss", 1), ("s_used", 0), ("u_used", 1), ("z_used", 1), ("y_used", 1), ("pool_d", 2),
                            ("v_mul", 0)):
                if k:
                    dve.sem_inc(sem(name), k)
            seq = Seq(dve, "dve_step")
            for q in range(0, 16, 2):
                dve.wait_ge(sem("x_turned"), q + 1)
                j, c = q // 4, q % 4
                nc.vector.tensor_copy(A[:, 4 * c:4 * c + 4, j * P:(j + 1) * P],
                                      X[:, q % 4, :].rearrange("p (k t) -> p k t", k=4)).then_inc(sem("x_evac0"), 1)
            dve.wait_ge(sem("x_turned"), 17)
            nc.vector.tensor_copy(A[:, :, SEQ:T], X[:, 0, 0:KT * NS].rearrange("p (k t) -> p k t", k=KT)).then_inc(
                sem("x_evac0"), 1)
            dve.wait_ge(sem("x_turned"), 19)
            nc.vector.tensor_copy(STP[:, 4:8, :], X[:, 2, 0:480].rearrange("p (k t) -> p k t", k=4)).then_inc(
                sem("x_evac0"), 1)
            dve.wait_ge(sem("setup"), SETUP)
            for b in range(2):
                dve.wait_ge(sem("x_turned"), 20 + b)
                nc.vector.tensor_tensor(WST[:, 4 * b:4 * b + 4, :],
                                        X[:, 3 * (1 - b), :].rearrange("p (k t) -> p k t", k=4),
                                        TRIL[:].unsqueeze(1).to_broadcast([P, 4, P]), ALU.mult).then_inc(
                    sem("x_evac0"), 1)
            nc.vector.tensor_tensor(DG[:], DI8[:].unsqueeze(1).to_broadcast([P, AH, NS]), over(W00[:], NS),
                                    ALU.mult).then_inc(sem("diag_ready"), 1)
            norm_dve(dve, 0, g_even, 0)
            split_lo(dve, 0, (0, 0))

            def norm_v(i, e):
                wait(dve, sem("v_sq"), 2 * i + e + 1)
                nc.vector.tensor_reduce(SS[:], C1[:, 0:TP].rearrange("p (j d) -> p j d", d=P), AX.X,
                                        ALU.add).then_inc(sem("v_ss"), 1)
                wait(dve, sem("v_rstd"), 2 * i + e + 1)
                wait(dve, sem("s_ready"), 2 * i + e + 1)
                wait(dve, sem("gv_out"), 16 * (2 * i + e) + 16)
                nc.vector.tensor_tensor(VN[:], pad5(0), over(SR[:], P), ALU.mult).then_inc(sem("v_mul"), 1)

            def add_bias(i, e):
                wait(dve, sem("s_ready"), 2 * i + e + 2)
                bs = BS[:, bass.ds((2 * i + e) * P, P)]
                dst = A[:, bass.ds(2 * i + e, 1), :]
                seq.do(nc.vector.tensor_tensor(dst[:, :, 0:SEQ].rearrange("p a (j t) -> p (a j) t", j=TT),
                                               X[:, 2, :].rearrange("p (j t) -> p j t", j=TT),
                                               bs.unsqueeze(1).to_broadcast([P, TT, P]), ALU.add))
                nc.vector.tensor_tensor(dst[:, :, SEQ:T].rearrange("p a t -> p (a t)"), X[:, 3, 0:NS],
                                        BS[:, bass.ds((2 * i + e) * P, 1)].to_broadcast([P, NS]),
                                        ALU.add).then_inc(sem("s_used"), 1)
                wait(dve, sem("s_used"), 2 * i + e + 1)

            def gate_a(i, e):
                n, (h, slot) = tile_no(N_EVEN_IN, 10, i, 3 * e + 2)
                wait(dve, evac[slot], h + 2)
                nc.vector.tensor_tensor(UT[:], UT[:], SZ[:], ALU.mult).then_inc(sem("z_used"), 1)
                wait(dve, sem("z_used"), 4 * i + e + 2)
                a = act_tile(2 * i + e)
                nc.vector.tensor_tensor(a, a, UT[:], ALU.mult).then_inc(sem("u_used"), 1)

            def pool_chain(i, e):
                n, (h, slot) = tile_no(N_EVEN_IN, 10, i, 6 + e)
                wait(dve, evac[slot], h + 2)
                wait(dve, sem("hist_ready"), 2 * i + e + 1)
                wait(dve, sem("group_ready"), 3 * i + 3)
                wait(dve, sem("y_ready"), 2 * i + 1)
                ex = EX[e]
                seq.do(nc.vector.tensor_tensor(C2[:, 1:EXT], ex[:, 1:EXT], ex[:, 0:EXT - 1], ALU.add))
                src, dst = C2, C1
                lo = 1
                for k, s_ in enumerate((2, 4, 8)):
                    a0 = lo + s_
                    seq.do(nc.vector.scalar_tensor_tensor(out=dst[:, a0:EXT], in0=src[:, a0 - s_:EXT - s_],
                                                          scalar=PARG[:, k:k + 1], in1=src[:, a0:EXT],
                                                          op0=ALU.mult, op1=ALU.add))
                    src, dst, lo = dst, src, a0
                s0 = PAD + SEQ + 15
                seq.do(nc.vector.scalar_tensor_tensor(out=PD[:, e, 0:SEQ], in0=src[:, PAD:PAD + SEQ],
                                                      scalar=PARG[:, 3:4], in1=ex[:, PAD:PAD + SEQ],
                                                      op0=ALU.mult, op1=ALU.subtract))
                seq.do(nc.vector.scalar_tensor_tensor(out=PD[:, e, SEQ:T], in0=src[:, s0::16],
                                                      scalar=PARG[:, 3:4], in1=ex[:, s0::16],
                                                      op0=ALU.mult, op1=ALU.subtract))
                seq.do(nc.vector.tensor_tensor(FIX[:], src[:, PAD:2 * PAD], PARG[:, 4:4 + PAD], ALU.mult))
                nc.vector.tensor_tensor(PD[:, e, 0:PAD], FIX[:], ex[:, PAD:2 * PAD],
                                        ALU.subtract).then_inc(sem("pool_d"), 1)

            def gate_m(i, e):
                wait(dve, sem("y_ready"), 2 * i + e + 2)
                n, (h, slot) = tile_no(N_EVEN_IN, 10, i, 8 + e)
                a = A[:, bass.ds(AH + 2 * i + e, 1), :].rearrange("p a (b t) -> p (a b) t", b=2)
                nc.vector.tensor_scalar(a, X[:, 2:4, 0:HALF], PSG[:, e:e + 1], None, ALU.mult).then_inc(
                    sem("y_used"), 1)
                wait(dve, sem("y_used"), 2 * i + e + 2)
                wait(dve, evac[slot], h + 2)
                a = act_tile(AH + 2 * i + e)
                nc.vector.tensor_tensor(a, a, SZ[:], ALU.mult).then_inc(sem("z_used"), 1)

            dve.wait_ge(sem("xT_out"), 16)
            with dve.Fori(0, PG) as i:
                seq.loop(i, 2 + 14, 0)
                for c, (kind, e) in enumerate(EV):
                    nn, nhalf = tile_no(N_EVEN_IN, 10, i, c + 1)
                    split_lo(dve, nn, nhalf)
                    if kind == "u":
                        norm_v(i, e)
                    if kind == "za":
                        add_bias(i, e)
                        gate_a(i, e)
                    if kind == "p":
                        pool_chain(i, e)
                    if kind == "zb":
                        gate_m(i, e)
            assert seq.n == 16, seq.n
            split_act_dve(dve, 1)
            with dve.Fori(0, 8) as i:
                for c in range(2):
                    nn, nhalf = tile_no(N_EVEN_OUT, 2, i, c + 1)
                    n, (h, slot) = tile_no(N_EVEN_OUT, 2, i, c)
                    split_lo(dve, nn, nhalf)
                    wait(dve, mm_done, n + 3)
                    wait(dve, sem(f"res_landed{c}"), 16 * i + 16)
                    a = A[:, bass.ds(2 * i + c, 1), :].rearrange("p a (b t) -> p (a b) t", b=2)
                    nc.vector.tensor_tensor(a, mp(slot), two(XR[:, slot]), ALU.add).then_inc(evac[slot], 1)

            norm_dve(dve, 1, g_odd, 2)
            dve.sem_inc(sem("rows_read"), 1)
            dve.sem_inc(sem("h_ss"), 1)
            dve.sem_inc(sem("vm_used"), 1)
            dve.wait_ge(sem("head_pads"), 4)

            def norm_head(m, kq, slot):
                wait(dve, sem("h_sq"), kq + 1)
                nc.vector.tensor_reduce(HS[:], SQ1[:], AX.X, ALU.add).then_inc(sem("h_ss"), 1)
                wait(dve, sem("h_rstd"), kq + 1)
                nc.vector.tensor_tensor(KN[:, slot], pad5(0), over(HR[:], P), ALU.mult).then_inc(
                    sem("rows_read"), 1)

            with dve.Fori(0, KV) as i:
                for c, (kind, col0, br) in enumerate(KVT):
                    nn, nhalf = tile_no(N_KV, 6, i, c + 1)
                    split_lo(dve, nn, nhalf)
                    for t_ in ([4, 5] if c == 5 else [c - 1] if c else []):
                        slot = t_ % 2
                        wait(dve, sem(f"rows_out{slot}"), 32 * (3 * i + t_ // 2) + 32)
                        if t_ < 2:
                            wait(dve, sem("v_copied"), 2 * i + 1 + t_)
                        elif t_ < 5:
                            wait(dve, sem("back_turned"), 3 * i + t_ - 1)
                        else:
                            wait(dve, sem("vm_done"), i + 1)
                        if t_ < 3:
                            norm_head(6 * i + t_, 3 * i + t_, slot)
                        else:
                            wait(dve, sem("head_turned"), 6 * i + t_ + 3)
                            nc.vector.tensor_copy(KN[:, slot], pad5(0)).then_inc(sem("rows_read"), 1)
                            if t_ == 3:
                                wait(dve, sem("rows_read"), 6 * i + 5)
                                dve.sem_inc(sem("vc_rows"), 1)
                    if c == 2:
                        wait(dve, sem("back_turned"), 3 * i + 1)
                        nc.vector.tensor_reduce(KSUM[:], X[:, 2, :].rearrange("p (b t) -> p b t", t=64), AX.X,
                                                ALU.add).then_inc(sem("ksum"), 1)
                        wait(dve, sem("ksum"), i + 1)
                        dve.sem_inc(sem("back_used"), 1)
                        nc.vector.tensor_scalar(KM[:, bass.ds(i, 1), 0:8].rearrange("p a n -> p (a n)"), KSUM[:],
                                                1.0 / 64, None, ALU.mult).then_inc(sem("km_ready"), 1)
                wait(dve, sem("vm_done"), i + 1)
                nc.vector.tensor_copy(VM4[:, bass.ds(i, 1), :].rearrange("p a n -> p (a n)"), X[:, 3, 0:P]).then_inc(
                    sem("vm_used"), 1)
            dve.wait_ge(sem("v_copied"), 10)
            for b in range(2):
                dve.wait_ge(sem(f"rows_out{b}"), 32 * 12 + 32)
            with dve.Fori(0, KV) as i:
                for c in range(8):
                    nn, nhalf = tile_no(N_QZ, 8, i, c + 1)
                    split_lo(dve, nn, nhalf)
                    if 1 <= c <= 4:
                        kq = 12 + 4 * i + c - 1
                        wait(dve, sem("back_turned"), kq - 1)
                        norm_head(24 + 4 * i + c - 1, kq, (c - 1) % 2)
            dve.wait_ge(sem("back_used"), 29)
            nc.vector.tensor_scalar(QP[:, :, :, 0:REP],
                                    A[:, :, SEQ:T].rearrange("p (g h) s -> p s g h", g=KV), SCALE, None,
                                    ALU.mult).then_inc(sem("qp_ready"), 1)
            dve.wait_ge(sem("gates_turned"), 1)
            seq.base, seq.n = 16 * PG, 0
            dve.wait_ge(mm_done, N_GATE + 3)
            seq.do(nc.vector.memset(G8[:], 0.0))
            for b in range(3):
                nc.vector.tensor_copy(G8[:, b].rearrange("s (g n) -> s g n", g=KV)[:, :, 0:REP],
                                      X[0:NS, 1, 0:48].rearrange("s (g h b) -> s g h b", g=KV, h=REP)[:, :, :, b]
                                      ).then_inc(sem("gate8_ready"), 1)
            dve.wait_ge(sem("gates_turned"), 2)
            nc.vector.tensor_copy(GS[:], X[:, 1, P:P + 3 * NS].rearrange("p (b s) -> p b s", b=3)).then_inc(
                sem("gates_copied"), 1)

            with dve.Fori(0, 2) as r:
                for hf in range(2):
                    wait(dve, sem("pages_used"), 16 * r + 8 * hf + 8 + 2)
                    it = bass.ds(2 * r + hf, 1)
                    nc.vector.tensor_copy(KMS[:, it, 512:1024].rearrange("p a n -> p (a n)"),
                                          X[:, 2 * hf + 1, :]).then_inc(sem("v_means"), 1)
            xs = X[:, 0, 0:NS * 32].rearrange("p (s n) -> p s n", n=32)
            seq2 = Seq(dve, "dve_step", 16 * PG + 1)
            dve.wait_ge(sem("cs_done"), 1)
            seq2.do(nc.vector.tensor_reduce(CM[:], xs, AX.X, ALU.max))
            nc.vector.tensor_tensor(CE[:], xs, over(CM[:], 32), ALU.subtract).then_inc(sem("cs_shifted"), 1)
            dve.wait_ge(sem("cs_exp"), 1)
            seq2.do(nc.vector.tensor_reduce(CR[:], CE[:], AX.X, ALU.add))
            seq2.do(nc.vector.reciprocal(CR[:], CR[:]))
            nc.vector.tensor_tensor(CE[:], CE[:], over(CR[:], 32), ALU.mult).then_inc(sem("cp_ready"), 1)
            dve.wait_ge(sem("cp_ready"), 1)
            nc.vector.memset(CP[:], 0.0).then_inc(sem("cpad_ready"), 1)
            dve.wait_ge(sem("cpad_ready"), 1)
            for it in range(4):
                r, hf = it // 2, it % 2
                nc.vector.tensor_copy(CP[:, it, :, 0:16], CE[:, 4 * r:4 * r + 4, 16 * hf:16 * hf + 16]).then_inc(
                    sem("cpad_ready"), 1)
            dve.wait_ge(sem("imp_done"), 1)
            nc.vector.tensor_copy(IMP[:], X[:, 1, 0:NS * 32].rearrange("p (s n) -> p s n", n=32)).then_inc(
                sem("imp_copied"), 1)
            dve.wait_ge(sem("cpt_turned"), 1)
            nc.vector.tensor_copy(CPT[:].rearrange("p i n -> p (i n)"), X[:, 2, :]).then_inc(sem("cpt_ready"), 1)
            dve.wait_ge(sem("imp_copied"), 1)
            dve.wait_ge(sem("cmp_consts"), 48)
            seq2.do(nc.vector.memset(SBIAS[:], 0.0))
            bef = BEF[:].rearrange("p (i j) -> p i j", j=30)
            with dve.Fori(0, NS) as i:
                seq3 = Seq(dve, "dve_step", 0)
                seq3.loop(i, 6, 69)
                v = IMP[:, bass.ds(i, 1), 1:31]
                v_j = v.to_broadcast([P, 30, 30])
                v_i = v.rearrange("p a n -> p (a n)").unsqueeze(2).to_broadcast([P, 30, 30])
                seq3.do(nc.vector.tensor_tensor(RK1[:], v_j, v_i, ALU.is_gt))
                seq3.do(nc.vector.tensor_tensor(RK2[:], v_j, v_i, ALU.is_equal))
                seq3.do(nc.vector.tensor_tensor(RK2[:], RK2[:], bef, ALU.mult))
                seq3.do(nc.vector.tensor_tensor(RK1[:], RK1[:], RK2[:], ALU.add))
                seq3.do(nc.vector.tensor_reduce(RNK[:], RK1[:], AX.X, ALU.add))
                seq3.do(nc.vector.tensor_scalar(SBIAS[:, bass.ds(i, 1), 1:31].rearrange("p a n -> p (a n)"), RNK[:],
                                                NSEL_FREE - 0.5, NEG, ALU.is_ge, ALU.mult))
                dve.sem_inc(held, 1)
            dve.wait_ge(sem("oc_done"), 1)
            dve.wait_ge(sem("gates_copied"), 2)
            for s4 in range(4):
                nc.vector.tensor_tensor(OC[:, s4::4, :], X[:, s4, 0:2 * P].rearrange("p (r n) -> p r n", r=2),
                                        over(GS[:, 0, s4::4], P), ALU.mult).then_inc(sem("oc_ready"), 1)
            dve.wait_ge(sem("oc_ready"), 4)

            dve.sem_inc(sem("sel_read"), 4)
            dve.sem_inc(sem("os_done"), 1)
            seq4 = Seq(dve, "dve_step", 0)
            with dve.Fori(0, NS) as i:
                seq4.loop(i, 5, 117)
                nc.vector.tensor_copy(QS[:], QP[:, bass.ds(i, 1)].rearrange("p a g n -> p (a g) n")).then_inc(
                    sem("q_static"), 1)
                wait(dve, sem("sc_done"), 5 * i + 2)
                nc.vector.tensor_reduce(SST[:, 0:1], X[:, 2, :], AX.X, ALU.max, negate=True).then_inc(
                    sem("win_max"), 1)
                for b in range(1, 5):
                    wait(dve, sem("sc_done"), 5 * i + b + 2)
                    sb_ = SBIAS[:, bass.ds(i, 1), 8 * (b - 1):8 * b].rearrange("p a n -> p (a n)")
                    nc.vector.tensor_tensor(SC[:, (b - 1) * 512:b * 512].rearrange("p (n t) -> p n t", t=64),
                                            X[:, 2 + b % 2, :].rearrange("p (n t) -> p n t", t=64),
                                            over(sb_, 64), ALU.add).then_inc(sem("sel_read"), 1)
                wait(dve, sem("new_scored"), i + 1)
                seq4.do(nc.vector.tensor_copy(SC[:, PAGES * P:PAGES * P + 1], X[:, 0, 8:9]))
                wait(dve, sem("sel_read"), 4 * i + 8)
                nc.vector.tensor_reduce(SST[:, 2:3], SC[:], AX.X, ALU.max, negate=True).then_inc(sem("sel_max"), 1)
                for q in range(6):
                    wait(dve, sem("p_turned"), 6 * i + q + 1)
                    if q == 0:
                        ins = nc.vector.tensor_copy(WPT[:].rearrange("p t n -> p (t n)"), X[:, 3, :])
                    elif q < 5:
                        ins = nc.vector.tensor_copy(SPT[:, 4 * (q - 1):4 * q, :].rearrange("p t n -> p (t n)"),
                                                    X[:, 2 + (q - 1) % 2, :])
                    else:
                        ins = nc.vector.tensor_copy(SPT[0:1, PAGES, :], X[0:1, 0, P:2 * P])
                    ins.then_inc(sem("p_evac"), 1)
                wait(dve, sem("sel_exp"), i + 1)
                seq4.do(nc.vector.reciprocal(SST[:, 4:6], SST[:, 1:4:2]))
                seq4.do(nc.vector.tensor_tensor(SST[:, 6:7], SST[:, 4:5], GS[:, 2, bass.ds(i, 1)], ALU.mult))
                seq4.do(nc.vector.tensor_tensor(SST[:, 7:8], SST[:, 5:6], GS[:, 1, bass.ds(i, 1)], ALU.mult))
                wait(dve, sem("pv_done"), i + 2)
                seq4.do(nc.vector.scalar_tensor_tensor(out=OSM[:, 0], in0=X[:, 1, 0:P], scalar=SST[:, 7:8],
                                                       in1=OC[:, bass.ds(i, 1), :].rearrange("p a n -> p (a n)"),
                                                       op0=ALU.mult, op1=ALU.add))
                nc.vector.scalar_tensor_tensor(out=OSM[:, 1], in0=X[:, 1, P:2 * P], scalar=SST[:, 6:7],
                                               in1=OSM[:, 0], op0=ALU.mult, op1=ALU.add).then_inc(sem("o_rows"), 1)
                wait(dve, sem("o_turned"), i + 1)
                nc.vector.tensor_copy(A[:, :, bass.ds(SEQ + i, 1)].rearrange("p (g h) a -> p g (h a)", g=KV),
                                      X[:, 0, 2 * P:3 * P].rearrange("p (g n) -> p g n", g=KV)[:, :, 0:REP]
                                      ).then_inc(sem("os_done"), 1)

            dve.wait_ge(sem("os_done"), NS + 1)
            dve.wait_ge(sem("attn_consts"), 48)
            nc.vector.tensor_copy(CAB[:], CAU[:]).then_inc(sem("attn_ready"), 1)
            nc.vector.tensor_copy(IDB[:], ident[:]).then_inc(sem("attn_ready"), 1)
            seq5 = Seq(dve, "dve_step", 157)
            seq5.do(nc.vector.memset(CPP[:], 0.0))
            dve.sem_inc(sem("p4_scaled_sum"), 8)
            dve.sem_inc(sem("o_used"), 2)
            with dve.Fori(0, KV) as i:
                seq5.loop(i, 7 + 32 + 4, 158)
                wait(dve, sem("pv4"), 8 * i + 2)
                nc.vector.tensor_scalar(QC[:], A[:, bass.ds(4 * i, REP), 0:SEQ], SCALE, None, ALU.mult).then_inc(
                    sem("qc_ready"), 1)
                wait(dve, sem("c4_scored"), i + 1)
                nc.vector.tensor_copy(CS[:], X[:, 0, :]).then_inc(sem("c4_rows"), 1)
                wait(dve, sem("c4_turned"), i + 1)
                cx = CX[:].rearrange("p j e n -> p (j e) n")
                x1 = X[:, 1, :].rearrange("p (q n) -> p q n", n=32)[:, :, 0:8]
                seq5.do(nc.vector.tensor_tensor(cx, x1, CBI[:].rearrange("p j e n -> p (j e) n"), ALU.add))
                cm, cs_ = CMX[:].rearrange("p j e -> p (j e)"), CSM[:].rearrange("p j e -> p (j e)")
                seq5.do(nc.vector.tensor_reduce(cm, cx, AX.X, ALU.max))
                nc.vector.tensor_tensor(cx, cx, over(cm, 8), ALU.subtract).then_inc(sem("c4_shifted"), 1)
                wait(dve, sem("c4_exp"), i + 1)
                seq5.do(nc.vector.tensor_reduce(cs_, cx, AX.X, ALU.add))
                seq5.do(nc.vector.reciprocal(cs_, cs_))
                g0 = GT[:, :, bass.ds(12 * i, 12)].rearrange("p j (e b) -> p j e b", b=3)[:, :, :, 0]
                seq5.do(nc.vector.tensor_tensor(CSM[:], CSM[:], g0, ALU.mult))
                seq5.do(nc.vector.tensor_tensor(cx, cx, over(cs_, 8), ALU.mult))
                nc.vector.tensor_tensor(CPP[:].rearrange("p j e n -> p (j e) n")[:, :, 0:8], cx,
                                        COK[:].rearrange("p j e n -> p (j e) n"), ALU.mult).then_inc(
                    sem("c4_probs"), 1)
                wait(dve, sem("c4_back"), i + 1)
                seq5.do(nc.vector.tensor_copy(CPX[:], X[:, 0, :]))
                dve.sem_inc(sem("c4_probs_t"), 1)

                def max4(w):
                    j = w % 4
                    wait(dve, sem("s4_done"), 32 * i + w + 1)
                    nc.vector.tensor_reduce(AMX[:, w % 8:w % 8 + 1], X[:, w % 4, 0:(j + 1) * P], AX.X, ALU.max,
                                            negate=True).then_inc(sem("max4"), 1)

                max4(0)
                max4(1)
                for w in range(32):
                    e, br, j = w // 8, (w // 4) % 2, w % 4
                    if w + 2 < 32:
                        max4(w + 2)
                    wait(dve, sem("p4_exp"), 32 * i + w + 5)
                    seq5.do(nc.vector.reciprocal(AW[:, w % 8:w % 8 + 1], ASM[:, w % 8:w % 8 + 1]))
                    dve.sem_inc(sem("p4_scaled_sum"), 1)
                    nc.vector.tensor_scalar(PR[:, w % 4, 0:(j + 1) * P], PR[:, w % 4, 0:(j + 1) * P],
                                            AW[:, w % 8:w % 8 + 1], GT[:, j, bass.ds(12 * i + 3 * e + 1 + br, 1)],
                                            ALU.mult, ALU.mult).then_inc(sem("p4_scaled"), 1)
                    for e2 in ([e - 1] if w % 8 == 3 and e >= 1 else []) + ([3] if w == 31 else []):
                        wait(dve, sem("pv4"), 8 * i + 2 * e2 + 4)
                        wait(dve, sem(f"sz_landed{e2 % 2}"), 32 * i + 16 * (e2 // 2) + 16)
                        a = A[:, bass.ds(4 * i + e2, 1), :].rearrange("p a t -> p (a t)")
                        seq5.do(nc.vector.tensor_tensor(a[:, SEQ:T], a[:, SEQ:T], SZH[:, e2 % 2, SEQ:T], ALU.mult))
                        nc.vector.tensor_tensor(a[:, 0:SEQ], MP[:, 1, e2 % 2, :], SZH[:, e2 % 2, 0:SEQ],
                                                ALU.mult).then_inc(sem("o_used"), 1)
                assert seq5.n == 43, seq5.n

            dve.sem_inc(held, 1)
            split_lo(dve, N_ODD_OUT, (N_ODD_OUT // 2, N_ODD_OUT % 2))
            split_act_dve(dve, 3)

            def out_dve(i, last):
                for c in range(2):
                    n, (h, slot) = tile_no(N_ODD_OUT, 2, i, c)
                    nn, nhalf = tile_no(N_ODD_OUT, 2, i, c + 1)
                    if not (last and c == 1):
                        split_lo(dve, nn, nhalf)
                    wait(dve, mm_done, n + 3)
                    wait(dve, sem(f"res_landed{slot}"), 128 + 16 * i + 16)
                    wait(dve, sem("y_turned"), 2 * i + c + 1)
                    nc.vector.tensor_tensor(two(YT[:, slot]), mp(slot), two(XR[:, slot]), ALU.add).then_inc(
                        evac[slot], 1)

            with dve.Fori(0, 7) as i:
                out_dve(i, False)
            out_dve(7, True)

        @block.gpsimd
        def _(pool):
            pseq = Seq(pool, "pool_step")
            nc.gpsimd.memset(eps_t[:], EPS).then_inc(sem("setup_set"), 1)
            nc.gpsimd.memset(mhalf[:], -0.5).then_inc(sem("setup_set"), 1)
            nc.gpsimd.dma_start(STR[:], I["state_pool"].rearrange("s r c -> (s r) c")).then_inc(
                sem("raw_landed"), 16)
            nc.gpsimd.dma_start(WSR[:], I["w_spatial"].rearrange("h i j -> i h j")).then_inc(
                sem("raw_landed"), 16)
            loads = [(ones[:], cst("ones")), (TRIL[:], cst("tril_t")), (DI8[:], cst("diag8")),
                     (PAR[:], cst("pool").rearrange("p (g n) -> p g n", g=PG)),
                     (g_even[:], I["norm_even"].rearrange("(k p) -> p k", p=P)),
                     (g_odd[:], I["norm_odd"].rearrange("(k p) -> p k", p=P)),
                     (VG[:], I["v_norm"].partition_broadcast(P)),
                     (BS[:], I["b_spatial"].rearrange("h i -> (h i)").partition_broadcast(P)),
                     (W00[:], I["w_spatial"][:, 0, 0].partition_broadcast(P)),
                     (PSC[:], I["pool_scale"].rearrange("(g e p) -> p g e", g=PG, p=P))]
            loads += [(WP[:, g], I["w_pool"][g].rearrange("(c p) e -> p c e", p=P)) for g in range(PG)]
            with nc.allow_non_contiguous_dma(reason="a few parameters, one element per row"):
                for dst, src in loads:
                    nc.gpsimd.dma_start(dst, src).then_inc(sem("setup"), 16)
            assert SETUP == 16 * len(loads)
            for lo, hi, s_ in ((0, 2, "gv_out"), (2, 5, "tail_out"), (5, 8, "tail_out")):
                nc.gpsimd.dma_start(O["pool_sample"][lo:hi, 0:PAD - 1, :], I["state_pool"][lo:hi, 1:PAD, :]).then_inc(
                    sem(s_), 16)
            pool.wait_ge(sem("x_evac0"), 9)
            pool.wait_ge(sem("x_evac1"), 9)
            nc.gpsimd.dma_start(xT_scr.rearrange("k p t -> p k t"), A[:]).then_inc(sem("xT_out"), 16)
            pool.wait_ge(sem("lo_done"), KT)
            pool.wait_ge(sem("x_evac0"), 12)
            nc.gpsimd.memset(VT[:, T:TP], 0.0).then_inc(sem("pads"), 1)
            for e in range(2):
                nc.gpsimd.memset(EX[e][:, 0:PAD], 0.0).then_inc(sem("pads"), 1)
            pool.wait_ge(sem("pads"), 3)

            with pool.Fori(0, PG) as i:
                pseq.loop(i, 2, 0)
                wait(pool, sem("y_ready"), 2 * i + 1)
                wait(pool, sem("y_used"), 2 * i + 1)
                wait(pool, sem("pool_d"), 2 * i + 2)
                nc.gpsimd.tensor_copy(PARG[:], PAR[:, bass.ds(i, 1), :].rearrange("p a n -> p (a n)")).then_inc(
                    sem("group_ready"), 1)
                nc.gpsimd.tensor_copy(PSG[:], PSC[:, bass.ds(i, 1), :].rearrange("p a n -> p (a n)")).then_inc(
                    sem("group_ready"), 1)
                nc.gpsimd.tensor_copy(WPG[:], WP[:, bass.ds(i, 1)].rearrange("p a c e -> p (a c) e")).then_inc(
                    sem("group_ready"), 1)
                for e in range(2):
                    wait(pool, sem("tail_turned"), 2 * i + e + 1)
                    hist = EX[e][:, PAD + SEQ:EXT].rearrange("p (s r) -> p s r", r=16)[:, :, 0:PAD]
                    nc.gpsimd.tensor_copy(hist, STP[:, bass.ds(2 * i + e, 1), :].rearrange(
                        "p a (s r) -> p (a s) r", r=PAD)).then_inc(sem("hist_ready"), 1)
                for e in range(2):
                    wait(pool, sem("v_ss"), 2 * i + e + 2)
                    pseq.do(nc.gpsimd.tensor_scalar(SR[:], SS[:], 1.0 / P, EPS, ALU.mult, ALU.add))
                    nc.gpsimd.tensor_tensor(SR[:], SR[:], mhalf[:, 0:5], ALU.pow).then_inc(sem("v_rstd"), 1)
                    wait(pool, sem("v_mul"), 2 * i + e + 1)
                    vg = VG[:, bass.ds((2 * i + e) * P, P)].unsqueeze(1).to_broadcast([P, 5, P])
                    nc.gpsimd.tensor_tensor(VN[:], VN[:], vg, ALU.mult).then_inc(sem("v_ready"), 1)
                    col = nc.gpsimd.snap((2 * i + e) * P, min_val=0, max_val=1024 - P)
                    wait(pool, sem("v_ready"), 2 * i + e + 1)
                    nc.gpsimd.dma_start(O["gmlp_v_sample"][:, bass.ds(col, P)], VN[0:NS, 4, :]).then_inc(
                        sem("gv_out"), 16)
                for e in range(2):
                    col = nc.gpsimd.snap((2 * i + e) * P, min_val=0, max_val=1024 - P)
                    wait(pool, sem("tail_copied"), 2 * i + e + 2)
                    wait(pool, sem("tail_first"), 2 * i + e + 1)
                    nc.gpsimd.dma_start(O["pool_prompt"][:, bass.ds(col, P)], TLP[:]).then_inc(sem("tail_out"), 16)
                    nc.gpsimd.dma_start(O["pool_sample"][:, PAD - 1, bass.ds(col, P)], TLS[:]).then_inc(
                        sem("tail_out"), 16)
            with pool.Fori(0, 8) as i:
                for c in range(2):
                    n, (h, slot) = tile_no(N_EVEN_OUT, 2, i, c)
                    kt = nc.gpsimd.snap(2 * i + c, min_val=0, max_val=KT - 1)
                    wait(pool, evac[slot], h + 2)
                    nc.gpsimd.dma_start(x1_scr[bass.ds(kt, 1)].rearrange("a p t -> p (a t)"),
                                        act_tile(2 * i + c)).then_inc(sem("x1_out"), 16)

            pool.wait_ge(sem("y_used"), 9)
            pool.wait_ge(sem("tail_out"), 32 + 32 * AH)
            pool.wait_ge(evac[0], 29)
            nc.gpsimd.dma_start(GQ[:, 0], I["q_norm"][0].partition_broadcast(P)).then_inc(sem("rows_out0"), 16)
            nc.gpsimd.dma_start(GQ[:, 1:4].rearrange("p a n -> p (a n)"), I["k_norm"].rearrange(
                "a n -> (a n)").partition_broadcast(P)).then_inc(sem("rows_out0"), 16)
            nc.gpsimd.dma_start(COS[:].rearrange("p j n -> p (j n)"), cst("cos")).then_inc(sem("rows_out1"), 16)
            nc.gpsimd.dma_start(SIN[:].rearrange("p j n -> p (j n)"), cst("sin")).then_inc(sem("rows_out1"), 16)
            pool.wait_ge(sem("lo_done"), 3 * KT)
            nc.gpsimd.dma_start(VMASK[:].rearrange("p j n -> p (j n)"), cst("prompt_blocks")).then_inc(
                sem("setup"), 16)
            nc.gpsimd.memset(KTT[:, :, T:TP], 0.0).then_inc(sem("head_pads"), 1)
            nc.gpsimd.memset(KM[:], 0.0).then_inc(sem("head_pads"), 1)
            nc.gpsimd.memset(QP[:], 0.0).then_inc(sem("head_pads"), 1)
            pool.wait_ge(sem("setup"), SETUP + 16)
            for b in range(2):
                pool.wait_ge(sem(f"rows_out{b}"), 32)
            pool.sem_inc(sem("head_pads"), 1)
            pool.sem_inc(sem("v_copied"), 2)
            pseq2 = Seq(pool, "pool_step", 0)

            def finish_head(kq, slot, gain):
                wait(pool, sem("h_ss"), kq + 2)
                pseq2.do(nc.gpsimd.tensor_scalar(HR[:], HS[:], 1.0 / P, EPS, ALU.mult, ALU.add))
                nc.gpsimd.tensor_tensor(HR[:], HR[:], mhalf[:, 0:5], ALU.pow).then_inc(sem("h_rstd"), 1)

            def rotate(m, kq, slot, gain):
                wait(pool, sem("rows_read"), m + 2)
                kn = KN[:, slot]
                pseq2.do(nc.gpsimd.tensor_tensor(kn, kn, GQ[:, gain].unsqueeze(1).to_broadcast([P, 5, P]), ALU.mult))
                x1, x2 = kn[:, :, 0:16], kn[:, :, 16:32]
                pseq2.do(nc.gpsimd.tensor_tensor(RA[:, :, 0:16], x1, COS[:], ALU.mult))
                pseq2.do(nc.gpsimd.tensor_tensor(RA[:, :, 16:32], x2, COS[:], ALU.mult))
                pseq2.do(nc.gpsimd.tensor_tensor(RB[:, :, 0:16], x2, SIN[:], ALU.mult))
                pseq2.do(nc.gpsimd.tensor_tensor(RB[:, :, 16:32], x1, SIN[:], ALU.mult))
                pseq2.do(nc.gpsimd.tensor_tensor(x1, RA[:, :, 0:16], RB[:, :, 0:16], ALU.subtract))
                pseq2.do(nc.gpsimd.tensor_tensor(x2, RA[:, :, 16:32], RB[:, :, 16:32], ALU.add))
                pool.sem_inc(sem("rows_ready"), 1)

            with pool.Fori(0, KV) as i:
                pseq2.loop(i, 8 * 3, 8)
                for c, (kind, col0, br) in enumerate(KVT):
                    slot = c % 2
                    if c < 3:
                        finish_head(3 * i + c, slot, 1 + br)
                        rotate(6 * i + c, 3 * i + c, slot, 1 + br)
                    else:
                        wait(pool, sem("rows_read"), 6 * i + c + 2)
                        if c > 3:
                            nc.gpsimd.tensor_copy(VS[:, br - 1, bass.ds(i, 1)].rearrange("p a j n -> p (a j) n"),
                                                  KN[:, slot, 0:TT, :]).then_inc(sem("v_copied"), 1)
                    col = nc.gpsimd.snap((0 if c < 3 else 512) + i * P, min_val=0, max_val=1024 - P)
                    nc.gpsimd.dma_start(kv_p[br].rearrange("(j p) c -> p j c", p=P)[:, :, bass.ds(col, P)],
                                        KN[:, slot, 0:TT, :]).then_inc(sem(f"rows_out{slot}"), 16)
                    dst = kv_s[br] if br < 2 else kv_s[2][:, 511, :]
                    nc.gpsimd.dma_start(dst[:, bass.ds(col, P)], KN[0:NS, slot, 4, :]).then_inc(
                        sem(f"rows_out{slot}"), 16)
            with pool.Fori(0, KV) as i:
                pseq2.loop(i, 8 * 4, 104)
                for e in range(REP):
                    finish_head(12 + 4 * i + e, e % 2, 0)
                    rotate(24 + 4 * i + e, 12 + 4 * i + e, e % 2, 0)

            pool.wait_ge(sem("os_done"), NS + 1)
            with pool.Fori(0, KV) as i:
                wait(pool, sem("pv4"), 8 * i + 2)
                for br in range(2):
                    nc.gpsimd.tensor_copy(VB[:, br], VS[:, br, bass.ds(i, 1)].rearrange("p a j n -> p (a j) n")
                                          ).then_inc(sem("static_copied"), 1)
                nc.gpsimd.tensor_copy(KMG[:], KM[:, bass.ds(i, 1), :].rearrange("p a n -> p (a n)")).then_inc(
                    sem("static_copied"), 1)
                nc.gpsimd.tensor_copy(VMG[:], VM4[:, bass.ds(i, 1), :].rearrange("p a n -> p (a n)")).then_inc(
                    sem("static_copied"), 1)
                wait(pool, sem("static_copied"), 4 * i + 4)
                pool.sem_inc(sem("group_static"), 1)

NPHYS = 160
SETUP = 16 * 14


def kernel(**inputs):
    import concourse.bacc as bacc
    from concourse.bass_utils import run_bass_kernel_spmd

    nc = bacc.Bacc("TRN2", target_bir_lowering=False, num_devices=1)
    views = {
        "x_prompt": (SEQ, D), "x_sample": (NS, D), "cache_cmp_kv": (-1, P, 1024), "cache_sel_kv": (-1, P, 1024),
        "state_win_kv": (NS, 512, 1024), "state_pool": (NS, PAD, 1024), "page_table": (1, NS * PAGES),
        "norm_even": (D,), "w_in_even": (D, 5120), "v_norm": (1024,), "w_spatial": (AH, P, P),
        "b_spatial": (AH, P), "w_pool": (PG, 256, 256), "pool_scale": (1024,), "w_out_even": (D, D),
        "norm_odd": (D,), "w_in_odd": (D, 7216), "q_norm": (1, P), "k_norm": (3, P), "w_out_odd": (D, D),
    }
    arrays = {name: np.ascontiguousarray(inputs[name]).reshape(shape) for name, shape in views.items()}
    arrays["consts"] = _lay_consts()
    I = {name: nc.dram_tensor(name, a.shape, mybir.dt.from_np(a.dtype), kind="ExternalInput").ap()
         for name, a in arrays.items()}
    outs = [("y_prompt", (SEQ, D)), ("y_sample", (NS, D)),
            ("cmp_kv_prompt", (SEQ, 1024)), ("cmp_kv_sample", (NS, 1024)),
            ("sel_kv_prompt", (SEQ, 1024)), ("sel_kv_sample", (NS, 1024)),
            ("win_kv_prompt", (SEQ, 1024)), ("win_kv_sample", (NS, 512, 1024)),
            ("pool_prompt", (PAD, 1024)), ("pool_sample", (NS, PAD, 1024)), ("gmlp_v_sample", (NS, 1024))]
    O = {name: nc.dram_tensor(name + "_out", shape, F32, kind="ExternalOutput").ap() for name, shape in outs}
    xT_scr = nc.dram_tensor("xT_scr", (KT, P, T), F32, kind="Internal").ap()
    x1_scr = nc.dram_tensor("x1_scr", (KT, P, T), F32, kind="Internal").ap()
    szT_scr = nc.dram_tensor("szT_scr", (KT, P, T), F32, kind="Internal").ap()
    build(nc, I, O, xT_scr, x1_scr, szT_scr)
    r = run_bass_kernel_spmd(nc, [arrays], core_ids=[0]).results[0]
    shapes = {"y_prompt": (1, SEQ, D), "y_sample": (NS, 1, D), "pool_prompt": (1, 1, PAD, 1024),
              "pool_sample": (1, NS, PAD, 1024), "gmlp_v_sample": (1, NS, 1, 1024),
              "cmp_kv_prompt": (1, 1, SEQ, 2, KV, HD), "cmp_kv_sample": (1, NS, 1, 2, KV, HD),
              "sel_kv_prompt": (1, 1, SEQ, 2, KV, HD), "sel_kv_sample": (1, NS, 1, 2, KV, HD),
              "win_kv_prompt": (1, 1, SEQ, 2, KV, HD), "win_kv_sample": (1, NS, 512, 2, KV, HD)}
    return tuple(r[name + "_out"].reshape(shapes[name]) if name in shapes else r[name + "_out"] for name, _ in outs)
```

```python
from contextlib import ExitStack

import numpy as np
import concourse.bass as bass
from concourse import mybir

F32 = mybir.dt.float32
F32R = mybir.dt.float32r
BF16 = mybir.dt.bfloat16
I32 = mybir.dt.int32
ALU = mybir.AluOpType
ACT = mybir.ActivationFunctionType
AX = mybir.AxisListType

P = 128
D = 2048
KT = D // P
SEQ = 512
NS = 8
T = SEQ + NS
HALF = T // 2
TT = SEQ // P
TP = 5 * P
EPS = 1e-6
AH = 8
PG = 4
PAD = 15
HEADS = 16
KV = 4
REP = HEADS // KV
HD = 128
PAGES = 16
NBLK = 32
NSEL_FREE = 13
NEG = -1e30
SCALE = HD ** -0.5
PAST = 2048
EXT = PAD + SEQ + NS * 16

N_EVEN_IN, N_EVEN_OUT, N_KV, N_QZ, N_GATE, N_ODD_OUT = 0, 40, 56, 80, 112, 113

CONSTS = {}


def _lay_consts():
    parts, at = [], 0

    def put(name, a):
        nonlocal at
        a = np.asarray(a, np.float32).reshape(P, -1)
        CONSTS[name] = (at, a.shape[1])
        parts.append(a)
        at += a.shape[1]

    p = np.arange(P)
    put("ident", np.eye(P))
    put("ones", np.ones((P, P)))
    put("tril_t", p[:, None] <= p[None, :])
    put("diag8", np.eye(P)[:, :NS])
    pos = np.zeros((P, 5), np.float32)
    pos[:, :TT] = p[:, None] + P * np.arange(TT)[None, :]
    pos[:, TT] = PAST
    inv_freq = np.float32(500000.0) ** (-np.arange(16, dtype=np.float32) * np.float32(2.0 / 32))
    ang = (pos[:, :, None] * inv_freq[None, None, :]).astype(np.float32).astype(np.float64)
    cos, sin = np.cos(ang), np.sin(ang)
    put("cos", cos)
    put("sin", sin)
    par = np.zeros((P, PG, 4 + PAD))
    for g, w in enumerate((2, 4, 8, 16)):
        par[:, g, 0:3] = [w >= 4, w >= 8, w >= 16]
        par[:, g, 3] = 1.0 / w
        par[:, g, 4:] = 1.0 / np.minimum(np.arange(PAD) + 1, w)
    put("pool", par)
    bm = np.zeros((P, 8, 32))
    for c in range(8):
        bm[p, c, 2 * c + p // 64] = 1.0 / 64
    put("page_blocks", bm)
    vm = np.zeros((P, TT, REP, 32))
    for j in range(TT):
        vm[p, j, :, 0] = 0
        for h in range(REP):
            vm[p, j, h, 2 * j + p // 64] = 1.0 / 64
    put("prompt_blocks", vm)
    t = p[:, None] + P * np.arange(TT)[None, :]
    ok = ((np.arange(8) + 1) * 64 - 1)[None, None, :] <= t[:, :, None]
    ok4 = np.repeat(ok[:, :, None, :], REP, 2)
    put("cmp_ok", ok4)
    put("cmp_bias", np.where(ok4, 0.0, NEG))
    put("causal", np.where(p[None, :] <= p[:, None], 0.0, NEG))
    rows = np.zeros((P, NS, 32))
    spread = np.zeros((P, NS, P))
    for smp in range(NS):
        for g in range(KV):
            rows[32 * g:32 * g + REP, smp, KV * smp + g] = 1.0
            spread[KV * smp + g, smp, 32 * g:32 * g + 32] = 1.0
    put("imp_rows", rows)
    put("imp_spread", spread)
    i30 = np.arange(30)
    put("before", np.broadcast_to((i30[None, :] < i30[:, None]).reshape(1, -1), (P, 900)))
    return np.ascontiguousarray(np.concatenate(parts, 1))


def build(nc, I, O, xT_scr, x1_scr, szT_scr):
    ctx = ExitStack()
    with ctx:
        base = nc.sbuf_base
        base = (base + 127) // 128 * 128
        LIMIT = nc.sbuf_usable_end

        def at(name, off, shape, dt=F32):
            size = int(np.prod(shape[1:])) * (2 if dt == BF16 else 4)
            assert base + off + size <= LIMIT, (name, base + off + size, LIMIT)
            t_ = nc.alloc_sbuf_tensor_at(name, shape, dt, offset=base + off)
            return t_, off + (size + 31) // 32 * 32

        o = 0
        H_OFF = o
        HH, o = at("act_hi", o, [P, KT, T], F32R)
        HL, o = at("act_lo", o, [P, KT, T], F32R)
        WHL_OFF = o
        WH, o = at("w_hi", o, [P, 2, KT, P], F32R)
        WL, o = at("w_lo", o, [P, 2, KT, P], F32R)
        RAW_OFF = o
        RAW, o = at("w_raw", o, [P, 2, KT, P])
        A, o = at("act", o, [P, KT, T])
        ident, o = at("ident", o, [P, P])
        ones, o = at("ones", o, [P, P])
        g_even, o = at("gain_even", o, [P, KT])
        g_odd, o = at("gain_odd", o, [P, KT])
        eps_t, o = at("eps", o, [P, 1])
        mhalf, o = at("minus_half", o, [P, 8])
        R_OFF = o

        o = R_OFF
        VG, o = at("v_gain", o, [P, AH * P])
        BS, o = at("b_spatial", o, [P, AH * P])
        WST, o = at("w_spatial_t", o, [P, AH, P])
        DG, o = at("w00_diag", o, [P, AH, NS])
        W00, o = at("w00", o, [P, AH])
        WP, o = at("w_pool", o, [P, PG, 2, 256])
        WPG, o = at("w_pool_group", o, [P, 2, 256])
        PSC, o = at("pool_scale", o, [P, PG, 2])
        PAR, o = at("pool_par", o, [P, PG, 4 + PAD])
        PARG, o = at("pool_par_group", o, [P, 4 + PAD])
        PSG, o = at("pool_scale_group", o, [P, 2])
        STP, o = at("pool_state_t", o, [P, AH, NS * PAD])
        E_OFF = o
        VT, o = at("v_t", o, [P, TP])
        VN, o = at("v_norm", o, [P, 5, P])
        C1, o = at("chain1", o, [P, EXT])
        C2, o = at("chain2", o, [P, EXT])
        UT, o = at("u_t", o, [P, T])
        SZ, o = at("silu_z", o, [P, T])
        EX0, o = at("pool_in0", o, [P, EXT])
        EX1, o = at("pool_in1", o, [P, EXT])
        PD, o = at("pool_diff", o, [P, 2, T])
        TLP, o = at("pool_tail", o, [PAD, P])
        TLS, o = at("pool_tail_s", o, [NS, P])
        SS, o = at("v_sumsq", o, [P, 5])
        SR, o = at("v_rstd", o, [P, 5])
        FIX, o = at("pool_fix", o, [P, PAD])
        EX = [EX0, EX1]
        o = E_OFF
        XS, o = at("x_stage", o, [P, 2, D])
        WSR, o = at("w_spatial_raw", o, [P, AH, P])
        STR, o = at("pool_state_raw", o, [NS * PAD, AH * P])
        TRIL, o = at("tril_t", o, [P, P])
        DI8, o = at("diag8", o, [P, NS])
        o = E_OFF
        SQ, o = at("sq", o, [P, 2, T])
        RS, o = at("rstd", o, [P, T])
        TM, o = at("norm_tmp", o, [P, 2, T])
        o = R_OFF
        XR, o = at("residual", o, [P, 2, T])
        YT, o = at("y_t", o, [P, 2, T])
        YS, o = at("y_rows", o, [P, 2, 5, P])

        o = R_OFF
        KTS, o = at("k_t", o, [P, 2, KV, SEQ])
        VS, o = at("v_rows", o, [P, 2, KV, TT, P])
        VM4, o = at("v_cmp_mean", o, [P, KV, P])
        KM, o = at("k_cmp_mean", o, [P, KV, 32])
        GT, o = at("gate_rows", o, [P, TT, P])
        GS, o = at("gate_sample", o, [P, 3, NS])
        QP, o = at("q_sample", o, [P, NS, KV, 32])
        L1_OFF = o
        KTT, o = at("head_t", o, [P, 2, TP])
        KN, o = at("head_rows", o, [P, 2, 5, P])
        SQ1, o = at("head_sq", o, [P, 5, P])
        GQ, o = at("qk_gain", o, [P, 4, P])
        COS, o = at("cos", o, [P, 5, 16])
        SIN, o = at("sin", o, [P, 5, 16])
        RA, o = at("rope_a", o, [P, 5, 32])
        RB, o = at("rope_b", o, [P, 5, 32])
        HS, o = at("head_ss", o, [P, 5])
        HR, o = at("head_rstd", o, [P, 5])
        VMASK, _ = at("prompt_blocks", o, [P, TT, P])
        ZT, o = at("z_t", o, [P, 2, T])
        KSUM, o = at("k_block_sum", o, [P, 8])
        o = L1_OFF
        PTAB, o = at("page_table", o, [1, P], I32)
        SBIAS, o = at("sel_bias", o, [P, NS, NBLK])
        OC, o = at("o_cmp", o, [P, NS, P])
        o = H_OFF
        PGT, o = at("cmp_pages", o, [P, 2, 4, 1024])
        KMS, o = at("cmp_means", o, [P, 4, 1024])
        KMT, o = at("cmp_k_t", o, [P, KV, NS, 32])
        o2 = WHL_OFF
        BM, o2 = at("page_blocks", o2, [P, 8, 32])
        CE, o2 = at("cmp_e", o2, [P, NS, 32])
        CP, o2 = at("cmp_p_pad", o2, [P, 4, 4, 32])
        CPT, o2 = at("cmp_p_t", o2, [P, 4, P])
        CM, o2 = at("cmp_max", o2, [P, NS])
        CR, o2 = at("cmp_sum", o2, [P, NS])
        GROWS, o2 = at("imp_rows", o2, [P, NS, 32])
        GSPR, o2 = at("imp_spread", o2, [P, NS, P])
        IMP, o2 = at("importance", o2, [32, 32])
        LOW, o2 = at("not_selected", o2, [32, 32])
        BEF, o2 = at("before", o2, [P, 900])
        RK1, o2 = at("rank1", o2, [32, 30, 30])
        RK2, o2 = at("rank2", o2, [32, 30, 30])
        RNK, o2 = at("rank", o2, [32, 30])
        GTT, o2 = at("gate_t", o2, [P, T])
        G8, o2 = at("gate8", o2, [NS, 3, P])
        assert o2 <= WHL_OFF + 32768
        o = H_OFF
        SK, o = at("sel_k", o, [P, 8, 512])
        SV, o = at("sel_v", o, [P, PAGES, 512])
        KWK, o = at("win_k", o, [P, 4, 512])
        KWV, o = at("win_v", o, [P, 4, 512])
        assert o <= WHL_OFF
        o = WHL_OFF
        SC, o = at("scores", o, [P, PAGES * P + 1])
        NRK, o = at("new_k", o, [1, 512])
        NRV, o = at("new_v", o, [1, 512])
        SPT, o = at("p_t", o, [P, 17, P])
        QS, o = at("q_static", o, [P, KV, 32])
        KNT, o = at("new_k_t", o, [P, KV])
        SWP, o = at("win_p", o, [P, SEQ])
        assert o <= WHL_OFF + 32768
        SKT, o = at("sel_k_t", RAW_OFF, [P, 2, KV, 512])
        o = L1_OFF + 8 * 1024
        WPT, o = at("win_p_t", o, [P, 4, P])
        SST, o = at("s_stat", o, [P, 8])
        OSM, o = at("o_sample", o, [P, 2, P])
        o = H_OFF
        VB, o = at("v_static", o, [P, 2, TT, P])
        QC, o = at("q_cmp", o, [P, REP, SEQ])
        PR, o = at("probs", o, [P, 4, SEQ])
        PT_, o = at("probs_t", o, [P, 2, TT, SEQ])
        CS, o = at("cmp_s_t", o, [P, SEQ])
        KMG, o = at("k_mean_static", o, [P, 32])
        VMG, o = at("v_mean_static", o, [P, P])
        o = WHL_OFF
        CPP, o = at("cmp_probs", o, [P, TT, REP, 32])
        CPX, o = at("cmp_probs_t", o, [P, SEQ])
        COK, o = at("cmp_ok", o, [P, TT, REP, 8])
        CBI, o = at("cmp_bias", o, [P, TT, REP, 8])
        CX, o = at("cmp_x", o, [P, TT, REP, 8])
        CMX, o = at("cmp_mx", o, [P, TT, REP])
        CSM, o = at("cmp_sm", o, [P, TT, REP])
        CAU, o = at("causal", o, [P, P])
        CAB, o = at("causal_bf", o, [P, P], BF16)
        IDB, o = at("ident_bf", o, [P, P], BF16)
        AMX, o = at("a_max", o, [P, 8])
        ASM, o = at("a_sum", o, [P, 8])
        AW, o = at("a_w", o, [P, 8])
        SZH, o = at("sz_head", o, [P, 2, T])
        assert o <= WHL_OFF + 32768

        MP = ctx.enter_context(nc.psum_tensor("main", [P, 2, 2, 512], F32))
        X = ctx.enter_context(nc.psum_tensor("aux", [P, 4, 512], F32))

        sems = {}

        def sem(name):
            if name not in sems:
                sems[name] = ctx.enter_context(nc.semaphore(name))
            return sems[name]

        w_landed = [sem("w_landed0"), sem("w_landed1")]
        w_hi, w_split, mm_done = sem("w_hi"), sem("w_split"), sem("mm_done")
        evac = [sem("evac0"), sem("evac1")]
        held = sem("held")

        def wait(eng, s, v):
            eng.wait_ge(s, v)
            if not isinstance(v, int):
                eng.sem_inc(held, 1)

        class Seq:

            def __init__(self, eng, name, base=0):
                self.eng, self.s, self.n, self.base = eng, sem(name), 0, base

            def loop(self, i, per, start):
                self.base, self.n = start + per * i, 0

            def do(self, ins):
                self.n += 1
                ins.then_inc(self.s, 1)
                wait(self.eng, self.s, self.base + self.n)

        def load_w(sp, n, half, src, width=P):
            slot = half[1]
            wait(sp, w_split, n + 1)
            nc.sync.dma_start(RAW[:, slot, :, 0:width], src).then_inc(w_landed[slot], 16)

        def split_hi(act, n, half):
            h, slot = half
            wait(act, w_landed[slot], 16 * h + 16)
            wait(act, mm_done, n + 1)
            nc.scalar.copy(WH[:, slot], RAW[:, slot]).then_inc(w_hi, 1)

        def split_lo(dve, n, half):
            slot = half[1]
            wait(dve, w_hi, n + 1)
            nc.vector.tensor_tensor(WL[:, slot], RAW[:, slot], WH[:, slot].bitcast(F32),
                                    ALU.subtract).then_inc(w_split, 1)

        def main(pe, n, half, first=False):
            h, slot = half
            wait(pe, w_split, n + 3)
            wait(pe, evac[slot], h + 1)
            for k in range(KT):
                if first is not False:
                    wait(pe, first, k + 1)
                for q, (w_, x_) in enumerate(((WH, HH), (WH, HL), (WL, HH))):
                    for b in range(2):
                        ins = nc.tensor.matmul(MP[:, slot, b, 0:HALF], w_[:, slot, k, :],
                                               x_[:, k, b * HALF:(b + 1) * HALF],
                                               start=(k == 0 and q == 0), stop=(k == KT - 1 and q == 2))
            ins.then_inc(mm_done, 1)

        def tile_no(n0, per, i, c):
            return n0 + per * i + c, ((n0 + c) // 2 + (per // 2) * i, (n0 + c) % 2)

        def mp(slot):
            return MP[:, slot, :, 0:HALF]

        def two(ap):
            return ap.rearrange("p (b t) -> p b t", b=2)

        w_even = I["w_in_even"].rearrange("(k p) n -> p k n", p=P)
        w_eout = I["w_out_even"].rearrange("(k p) n -> p k n", p=P)
        w_odd = I["w_in_odd"].rearrange("(k p) n -> p k n", p=P)
        w_oout = I["w_out_odd"].rearrange("(k p) n -> p k n", p=P)

        EV = [("v", 0), ("u", 0), ("za", 0), ("v", 1), ("u", 1), ("za", 1), ("p", 0), ("p", 1), ("zb", 0), ("zb", 1)]
        EV_COL = {"u": 0, "v": 1024, "za": 2048, "p": 3072, "zb": 4096}
        KVT = [("k", 2048, 0), ("k", 3072, 1), ("k", 4096, 2), ("v", 2560, 0), ("v", 3584, 1), ("v", 4608, 2)]
        kv_p = [O.get(b + "_kv_prompt") for b in ("cmp", "sel", "win")]
        kv_s = [O.get(b + "_kv_sample") for b in ("cmp", "sel", "win")]
        QKV_Z, QKV_G = 5168, 5120

        def cst(name):
            a, n_ = CONSTS[name]
            return I["consts"][:, a:a + n_]

        block = ctx.enter_context(nc.Block())

        def pad5(bank):
            return X[:, bank:bank + 2, :].rearrange("p b n -> p (b n)")[:, 0:TP].rearrange("p (j d) -> p j d", d=P)

        def over(ap, n):
            return ap.unsqueeze(2).to_broadcast([ap.shape[0], ap.shape[1], n])

        def window_half(queue, smp, dst, col0, s_):
            cols = slice(col0, col0 + 512)
            win = I["state_win_kv"][bass.ds(smp, 1), :, cols].rearrange("a (p j) c -> p (a j) c", j=4)
            queue.dma_start(dst[1:P], win[1:P]).then_inc(s_, 16)
            queue.dma_start(dst[0:1, 1:4], win[0:1, 1:4]).then_inc(s_, 16)
            queue.dma_start(dst[0:1, 0, :], O["win_kv_sample"][bass.ds(smp, 1), 511, cols]).then_inc(s_, 16)

        def page_at(queue, cache, idx):
            pg = queue.value_load(PTAB[0:1, idx:idx + 1] if isinstance(idx, int) else PTAB[0:1, bass.ds(idx, 1)],
                                  min_val=0, max_val=NPHYS - 1)
            return I[cache][bass.ds(pg, 1)].rearrange("a t c -> t (a c)")

        def act_tile(idx):
            if isinstance(idx, int):
                return A[:, idx, :]
            return A[:, bass.ds(idx, 1), :].rearrange("p a t -> p (a t)")

        @block.sync
        def _(sp):
            nc.sync.dma_start(ident[:], cst("ident")).then_inc(sem("ident_landed"), 16)
            xp = I["x_prompt"].rearrange("(j p) d -> j p d", p=P)
            for j in range(2):
                nc.sync.dma_start(XS[:, j], xp[j]).then_inc(sem(f"x_landed{j}"), 16)
            for j in range(2, 5):
                sp.wait_ge(sem("x_turned"), 4 * (j - 1))
                if j < 4:
                    nc.sync.dma_start(XS[:, j % 2], xp[j]).then_inc(sem(f"x_landed{j % 2}"), 16)
                else:
                    nc.sync.dma_start(XS[0:NS, 0], I["x_sample"]).then_inc(sem("x_landed0"), 16)
            with sp.Fori(0, PG) as i:
                for c, (kind, e) in enumerate(EV):
                    n, half = tile_no(N_EVEN_IN, 10, i, c)
                    col = nc.sync.snap(EV_COL[kind] + (2 * i + e) * P, min_val=0, max_val=4992)
                    load_w(sp, n, half, w_even[:, :, bass.ds(col, P)])
            sp.wait_ge(sem("xT_out"), 16)
            with sp.Fori(0, 8) as i:
                for c in range(2):
                    n, half = tile_no(N_EVEN_OUT, 2, i, c)
                    col = nc.sync.snap((2 * i + c) * P, min_val=0, max_val=D - P)
                    kt = nc.sync.snap(2 * i + c, min_val=0, max_val=KT - 1)
                    load_w(sp, n, half, w_eout[:, :, bass.ds(col, P)])
                    wait(sp, evac[c], half[0] + 1)
                    nc.sync.dma_start(XR[:, c], xT_scr[bass.ds(kt, 1)].rearrange("a p t -> p (a t)")).then_inc(
                        sem(f"res_landed{c}"), 16)
            with sp.Fori(0, KV) as i:
                for c, (kind, col0, br) in enumerate(KVT):
                    n, half = tile_no(N_KV, 6, i, c)
                    col = nc.sync.snap(col0 + i * P, min_val=0, max_val=7216 - P)
                    load_w(sp, n, half, w_odd[:, :, bass.ds(col, P)])
                    if c in (1, 4):
                        smp = nc.sync.snap(2 * i + c // 4, min_val=0, max_val=NS - 1)
                        nc.sync.dma_start(O["win_kv_sample"][bass.ds(smp, 1), 0:511, :].rearrange("a r c -> a (r c)"),
                                          I["state_win_kv"][bass.ds(smp, 1), 1:512, :].rearrange("a r c -> a (r c)")
                                          ).then_inc(sem("win_moved"), 16)
            with sp.Fori(0, KV) as i:
                for c in range(8):
                    n, half = tile_no(N_QZ, 8, i, c)
                    col0 = 0 if c < 4 else QKV_Z
                    col = nc.sync.snap(col0 + (4 * i + c % 4) * P, min_val=0, max_val=7216 - P)
                    load_w(sp, n, half, w_odd[:, :, bass.ds(col, P)])
            load_w(sp, N_GATE, (N_GATE // 2, 0), w_odd[:, :, QKV_G:QKV_G + 48], 48)

            sp.wait_ge(mm_done, N_GATE + 3)
            sp.wait_ge(sem("head_turned"), 42)
            nc.sync.dma_start(PTAB[:], I["page_table"]).then_inc(sem("table_landed"), 16)
            for dst, name in ((BM[:].rearrange("p c n -> p (c n)"), "page_blocks"),
                              (GROWS[:].rearrange("p s n -> p (s n)"), "imp_rows"),
                              (GSPR[:].rearrange("p s n -> p (s n)"), "imp_spread"), (BEF[:], "before")):
                nc.sync.dma_start(dst, cst(name)).then_inc(sem("cmp_consts"), 16)
            sp.wait_ge(sem("table_landed"), 16)
            with sp.Fori(0, 2) as r:
                for hf in range(2):
                    for c in range(8):
                        for s4 in range(4):
                            pg = nc.sync.value_load(PTAB[0:1, bass.ds(64 * r + 16 * s4 + 8 * hf + c, 1)],
                                                    min_val=0, max_val=NPHYS - 1)
                            if s4 == 0:
                                wait(sp, sem("pages_used"), 16 * r + 8 * hf + c + 1)
                            nc.sync.dma_start(PGT[:, c % 2, s4], I["cache_cmp_kv"][bass.ds(pg, 1)].rearrange(
                                "a t c -> t (a c)")).then_inc(sem(f"pages_landed{c % 2}"), 16)

            sp.wait_ge(sem("bias_ready"), 1)
            for b in range(2):
                sp.wait_ge(sem(f"rows_out{b}"), 32 * 12 + 32)

            def key_loads(i, first):
                if not first:
                    wait(sp, sem("k_turned"), 20 * i - 15)
                    wait(sp, sem("new_turned"), i)
                smp = i if first else nc.sync.snap(i, min_val=0, max_val=NS - 1)
                nc.sync.dma_start(NRK[:], O["sel_kv_sample"][bass.ds(smp, 1), 0:512]).then_inc(sem("win_landed"), 16)
                window_half(nc.sync, smp, KWK, 0, sem("win_landed"))
                for j in range(PAGES):
                    page = page_at(nc.sync, "cache_sel_kv", PAGES * i + j)
                    if j >= 8:
                        wait(sp, sem("k_turned"), 20 * i + j - 2)
                    elif not first:
                        wait(sp, sem("k_turned"), 20 * i + j - 6)
                    nc.sync.dma_start(SK[:, j % 8], page[:, 0:512]).then_inc(sem(f"sk_landed{j % 8}"), 16)

            key_loads(0, True)
            with sp.Fori(1, NS) as i:
                key_loads(i, False)

            sp.wait_ge(sem("os_done"), NS + 1)
            for dst, name in ((COK[:], "cmp_ok"), (CBI[:], "cmp_bias")):
                nc.sync.dma_start(dst.rearrange("p j e n -> p (j e n)"), cst(name)).then_inc(sem("attn_consts"), 16)
            nc.sync.dma_start(CAU[:], cst("causal")).then_inc(sem("attn_consts"), 16)
            for b in range(2):
                sp.wait_ge(sem(f"z_out{b}"), 16 * 8 + 16)
            with sp.Fori(0, KV) as i:
                for e in range(REP):
                    head = nc.sync.snap(4 * i + e, min_val=0, max_val=HEADS - 1)
                    wait(sp, sem("o_used"), 4 * i + e + 1)
                    nc.sync.dma_start(SZH[:, e % 2], szT_scr[bass.ds(head, 1)].rearrange("a p t -> p (a t)")).then_inc(
                        sem(f"sz_landed{e % 2}"), 16)

            sp.wait_ge(sem("x1_out"), 256)
            with sp.Fori(0, 8) as i:
                for c in range(2):
                    n, half = tile_no(N_ODD_OUT, 2, i, c)
                    h, slot = half
                    col = nc.sync.snap((2 * i + c) * P, min_val=0, max_val=D - P)
                    kt = nc.sync.snap(2 * i + c, min_val=0, max_val=KT - 1)
                    load_w(sp, n, half, w_oout[:, :, bass.ds(col, P)])
                    wait(sp, evac[slot], h + 1)
                    nc.sync.dma_start(XR[:, slot], x1_scr[bass.ds(kt, 1)].rearrange("a p t -> p (a t)")).then_inc(
                        sem(f"res_landed{slot}"), 16)
            for b in range(2):
                sp.wait_ge(sem(f"y_out{b}"), 32 * 8 + 32)
            sp.wait_ge(sem("win_moved"), 16 * NS)
            sp.wait_ge(sem("gv_out"), 16 + 16 * AH)
            sp.wait_ge(sem("tail_out"), 32 + 32 * AH)

        def norm_act(act, r):
            for k in range(KT):
                if k >= 2:
                    act.wait_ge(sem("norm_summed"), KT * r + k - 1)
                nc.scalar.activation(SQ[:, k % 2], A[:, k, :], ACT.Square).then_inc(sem("norm_sq"), 1)
            act.wait_ge(sem("norm_summed"), KT * (r + 1))
            nc.scalar.activation(two(RS[:]), X[:, 2:4, 0:HALF], ACT.Sqrt, bias=eps_t[:, 0:1],
                                 scale=1.0 / D).then_inc(sem("norm_root"), 1)
            for k in range(KT):
                act.wait_ge(sem("norm_scaled"), KT * r + k + 1)
                nc.scalar.copy(HH[:, k], TM[:, k % 2]).then_inc(sem("hi_done"), 1)

        def norm_dve(dve, r, gain, q):
            dve.wait_ge(sem("norm_root"), r + 1)
            nc.vector.reciprocal(RS[:], RS[:]).then_inc(sem("norm_rstd"), 1)
            dve.wait_ge(sem("norm_rstd"), r + 1)

            def scaled(k):
                if k >= 2:
                    dve.wait_ge(sem("lo_done"), KT * q + k - 1)
                nc.vector.scalar_tensor_tensor(out=TM[:, k % 2], in0=A[:, k, :], scalar=gain[:, k:k + 1],
                                               in1=RS[:], op0=ALU.mult, op1=ALU.mult).then_inc(sem("norm_scaled"), 1)

            scaled(0)
            for k in range(KT):
                if k + 1 < KT:
                    scaled(k + 1)
                dve.wait_ge(sem("norm_scaled"), KT * r + k + 1)
                dve.wait_ge(sem("hi_done"), KT * q + k + 1)
                nc.vector.tensor_tensor(HL[:, k], TM[:, k % 2], HH[:, k].bitcast(F32),
                                        ALU.subtract).then_inc(sem("lo_done"), 1)

        def norm_pe(pe, r):
            for k in range(KT):
                pe.wait_ge(sem("norm_sq"), KT * r + k + 1)
                for b in range(2):
                    ins = nc.tensor.matmul(X[:, 2 + b, 0:HALF], ones[:], SQ[:, k % 2, b * HALF:(b + 1) * HALF],
                                           start=(k == 0), stop=(k == KT - 1))
                ins.then_inc(sem("norm_summed"), 1)

        def split_act_act(act, q):
            for k in range(KT):
                nc.scalar.copy(HH[:, k], A[:, k, :]).then_inc(sem("hi_done"), 1)

        def split_act_dve(dve, q):
            for k in range(KT):
                dve.wait_ge(sem("hi_done"), KT * q + k + 1)
                nc.vector.tensor_tensor(HL[:, k], A[:, k, :], HH[:, k].bitcast(F32),
                                        ALU.subtract).then_inc(sem("lo_done"), 1)

        @block.tensor
        def _(pe):
            pe.sem_inc(mm_done, 2)
            pe.sem_inc(sem("v_turned"), 1)
            pe.sem_inc(sem("s_ready"), 1)
            pe.sem_inc(sem("y_ready"), 1)
            pe.sem_inc(sem("tail_turned"), 2)

            def main_split(pe, n, half, q):
                h, slot = half
                wait(pe, w_split, n + 3)
                wait(pe, evac[slot], h + 1)
                for k in range(KT):
                    pe.wait_ge(sem("lo_done"), KT * q + k + 1)
                    for qq, (w_, x_) in enumerate(((WH, HH), (WH, HL), (WL, HH))):
                        for b in range(2):
                            ins = nc.tensor.matmul(MP[:, slot, b, 0:HALF], w_[:, slot, k, :],
                                                   x_[:, k, b * HALF:(b + 1) * HALF],
                                                   start=(k == 0 and qq == 0), stop=(k == KT - 1 and qq == 2))
                ins.then_inc(mm_done, 1)

            x_ev = [sem("x_evac0"), sem("x_evac1")]
            pe.wait_ge(sem("ident_landed"), 16)
            for j in range(4):
                pe.wait_ge(sem(f"x_landed{j % 2}"), 16 * (j // 2) + 16)
                for c in range(4):
                    q = 4 * j + c
                    if q >= 4:
                        pe.wait_ge(x_ev[q % 2], (q - 4) // 2 + 1)
                    for kk in range(4):
                        ins = nc.tensor.transpose(X[:, q % 4, kk * P:(kk + 1) * P],
                                                  XS[:, j % 2, (4 * c + kk) * P:(4 * c + kk + 1) * P], ident[:])
                    ins.then_inc(sem("x_turned"), 1)
            pe.wait_ge(sem("x_landed0"), 48)
            pe.wait_ge(x_ev[0], 7)
            for k in range(KT):
                ins = nc.tensor.transpose(X[:, 0, k * NS:(k + 1) * NS], XS[0:NS, 0, k * P:(k + 1) * P],
                                          ident[0:NS, 0:NS])
            ins.then_inc(sem("x_turned"), 1)
            pe.wait_ge(sem("raw_landed"), 32)
            for b in range(2):
                pe.wait_ge(x_ev[1 - b], 7 + b)
                for t_ in range(4):
                    ins = nc.tensor.transpose(X[:, 1 + b, t_ * 120:(t_ + 1) * 120],
                                              STR[:, (4 * b + t_) * P:(4 * b + t_ + 1) * P], ident[0:120, 0:120])
                ins.then_inc(sem("x_turned"), 1)
            pe.wait_ge(sem("raw_landed"), 32)
            for b in range(2):
                pe.wait_ge(x_ev[1 - b], 8 + b)
                for t_ in range(4):
                    ins = nc.tensor.transpose(X[:, 3 * (1 - b), t_ * P:(t_ + 1) * P], WSR[:, 4 * b + t_, :], ident[:])
                ins.then_inc(sem("x_turned"), 1)
            pe.wait_ge(sem("setup"), SETUP)
            pe.wait_ge(x_ev[0], 12)
            norm_pe(pe, 0)
            pe.wait_ge(sem("pads"), 3)
            pe.wait_ge(sem("diag_ready"), 1)

            def turn_v(i, e):
                n, (h, slot) = tile_no(N_EVEN_IN, 10, i, 3 * e)
                wait(pe, evac[slot], h + 2)
                if e == 0:
                    wait(pe, sem("tail_copied"), 2 * i + 1)
                else:
                    wait(pe, sem("v_mul"), 2 * i + 1)
                for j in range(5):
                    ins = nc.tensor.transpose(pad5(0)[:, j, :], VT[:, j * P:(j + 1) * P], ident[:])
                ins.then_inc(sem("v_turned"), 1)

            def spatial(i, e):
                wait(pe, sem("v_ready"), 2 * i + e + 1)
                if e == 0:
                    wait(pe, sem("y_used"), 2 * i + 1)
                else:
                    wait(pe, sem("s_used"), 2 * i + 1)
                wst = WST[:, bass.ds(2 * i + e, 1), :].rearrange("p a t -> p (a t)")
                dg = DG[:, bass.ds(2 * i + e, 1), :].rearrange("p a t -> p (a t)")
                for j in range(TT):
                    nc.tensor.matmul(X[:, 2, j * P:(j + 1) * P], VN[:, j, :], wst, start=True, stop=True)
                nc.tensor.matmul(X[:, 3, 0:NS], VN[:, 4, :], dg, start=True, stop=True).then_inc(sem("s_ready"), 1)

            def turn_tail(i, e):
                n, (h, slot) = tile_no(N_EVEN_IN, 10, i, 6 + e)
                wait(pe, evac[slot], h + 2)
                if e == 0:
                    wait(pe, sem("v_mul"), 2 * i + 2)
                else:
                    wait(pe, sem("tail_copied"), 2 * i + 2)
                nc.tensor.transpose(X[0:PAD, 0, 0:P], EX[e][:, SEQ:SEQ + PAD], ident[:])
                nc.tensor.transpose(X[0:NS, 1, 0:P], EX[e][:, PAD + SEQ + 15::16], ident[:]).then_inc(
                    sem("tail_turned"), 1)

            def pool_y(i, e):
                wait(pe, sem("pool_d"), 2 * i + 4)
                wait(pe, sem("group_ready"), 3 * i + 3)
                if e == 0:
                    wait(pe, sem("s_used"), 2 * i + 2)
                else:
                    wait(pe, sem("y_used"), 2 * i + 2)
                for b in range(2):
                    for c in range(2):
                        ins = nc.tensor.matmul(X[:, 2 + b, 0:HALF], WPG[:, c, e * P:(e + 1) * P],
                                               PD[:, c, b * HALF:(b + 1) * HALF], start=(c == 0), stop=(c == 1))
                ins.then_inc(sem("y_ready"), 1)

            with pe.Fori(0, PG) as i:
                for c, (kind, e) in enumerate(EV):
                    n, half = tile_no(N_EVEN_IN, 10, i, c)
                    if c == 0:
                        main_split(pe, n, half, 0)
                    else:
                        main(pe, n, half)
                    if kind == "u":
                        turn_v(i, e)
                    if kind == "za":
                        spatial(i, e)
                    if c == 7:
                        turn_tail(i, 0)
                    if c == 8:
                        turn_tail(i, 1)
                        pool_y(i, 0)
                    if c == 9:
                        pool_y(i, 1)
            with pe.Fori(0, 8) as i:
                for c in range(2):
                    n, half = tile_no(N_EVEN_OUT, 2, i, c)
                    if c == 0:
                        main_split(pe, n, half, 1)
                    else:
                        main(pe, n, half)

            pe.wait_ge(sem("y_used"), 9)
            norm_pe(pe, 1)
            pe.sem_inc(sem("head_turned"), 2)
            pe.wait_ge(sem("tail_copied"), 9)
            pe.wait_ge(sem("head_pads"), 4)

            def turn_head(i, m, n, h, slot):
                wait(pe, evac[slot], h + 2)
                wait(pe, sem("rows_read"), m + 1)
                for j in range(5):
                    ins = nc.tensor.transpose(pad5(0)[:, j, :], KTT[:, slot, j * P:(j + 1) * P], ident[:])
                ins.then_inc(sem("head_turned"), 1)

            def turn_back(kq, slot, tiles):
                wait(pe, sem("rows_ready"), kq + 1)
                wait(pe, sem("back_used"), kq + 1)
                for j in range(tiles):
                    ins = nc.tensor.transpose(pad5(2)[:, j, :], KN[:, slot, j, :], ident[:])
                ins.then_inc(sem("back_turned"), 1)

            with pe.Fori(0, KV) as i:
                for c, (kind, col0, br) in enumerate(KVT):
                    n, half = tile_no(N_KV, 6, i, c)
                    if c == 0:
                        main_split(pe, n, half, 2)
                    else:
                        main(pe, n, half)
                    for t_ in ([c - 1, 5] if c == 5 else [c - 1] if c else []):
                        m_n, (mh, ms) = tile_no(N_KV, 6, i, t_)
                        turn_head(i, 6 * i + t_, m_n, mh, ms)
                        if t_ == 4:
                            wait(pe, sem("vc_rows"), i + 1)
                            wait(pe, sem("vm_used"), i + 1)
                            for j in range(TT):
                                ins = nc.tensor.matmul(X[:, 3, 0:P], VMASK[:, j, :], KN[:, 1, j, :],
                                                       start=(j == 0), stop=(j == TT - 1))
                            ins.then_inc(sem("vm_done"), 1)
                    if 2 <= c <= 4:
                        turn_back(3 * i + c - 2, (c - 2) % 2, TT)
            with pe.Fori(0, KV) as i:
                for c in range(8):
                    n, half = tile_no(N_QZ, 8, i, c)
                    main(pe, n, half)
                    if 1 <= c <= 4:
                        m_n, (mh, ms) = tile_no(N_QZ, 8, i, c - 1)
                        turn_head(i, 24 + 4 * i + c - 1, m_n, mh, ms)
                    if 2 <= c <= 5:
                        turn_back(12 + 4 * i + c - 2, (c - 2) % 2, 5)
            main(pe, N_GATE, (N_GATE // 2, 0))
            pe.wait_ge(evac[0], N_GATE // 2 + 2)
            pe.wait_ge(sem("rows_read"), 41)
            for j in range(TT):
                nc.tensor.transpose(X[:, 0, j * P:(j + 1) * P], GTT[:, j * P:(j + 1) * P], ident[:])
            nc.tensor.transpose(X[0:NS, 1, 0:P], GTT[:, SEQ:T], ident[:]).then_inc(sem("gates_turned"), 1)
            pe.wait_ge(sem("gate8_ready"), 3)
            for b in range(3):
                ins = nc.tensor.transpose(X[:, 1, P + b * NS:P + (b + 1) * NS], G8[:, b, :], ident[0:NS, 0:NS])
            ins.then_inc(sem("gates_turned"), 1)

            pe.wait_ge(sem("cmp_consts"), 64)
            pe.wait_ge(sem("gates_copied"), 2)
            pe.wait_ge(sem("back_used"), 29)
            pe.sem_inc(sem("pages_used"), 2)
            with pe.Fori(0, 2) as r:
                for hf in range(2):
                    wait(pe, sem("means_used_a"), r + 1) if hf == 0 else wait(pe, sem("means_used_b"), r + 1)
                    for c in range(8):
                        wait(pe, sem(f"pages_landed{c % 2}"), 512 * r + 256 * hf + 64 * (c // 2) + 64)
                        for kv in range(2):
                            for s4 in range(4):
                                ins = nc.tensor.matmul(X[32 * s4:32 * s4 + 32, 2 * hf + kv, :], BM[:, c, :],
                                                       PGT[:, c % 2, s4, kv * 512:(kv + 1) * 512],
                                                       start=(c == 0), stop=(c == 7))
                        ins.then_inc(sem("pages_used"), 1)
            pe.wait_ge(sem("means_used_a"), 3)
            pe.wait_ge(sem("means_used_b"), 3)
            for it in range(4):
                for g in range(KV):
                    ins = nc.tensor.transpose(X[:, it, g * P:(g + 1) * P], KMS[:, it, g * P:(g + 1) * P], ident[:])
                ins.then_inc(sem("km_turned"), 1)
            pe.wait_ge(sem("kmt_ready"), 4)
            pe.wait_ge(sem("qp_ready"), 1)
            for s_ in range(NS):
                for g in range(KV):
                    ins = nc.tensor.matmul(X[32 * g:32 * g + 32, 0, s_ * 32:(s_ + 1) * 32], QP[:, s_, g, :],
                                           KMT[:, g, s_, :], start=True, stop=True)
            ins.then_inc(sem("cs_done"), 1)
            pe.wait_ge(sem("cp_ready"), 1)
            for s_ in range(NS):
                ins = nc.tensor.matmul(X[0:32, 1, 0:32], GROWS[:, s_, :], CE[:, s_, :], start=(s_ == 0),
                                       stop=(s_ == NS - 1))
            ins.then_inc(sem("imp_done"), 1)
            pe.wait_ge(sem("cpad_ready"), 5)
            for it in range(4):
                ins = nc.tensor.transpose(X[:, 2, it * P:(it + 1) * P], CP[:, it].rearrange("p s n -> p (s n)"),
                                          ident[:])
            ins.then_inc(sem("cpt_turned"), 1)
            pe.wait_ge(sem("cpt_ready"), 1)
            pe.wait_ge(sem("imp_copied"), 1)
            for s4 in range(4):
                for r in range(2):
                    for g in range(KV):
                        for hf in range(2):
                            ins = nc.tensor.matmul(
                                X[32 * g:32 * g + 32, s4, r * P:(r + 1) * P],
                                CPT[32 * s4:32 * s4 + 32, 2 * r + hf, 32 * g:32 * g + 32],
                                KMS[32 * s4:32 * s4 + 32, 2 * r + hf, 512 + g * P:512 + (g + 1) * P],
                                start=(hf == 0), stop=(hf == 1))
            ins.then_inc(sem("oc_done"), 1)
            pe.wait_ge(sem("low_ready"), 1)
            pe.wait_ge(sem("oc_ready"), 4)
            for s_ in range(NS):
                ins = nc.tensor.matmul(X[:, 0, s_ * 32:(s_ + 1) * 32], GSPR[0:32, s_, :], LOW[:], start=True,
                                       stop=True)
            ins.then_inc(sem("low_spread"), 1)

            pe.wait_ge(sem("bias_ready"), 1)
            pe.sem_inc(sem("k_turned"), 1)
            pe.sem_inc(sem("sc_done"), 1)
            pe.sem_inc(sem("pv_done"), 1)
            pe.sem_inc(sem("new_scored"), 1)
            new = MP[:, 0, 1, :]

            def sample_scores(i):
                def turn_k(t_):
                    if t_ >= 4:
                        j = t_ - 4
                        wait(pe, sem(f"sk_landed{j % 8}"), 32 * i + 16 * (j // 8) + 16)
                    wait(pe, sem("k_evac"), 20 * i + t_ + 1)
                    src = KWK[:, t_] if t_ < 4 else SK[:, (t_ - 4) % 8]
                    for g in range(KV):
                        ins = nc.tensor.transpose(X[:, t_ % 2, g * P:(g + 1) * P], src[:, g * P:(g + 1) * P],
                                                  ident[:])
                    ins.then_inc(sem("k_turned"), 1)

                def score_block(b):
                    wait(pe, sem("k_evac"), 20 * i + 4 * b + 6)
                    if b == 2:
                        wait(pe, sem("win_exp"), i + 1)
                    else:
                        wait(pe, sem("sel_read"), 4 * i + 4 if b < 2 else 4 * i + 2 + b)
                    for g in range(KV):
                        ins = nc.tensor.matmul(X[32 * g:32 * g + 32, 2 + b % 2, :], QS[:, g, :],
                                               SKT[:, b % 2, g, :], start=True, stop=True)
                    ins.then_inc(sem("sc_done"), 1)

                wait(pe, sem("win_landed"), 64 * i + 64)
                wait(pe, sem("q_static"), i + 1)
                for t_ in range(20):
                    turn_k(t_)
                    if t_ == 3:
                        if not isinstance(i, int):
                            wait(pe, sem("os_done"), i)
                        for g in range(KV):
                            ins = nc.tensor.transpose(new[:, g:g + 1], NRK[0:1, g * P:(g + 1) * P], ident[0:1, 0:1])
                        ins.then_inc(sem("new_turned"), 1)
                    if t_ == 5:
                        wait(pe, sem("new_evac"), i + 1)
                        for g in range(KV):
                            ins = nc.tensor.matmul(MP[32 * g:32 * g + 32, 0, 1, 8:9], QS[:, g, :], KNT[:, g:g + 1],
                                                   start=True, stop=True)
                        ins.then_inc(sem("new_scored"), 1)
                    if t_ % 4 == 1 and t_ > 4:
                        score_block(t_ // 4 - 1)
                score_block(4)

            def sample_values(i):
                wait(pe, sem("vals_landed"), 320 * i)
                wait(pe, sem("p_evac"), 6 * i)
                wait(pe, sem("o_rows"), i)
                for j in range(PAGES):
                    for g in range(KV):
                        nc.tensor.matmul(MP[32 * g:32 * g + 32, 0, 0, 0:P], SPT[:, j, 32 * g:32 * g + 32],
                                         SV[:, j, g * P:(g + 1) * P], start=(j == 0), stop=False)
                for g in range(KV):
                    nc.tensor.matmul(MP[32 * g:32 * g + 32, 0, 0, 0:P], SPT[0:1, PAGES, 32 * g:32 * g + 32],
                                     NRV[0:1, g * P:(g + 1) * P], start=False, stop=True)
                for t_ in range(4):
                    for g in range(KV):
                        ins = nc.tensor.matmul(MP[32 * g:32 * g + 32, 0, 0, P:2 * P],
                                               WPT[:, t_, 32 * g:32 * g + 32], KWV[:, t_, g * P:(g + 1) * P],
                                               start=(t_ == 0), stop=(t_ == 3))
                ins.then_inc(sem("pv_done"), 1)

            def sample_probs(i):
                wait(pe, sem("win_exp"), i + 1)
                for t_ in range(4):
                    ins = nc.tensor.transpose(MP[:, 1, 0, t_ * P:(t_ + 1) * P], SWP[:, t_ * P:(t_ + 1) * P], ident[:])
                ins.then_inc(sem("p_turned"), 1)
                wait(pe, sem("sel_exp"), i + 1)
                for q in range(1, 5):
                    if q >= 2:
                        wait(pe, sem("p_evac"), 6 * i + q - 1)
                    for t_ in range(4):
                        ins = nc.tensor.transpose(MP[:, 1, q % 2, t_ * P:(t_ + 1) * P],
                                                  SC[:, (4 * q - 4 + t_) * P:(4 * q - 3 + t_) * P], ident[:])
                    ins.then_inc(sem("p_turned"), 1)
                nc.tensor.transpose(MP[0:1, 0, 1, P:2 * P], SC[:, PAGES * P:PAGES * P + 1], ident[:]).then_inc(
                    sem("p_turned"), 1)

            def sample_out(i):
                wait(pe, sem("o_rows"), i + 1)
                wait(pe, sem("p_evac"), 6 * i + (0 if isinstance(i, int) else 6))
                nc.tensor.transpose(new[:, 2 * P:3 * P], OSM[:, 1, :], ident[:]).then_inc(sem("o_turned"), 1)

            sample_scores(0)
            sample_probs(0)
            with pe.Fori(1, NS) as i:
                sample_scores(i)
                sample_values(i)
                sample_probs(i)
                sample_out(i)
            sample_values(NS)
            sample_out(NS)

            pe.wait_ge(sem("os_done"), NS + 1)
            pe.wait_ge(sem("attn_ready"), 2)
            pe.sem_inc(sem("p4_turned"), 4)
            pe.sem_inc(sem("pv4"), 2)

            def unit(w):
                return w // 8, (w // 4) % 2, w % 4

            with pe.Fori(0, KV) as i:
                def score(w):
                    e, br, j = unit(w)
                    wait(pe, sem("p4_exp"), 32 * i + w + 1)
                    nc.tensor.matmul(X[:, w % 4, 0:(j + 1) * P], QC[:, e, j * P:(j + 1) * P],
                                     KTS[:, br, bass.ds(i, 1), 0:(j + 1) * P].rearrange("p a t -> p (a t)"),
                                     start=True, stop=False)
                    nc.tensor.matmul(X[:, w % 4, j * P:(j + 1) * P], IDB[:], CAB[:], start=False,
                                     stop=True).then_inc(sem("s4_done"), 1)

                wait(pe, sem("group_static"), i + 1)
                wait(pe, sem("qc_ready"), i + 1)
                wait(pe, sem("p4_exp"), 32 * i + 4)
                for e in range(REP):
                    ins = nc.tensor.matmul(X[32 * e:32 * e + 32, 0, :], KMG[:], QC[:, e, :], start=True, stop=True)
                ins.then_inc(sem("c4_scored"), 1)
                wait(pe, sem("c4_rows"), i + 1)
                for j in range(TT):
                    ins = nc.tensor.transpose(X[:, 1, j * P:(j + 1) * P], CS[:, j * P:(j + 1) * P], ident[:])
                ins.then_inc(sem("c4_turned"), 1)
                wait(pe, sem("c4_probs"), i + 1)
                for j in range(TT):
                    ins = nc.tensor.transpose(X[:, 0, j * P:(j + 1) * P], CPP[:, j].rearrange("p e n -> p (e n)"),
                                              ident[:])
                ins.then_inc(sem("c4_back"), 1)
                wait(pe, sem("c4_probs_t"), i + 1)
                for w in range(3):
                    score(w)

                def values(w):
                    e, br, j = unit(w)
                    o_ = MP[:, 1, e % 2, :]
                    if br == 0:
                        wait(pe, sem("o_used"), 4 * i + e + 1)
                        nc.tensor.matmul(o_, VMG[32 * e:32 * e + 32, :], CPX[32 * e:32 * e + 32, :], start=True,
                                         stop=False)
                    wait(pe, sem("pt4_evac"), 32 * i + w + 3)
                    for m in range(TT):
                        ins = nc.tensor.matmul(o_[:, m * P:SEQ], VB[:, br, m, :], PT_[:, br, m, m * P:SEQ],
                                               start=False, stop=(br == 1 and m == 3))
                    ins.then_inc(sem("pv4"), 1)

                for w in range(32):
                    e, br, j = unit(w)
                    if w + 3 < 32:
                        score(w + 3)
                    wait(pe, sem("p4_scaled"), 32 * i + w + 9)
                    wait(pe, sem("pt4_evac"), 32 * i + w + 1)
                    for m in range(j + 1):
                        ins = nc.tensor.transpose(MP[:, 0, w % 2, m * P:(m + 1) * P],
                                                  PR[:, w % 4, m * P:(m + 1) * P], ident[:])
                    ins.then_inc(sem("p4_turned"), 1)
                    if w % 4 == 1 and w > 4:
                        values(w - 2)
                values(31)

            pe.wait_ge(sem("o_used"), HEADS + 2)
            pe.wait_ge(sem("c4_probs_t"), KV)

            def turn_y(k, slot, n, h):
                bank = 2 * (1 - slot)
                wait(pe, evac[slot], h + 2)
                wait(pe, sem("y_read"), k + 1)
                for j in range(TT):
                    nc.tensor.transpose(pad5(bank)[:, j, :], YT[:, slot, j * P:(j + 1) * P], ident[:])
                nc.tensor.transpose(X[0:NS, bank + 1, 0:P], YT[:, slot, SEQ:T], ident[:]).then_inc(sem("y_turned"), 1)

            pe.sem_inc(sem("y_turned"), 2)

            def out_pass(i, first):
                for c in range(2):
                    n, half = tile_no(N_ODD_OUT, 2, i, c)
                    if first and c == 0:
                        main_split(pe, n, half, 3)
                    else:
                        main(pe, n, half)
                    if not (first and c == 0):
                        pn, (ph, ps_) = tile_no(N_ODD_OUT - 1, 2, i, c)
                        turn_y(2 * i + c - 1, ps_, pn, ph)

            out_pass(0, True)
            with pe.Fori(1, 8) as i:
                out_pass(i, False)
            turn_y(15, (N_ODD_OUT + 15) % 2, N_ODD_OUT + 15, (N_ODD_OUT + 15) // 2)

        @block.scalar
        def _(act):
            act.sem_inc(sem("tail_copied"), 1)
            for q in range(1, 16, 2):
                act.wait_ge(sem("x_turned"), q + 1)
                j, c = q // 4, q % 4
                nc.scalar.copy(A[:, 4 * c:4 * c + 4, j * P:(j + 1) * P],
                               X[:, q % 4, :].rearrange("p (k t) -> p k t", k=4)).then_inc(sem("x_evac1"), 1)
            act.wait_ge(sem("x_turned"), 18)
            nc.scalar.copy(STP[:, 0:4, :], X[:, 1, 0:480].rearrange("p (k t) -> p k t", k=4)).then_inc(
                sem("x_evac1"), 1)
            act.wait_ge(sem("x_evac0"), 9)
            act.wait_ge(sem("x_evac1"), 9)
            act.wait_ge(sem("setup"), SETUP)
            act.wait_ge(sem("setup_set"), 2)
            norm_act(act, 0)
            split_hi(act, 0, (0, 0))

            def evac_p(i, e, slot):
                wait(act, sem("pool_d"), 2 * i + e + 1)
                wait(act, sem("tail_turned"), 2 * i + e + 1)
                nc.scalar.copy(EX[e][:, PAD:PAD + HALF], MP[:, slot, 0, 0:HALF])
                nc.scalar.copy(EX[e][:, PAD + HALF:PAD + SEQ], MP[:, slot, 1, 0:SEQ - HALF])
                nc.scalar.copy(EX[e][:, PAD + SEQ + 15::16], MP[:, slot, 1, SEQ - HALF:HALF]).then_inc(evac[slot], 1)

            def square_v(i, e):
                wait(act, sem("v_turned"), 2 * i + e + 2)
                wait(act, sem("v_ss"), 2 * i + e + 1)
                wait(act, sem("pool_d"), 2 * i + 2)
                nc.scalar.activation(C1[:, 0:TP].rearrange("p (j d) -> p j d", d=P), pad5(0),
                                     ACT.Square).then_inc(sem("v_sq"), 1)

            def copy_tail(i, e):
                wait(act, sem("tail_turned"), 2 * i + e + 3)
                wait(act, sem("tail_out"), 32 * (2 * i + e) + 32)
                nc.scalar.copy(TLP[:], X[0:PAD, 0, 0:P]).then_inc(sem("tail_first"), 1)
                nc.scalar.copy(TLS[:], X[0:NS, 1, 0:P]).then_inc(sem("tail_copied"), 1)

            with act.Fori(0, PG) as i:
                for c, (kind, e) in enumerate(EV):
                    n, half = tile_no(N_EVEN_IN, 10, i, c)
                    nn, nhalf = tile_no(N_EVEN_IN, 10, i, c + 1)
                    slot = half[1]
                    split_hi(act, nn, nhalf)
                    wait(act, mm_done, n + 3)
                    if kind == "v":
                        wait(act, sem("v_turned"), 2 * i + e + 1)
                        nc.scalar.copy(two(VT[:, 0:T]), mp(slot)).then_inc(evac[slot], 1)
                    elif kind == "u":
                        wait(act, sem("u_used"), 2 * i + e + 1)
                        nc.scalar.copy(two(UT[:]), mp(slot)).then_inc(evac[slot], 1)
                        square_v(i, e)
                    elif kind in ("za", "zb"):
                        wait(act, sem("z_used"), 4 * i + (0 if kind == "za" else 2) + e + 1)
                        nc.scalar.activation(two(SZ[:]), mp(slot), ACT.Silu).then_inc(evac[slot], 1)
                    else:
                        evac_p(i, e, slot)
                    if c == 7:
                        copy_tail(i, 0)
                    if c == 8:
                        copy_tail(i, 1)
            act.wait_ge(sem("z_used"), 17)
            act.wait_ge(mm_done, N_EVEN_OUT + 2)
            split_act_act(act, 1)
            with act.Fori(0, 8) as i:
                for c in range(2):
                    n, half = tile_no(N_EVEN_OUT, 2, i, c + 1)
                    split_hi(act, n, half)

            act.wait_ge(evac[0], 29)
            act.wait_ge(evac[1], 29)
            norm_act(act, 1)
            for b in range(2):
                act.sem_inc(sem(f"z_out{b}"), 16)
            act.sem_inc(sem("back_used"), 1)
            act.wait_ge(sem("head_pads"), 4)

            def square_head(m, kq):
                wait(act, sem("head_turned"), m + 3)
                wait(act, sem("h_ss"), kq + 1)
                nc.scalar.activation(SQ1[:], pad5(0), ACT.Square).then_inc(sem("h_sq"), 1)

            with act.Fori(0, KV) as i:
                for c, (kind, col0, br) in enumerate(KVT):
                    n, (h, slot) = tile_no(N_KV, 6, i, c)
                    nn, nhalf = tile_no(N_KV, 6, i, c + 1)
                    split_hi(act, nn, nhalf)
                    wait(act, mm_done, n + 3)
                    wait(act, sem("head_turned"), 6 * i + c + 1)
                    nc.scalar.copy(two(KTT[:, slot, 0:T]), mp(slot)).then_inc(evac[slot], 1)
                    if 1 <= c <= 3:
                        square_head(6 * i + c - 1, 3 * i + c - 1)
                    if c in (3, 4):
                        wait(act, sem("back_turned"), 3 * i + c - 1)
                        nc.scalar.copy(KTS[:, c - 3, bass.ds(i, 1), :].rearrange("p a t -> p (a t)"),
                                       X[:, 2, :]).then_inc(sem("back_used"), 1)
            act.wait_ge(sem("x1_out"), 256)
            with act.Fori(0, KV) as i:
                for c in range(8):
                    n, (h, slot) = tile_no(N_QZ, 8, i, c)
                    nn, nhalf = tile_no(N_QZ, 8, i, c + 1)
                    split_hi(act, nn, nhalf)
                    wait(act, mm_done, n + 3)
                    if c < 4:
                        wait(act, sem("head_turned"), 24 + 4 * i + c + 1)
                        nc.scalar.copy(two(KTT[:, slot, 0:T]), mp(slot)).then_inc(evac[slot], 1)
                    else:
                        wait(act, sem(f"z_out{slot}"), 32 * i + 16 * (c // 2 - 2) + 16)
                        nc.scalar.activation(two(ZT[:, slot]), mp(slot), ACT.Silu).then_inc(evac[slot], 1)
                    if 1 <= c <= 4:
                        square_head(24 + 4 * i + c - 1, 12 + 4 * i + c - 1)
                    if 2 <= c <= 5:
                        kq = 12 + 4 * i + c - 2
                        wait(act, sem("back_turned"), kq + 1)
                        nc.scalar.copy(act_tile(4 * i + c - 2), X[:, 2:4, :].rearrange("p b n -> p (b n)")[:, 0:T]
                                       ).then_inc(sem("back_used"), 1)
                    if c >= 4:
                        head = nc.scalar.snap(4 * i + c - 4, min_val=0, max_val=HEADS - 1)
                        wait(act, evac[slot], h + 2)
                        nc.scalar.dma_start(szT_scr[bass.ds(head, 1)].rearrange("a p t -> p (a t)"), ZT[:, slot]
                                            ).then_inc(sem(f"z_out{slot}"), 16)
            act.wait_ge(mm_done, N_GATE + 3)
            nc.scalar.activation(two(GTT[:]), mp(0), ACT.Sigmoid).then_inc(evac[0], 1)
            act.wait_ge(sem("gates_turned"), 1)
            nc.scalar.copy(GT[:].rearrange("p j n -> p (j n)"), X[:, 0, :]).then_inc(sem("gates_copied"), 1)

            act.sem_inc(sem("means_used_a"), 1)
            act.sem_inc(sem("means_used_b"), 1)
            with act.Fori(0, 2) as r:
                for hf in range(2):
                    wait(act, sem("pages_used"), 16 * r + 8 * hf + 8 + 2)
                    it = bass.ds(2 * r + hf, 1)
                    nc.scalar.copy(KMS[:, it, 0:512].rearrange("p a n -> p (a n)"), X[:, 2 * hf, :]).then_inc(
                        sem("k_means"), 1)
                    wait(act, sem("k_means"), 2 * r + hf + 1)
                    wait(act, sem("v_means"), 2 * r + hf + 1)
                    act.sem_inc(sem("means_used_a" if hf == 0 else "means_used_b"), 1)
            for it in range(4):
                r, hf = it // 2, it % 2
                act.wait_ge(sem("km_turned"), it + 1)
                nc.scalar.copy(KMT[:, :, 4 * r:4 * r + 4, 16 * hf:16 * hf + 16],
                               X[:, it, :].rearrange("p (g s n) -> p g s n", g=KV, s=4)[:, :, :, 0:16]).then_inc(
                    sem("kmt_ready"), 1)
            act.wait_ge(sem("cs_shifted"), 1)
            nc.scalar.activation(CE[:], CE[:], ACT.Exp).then_inc(sem("cs_exp"), 1)

            act.wait_ge(sem("bias_ready"), 1)
            act.sem_inc(sem("k_evac"), 2)

            def sample_act(i, first):
                for t_ in range(20):
                    b = t_ // 4
                    if t_ % 4 == 0:
                        wait(act, sem("sc_done"), 5 * i + 1 if b < 2 else 5 * i + b)
                    wait(act, sem("k_turned"), 20 * i + t_ + 2)
                    nc.scalar.copy(SKT[:, b % 2, :, (t_ % 4) * P:(t_ % 4 + 1) * P],
                                   X[:, t_ % 2, :].rearrange("p (g t) -> p g t", g=KV)).then_inc(sem("k_evac"), 1)
                    if t_ == 3:
                        wait(act, sem("new_scored"), i + 1)
                        wait(act, sem("new_turned"), i + 1)
                        nc.scalar.copy(KNT[:], MP[:, 0, 1, 0:KV]).then_inc(sem("new_evac"), 1)
                    if t_ == 9:
                        if not first:
                            wait(act, sem("p_turned"), 6 * i)
                        wait(act, sem("win_max"), i + 1)
                        nc.scalar.activation(SWP[:], X[:, 2, :], ACT.Exp, bias=SST[:, 0:1],
                                             accum_out=SST[:, 1:2]).then_inc(sem("win_exp"), 1)
                wait(act, sem("sel_max"), i + 1)
                nc.scalar.activation(SC[:], SC[:], ACT.Exp, bias=SST[:, 2:3], accum_out=SST[:, 3:4]).then_inc(
                    sem("sel_exp"), 1)

            sample_act(0, True)
            with act.Fori(1, NS) as i:
                sample_act(i, False)

            act.wait_ge(sem("os_done"), NS + 1)
            act.sem_inc(sem("p4_exp"), 4)
            act.sem_inc(sem("pt4_evac"), 2)
            with act.Fori(0, KV) as i:
                def exp4(w):
                    j = w % 4
                    wait(act, sem("max4"), 32 * i + w + 1)
                    wait(act, sem("p4_turned"), 32 * i + w + 1)
                    wait(act, sem("p4_scaled"), 32 * i + w + 1)
                    nc.scalar.activation(PR[:, w % 4, 0:(j + 1) * P], X[:, w % 4, 0:(j + 1) * P], ACT.Exp,
                                         bias=AMX[:, w % 8:w % 8 + 1], accum_out=ASM[:, w % 8:w % 8 + 1]).then_inc(
                        sem("p4_exp"), 1)

                wait(act, sem("c4_shifted"), i + 1)
                nc.scalar.activation(CX[:], CX[:], ACT.Exp).then_inc(sem("c4_exp"), 1)
                exp4(0)
                exp4(1)
                for w in range(32):
                    e, br, j = w // 8, (w // 4) % 2, w % 4
                    if w + 2 < 32:
                        exp4(w + 2)
                    wait(act, sem("p4_turned"), 32 * i + w + 5)
                    if j == 0:
                        wait(act, sem("pv4"), 8 * i + 2 * e + br + 1)
                    nc.scalar.copy(PT_[:, br, 0:j + 1, j * P:(j + 1) * P],
                                   MP[:, 0, w % 2, 0:(j + 1) * P].rearrange("p (m t) -> p m t", t=P)).then_inc(
                        sem("pt4_evac"), 1)

            act.wait_ge(sem("o_used"), HEADS + 2)
            for b in range(2):
                act.sem_inc(sem(f"y_out{b}"), 32)
            split_hi(act, N_ODD_OUT, (N_ODD_OUT // 2, N_ODD_OUT % 2))
            split_act_act(act, 3)
            act.sem_inc(sem("y_read"), 1)
            act.sem_inc(sem("y_read"), 1)
            y_p = O["y_prompt"].rearrange("(j p) c -> p j c", p=P)

            def rows_y(k, slot, uses):
                bank = 2 * (1 - slot)
                wait(act, sem("y_turned"), k + 3)
                wait(act, sem(f"y_out{slot}"), 32 * uses + 32)
                nc.scalar.copy(YS[:, slot, 0:TT, :], pad5(bank)[:, 0:TT, :]).then_inc(sem("y_rows"), 1)
                nc.scalar.copy(YS[0:NS, slot, 4, :], X[0:NS, bank + 1, 0:P]).then_inc(sem("y_read"), 1)
                col = k * P if isinstance(k, int) else nc.scalar.snap(k * P, min_val=0, max_val=D - P)
                wait(act, sem("y_rows"), k + 1)
                wait(act, sem("y_read"), k + 3)
                cols = bass.ds(col, P)
                nc.scalar.dma_start(y_p[:, :, cols], YS[:, slot, 0:TT, :]).then_inc(sem(f"y_out{slot}"), 16)
                nc.scalar.dma_start(O["y_sample"][:, cols], YS[0:NS, slot, 4, :]).then_inc(sem(f"y_out{slot}"), 16)

            def out_act(i, first, last):
                for c in range(2):
                    nn, nhalf = tile_no(N_ODD_OUT, 2, i, c + 1)
                    if not (last and c == 1):
                        split_hi(act, nn, nhalf)
                    if not (first and c == 0):
                        rows_y(2 * i + c - 1, (N_ODD_OUT + c - 1) % 2, i - 1 if c == 0 else i)

            out_act(0, True, False)
            with act.Fori(1, 7) as i:
                out_act(i, False, False)
            out_act(7, False, True)
            rows_y(15, (N_ODD_OUT + 15) % 2, 7)

        @block.vector
        def _(dve):
            dve.sem_inc(w_split, 2)
            dve.sem_inc(evac[0], 1)
            dve.sem_inc(evac[1], 1)
            for name, k in (("v_ss", 1), ("s_used", 0), ("u_used", 1), ("z_used", 1), ("y_used", 1), ("pool_d", 2),
                            ("v_mul", 0)):
                if k:
                    dve.sem_inc(sem(name), k)
            seq = Seq(dve, "dve_step")
            for q in range(0, 16, 2):
                dve.wait_ge(sem("x_turned"), q + 1)
                j, c = q // 4, q % 4
                nc.vector.tensor_copy(A[:, 4 * c:4 * c + 4, j * P:(j + 1) * P],
                                      X[:, q % 4, :].rearrange("p (k t) -> p k t", k=4)).then_inc(sem("x_evac0"), 1)
            dve.wait_ge(sem("x_turned"), 17)
            nc.vector.tensor_copy(A[:, :, SEQ:T], X[:, 0, 0:KT * NS].rearrange("p (k t) -> p k t", k=KT)).then_inc(
                sem("x_evac0"), 1)
            dve.wait_ge(sem("x_turned"), 19)
            nc.vector.tensor_copy(STP[:, 4:8, :], X[:, 2, 0:480].rearrange("p (k t) -> p k t", k=4)).then_inc(
                sem("x_evac0"), 1)
            dve.wait_ge(sem("setup"), SETUP)
            for b in range(2):
                dve.wait_ge(sem("x_turned"), 20 + b)
                nc.vector.tensor_tensor(WST[:, 4 * b:4 * b + 4, :],
                                        X[:, 3 * (1 - b), :].rearrange("p (k t) -> p k t", k=4),
                                        TRIL[:].unsqueeze(1).to_broadcast([P, 4, P]), ALU.mult).then_inc(
                    sem("x_evac0"), 1)
            nc.vector.tensor_tensor(DG[:], DI8[:].unsqueeze(1).to_broadcast([P, AH, NS]), over(W00[:], NS),
                                    ALU.mult).then_inc(sem("diag_ready"), 1)
            norm_dve(dve, 0, g_even, 0)
            split_lo(dve, 0, (0, 0))

            def norm_v(i, e):
                wait(dve, sem("v_sq"), 2 * i + e + 1)
                nc.vector.tensor_reduce(SS[:], C1[:, 0:TP].rearrange("p (j d) -> p j d", d=P), AX.X,
                                        ALU.add).then_inc(sem("v_ss"), 1)
                wait(dve, sem("v_rstd"), 2 * i + e + 1)
                wait(dve, sem("s_ready"), 2 * i + e + 1)
                wait(dve, sem("gv_out"), 16 * (2 * i + e) + 16)
                nc.vector.tensor_tensor(VN[:], pad5(0), over(SR[:], P), ALU.mult).then_inc(sem("v_mul"), 1)

            def add_bias(i, e):
                wait(dve, sem("s_ready"), 2 * i + e + 2)
                bs = BS[:, bass.ds((2 * i + e) * P, P)]
                dst = A[:, bass.ds(2 * i + e, 1), :]
                seq.do(nc.vector.tensor_tensor(dst[:, :, 0:SEQ].rearrange("p a (j t) -> p (a j) t", j=TT),
                                               X[:, 2, :].rearrange("p (j t) -> p j t", j=TT),
                                               bs.unsqueeze(1).to_broadcast([P, TT, P]), ALU.add))
                nc.vector.tensor_tensor(dst[:, :, SEQ:T].rearrange("p a t -> p (a t)"), X[:, 3, 0:NS],
                                        BS[:, bass.ds((2 * i + e) * P, 1)].to_broadcast([P, NS]),
                                        ALU.add).then_inc(sem("s_used"), 1)
                wait(dve, sem("s_used"), 2 * i + e + 1)

            def gate_a(i, e):
                n, (h, slot) = tile_no(N_EVEN_IN, 10, i, 3 * e + 2)
                wait(dve, evac[slot], h + 2)
                nc.vector.tensor_tensor(UT[:], UT[:], SZ[:], ALU.mult).then_inc(sem("z_used"), 1)
                wait(dve, sem("z_used"), 4 * i + e + 2)
                a = act_tile(2 * i + e)
                nc.vector.tensor_tensor(a, a, UT[:], ALU.mult).then_inc(sem("u_used"), 1)

            def pool_chain(i, e):
                n, (h, slot) = tile_no(N_EVEN_IN, 10, i, 6 + e)
                wait(dve, evac[slot], h + 2)
                wait(dve, sem("hist_ready"), 2 * i + e + 1)
                wait(dve, sem("group_ready"), 3 * i + 3)
                wait(dve, sem("y_ready"), 2 * i + 1)
                ex = EX[e]
                seq.do(nc.vector.tensor_tensor(C2[:, 1:EXT], ex[:, 1:EXT], ex[:, 0:EXT - 1], ALU.add))
                src, dst = C2, C1
                lo = 1
                for k, s_ in enumerate((2, 4, 8)):
                    a0 = lo + s_
                    seq.do(nc.vector.scalar_tensor_tensor(out=dst[:, a0:EXT], in0=src[:, a0 - s_:EXT - s_],
                                                          scalar=PARG[:, k:k + 1], in1=src[:, a0:EXT],
                                                          op0=ALU.mult, op1=ALU.add))
                    src, dst, lo = dst, src, a0
                s0 = PAD + SEQ + 15
                seq.do(nc.vector.scalar_tensor_tensor(out=PD[:, e, 0:SEQ], in0=src[:, PAD:PAD + SEQ],
                                                      scalar=PARG[:, 3:4], in1=ex[:, PAD:PAD + SEQ],
                                                      op0=ALU.mult, op1=ALU.subtract))
                seq.do(nc.vector.scalar_tensor_tensor(out=PD[:, e, SEQ:T], in0=src[:, s0::16],
                                                      scalar=PARG[:, 3:4], in1=ex[:, s0::16],
                                                      op0=ALU.mult, op1=ALU.subtract))
                seq.do(nc.vector.tensor_tensor(FIX[:], src[:, PAD:2 * PAD], PARG[:, 4:4 + PAD], ALU.mult))
                nc.vector.tensor_tensor(PD[:, e, 0:PAD], FIX[:], ex[:, PAD:2 * PAD],
                                        ALU.subtract).then_inc(sem("pool_d"), 1)

            def gate_m(i, e):
                wait(dve, sem("y_ready"), 2 * i + e + 2)
                n, (h, slot) = tile_no(N_EVEN_IN, 10, i, 8 + e)
                a = A[:, bass.ds(AH + 2 * i + e, 1), :].rearrange("p a (b t) -> p (a b) t", b=2)
                nc.vector.tensor_scalar(a, X[:, 2:4, 0:HALF], PSG[:, e:e + 1], None, ALU.mult).then_inc(
                    sem("y_used"), 1)
                wait(dve, sem("y_used"), 2 * i + e + 2)
                wait(dve, evac[slot], h + 2)
                a = act_tile(AH + 2 * i + e)
                nc.vector.tensor_tensor(a, a, SZ[:], ALU.mult).then_inc(sem("z_used"), 1)

            dve.wait_ge(sem("xT_out"), 16)
            with dve.Fori(0, PG) as i:
                seq.loop(i, 2 + 14, 0)
                for c, (kind, e) in enumerate(EV):
                    nn, nhalf = tile_no(N_EVEN_IN, 10, i, c + 1)
                    split_lo(dve, nn, nhalf)
                    if kind == "u":
                        norm_v(i, e)
                    if kind == "za":
                        add_bias(i, e)
                        gate_a(i, e)
                    if kind == "p":
                        pool_chain(i, e)
                    if kind == "zb":
                        gate_m(i, e)
            assert seq.n == 16, seq.n
            split_act_dve(dve, 1)
            with dve.Fori(0, 8) as i:
                for c in range(2):
                    nn, nhalf = tile_no(N_EVEN_OUT, 2, i, c + 1)
                    n, (h, slot) = tile_no(N_EVEN_OUT, 2, i, c)
                    split_lo(dve, nn, nhalf)
                    wait(dve, mm_done, n + 3)
                    wait(dve, sem(f"res_landed{c}"), 16 * i + 16)
                    a = A[:, bass.ds(2 * i + c, 1), :].rearrange("p a (b t) -> p (a b) t", b=2)
                    nc.vector.tensor_tensor(a, mp(slot), two(XR[:, slot]), ALU.add).then_inc(evac[slot], 1)

            norm_dve(dve, 1, g_odd, 2)
            dve.sem_inc(sem("rows_read"), 1)
            dve.sem_inc(sem("h_ss"), 1)
            dve.sem_inc(sem("vm_used"), 1)
            dve.wait_ge(sem("head_pads"), 4)

            def norm_head(m, kq, slot):
                wait(dve, sem("h_sq"), kq + 1)
                nc.vector.tensor_reduce(HS[:], SQ1[:], AX.X, ALU.add).then_inc(sem("h_ss"), 1)
                wait(dve, sem("h_rstd"), kq + 1)
                nc.vector.tensor_tensor(KN[:, slot], pad5(0), over(HR[:], P), ALU.mult).then_inc(
                    sem("rows_read"), 1)

            with dve.Fori(0, KV) as i:
                for c, (kind, col0, br) in enumerate(KVT):
                    nn, nhalf = tile_no(N_KV, 6, i, c + 1)
                    split_lo(dve, nn, nhalf)
                    for t_ in ([4, 5] if c == 5 else [c - 1] if c else []):
                        slot = t_ % 2
                        wait(dve, sem(f"rows_out{slot}"), 32 * (3 * i + t_ // 2) + 32)
                        if t_ < 2:
                            wait(dve, sem("v_copied"), 2 * i + 1 + t_)
                        elif t_ < 5:
                            wait(dve, sem("back_turned"), 3 * i + t_ - 1)
                        else:
                            wait(dve, sem("vm_done"), i + 1)
                        if t_ < 3:
                            norm_head(6 * i + t_, 3 * i + t_, slot)
                        else:
                            wait(dve, sem("head_turned"), 6 * i + t_ + 3)
                            nc.vector.tensor_copy(KN[:, slot], pad5(0)).then_inc(sem("rows_read"), 1)
                            if t_ == 3:
                                wait(dve, sem("rows_read"), 6 * i + 5)
                                dve.sem_inc(sem("vc_rows"), 1)
                    if c == 2:
                        wait(dve, sem("back_turned"), 3 * i + 1)
                        nc.vector.tensor_reduce(KSUM[:], X[:, 2, :].rearrange("p (b t) -> p b t", t=64), AX.X,
                                                ALU.add).then_inc(sem("ksum"), 1)
                        wait(dve, sem("ksum"), i + 1)
                        dve.sem_inc(sem("back_used"), 1)
                        nc.vector.tensor_scalar(KM[:, bass.ds(i, 1), 0:8].rearrange("p a n -> p (a n)"), KSUM[:],
                                                1.0 / 64, None, ALU.mult).then_inc(sem("km_ready"), 1)
                wait(dve, sem("vm_done"), i + 1)
                nc.vector.tensor_copy(VM4[:, bass.ds(i, 1), :].rearrange("p a n -> p (a n)"), X[:, 3, 0:P]).then_inc(
                    sem("vm_used"), 1)
            dve.wait_ge(sem("v_copied"), 10)
            for b in range(2):
                dve.wait_ge(sem(f"rows_out{b}"), 32 * 12 + 32)
            with dve.Fori(0, KV) as i:
                for c in range(8):
                    nn, nhalf = tile_no(N_QZ, 8, i, c + 1)
                    split_lo(dve, nn, nhalf)
                    if 1 <= c <= 4:
                        kq = 12 + 4 * i + c - 1
                        wait(dve, sem("back_turned"), kq - 1)
                        norm_head(24 + 4 * i + c - 1, kq, (c - 1) % 2)
            dve.wait_ge(sem("back_used"), 29)
            nc.vector.tensor_scalar(QP[:, :, :, 0:REP],
                                    A[:, :, SEQ:T].rearrange("p (g h) s -> p s g h", g=KV), SCALE, None,
                                    ALU.mult).then_inc(sem("qp_ready"), 1)
            dve.wait_ge(sem("gates_turned"), 1)
            seq.base, seq.n = 16 * PG, 0
            dve.wait_ge(mm_done, N_GATE + 3)
            seq.do(nc.vector.memset(G8[:], 0.0))
            for b in range(3):
                nc.vector.tensor_copy(G8[:, b].rearrange("s (g n) -> s g n", g=KV)[:, :, 0:REP],
                                      X[0:NS, 1, 0:48].rearrange("s (g h b) -> s g h b", g=KV, h=REP)[:, :, :, b]
                                      ).then_inc(sem("gate8_ready"), 1)
            dve.wait_ge(sem("gates_turned"), 2)
            nc.vector.tensor_copy(GS[:], X[:, 1, P:P + 3 * NS].rearrange("p (b s) -> p b s", b=3)).then_inc(
                sem("gates_copied"), 1)

            with dve.Fori(0, 2) as r:
                for hf in range(2):
                    wait(dve, sem("pages_used"), 16 * r + 8 * hf + 8 + 2)
                    it = bass.ds(2 * r + hf, 1)
                    nc.vector.tensor_copy(KMS[:, it, 512:1024].rearrange("p a n -> p (a n)"),
                                          X[:, 2 * hf + 1, :]).then_inc(sem("v_means"), 1)
            xs = X[:, 0, 0:NS * 32].rearrange("p (s n) -> p s n", n=32)
            seq2 = Seq(dve, "dve_step", 16 * PG + 1)
            dve.wait_ge(sem("cs_done"), 1)
            seq2.do(nc.vector.tensor_reduce(CM[:], xs, AX.X, ALU.max))
            nc.vector.tensor_tensor(CE[:], xs, over(CM[:], 32), ALU.subtract).then_inc(sem("cs_shifted"), 1)
            dve.wait_ge(sem("cs_exp"), 1)
            seq2.do(nc.vector.tensor_reduce(CR[:], CE[:], AX.X, ALU.add))
            seq2.do(nc.vector.reciprocal(CR[:], CR[:]))
            nc.vector.tensor_tensor(CE[:], CE[:], over(CR[:], 32), ALU.mult).then_inc(sem("cp_ready"), 1)
            dve.wait_ge(sem("cp_ready"), 1)
            nc.vector.memset(CP[:], 0.0).then_inc(sem("cpad_ready"), 1)
            dve.wait_ge(sem("cpad_ready"), 1)
            for it in range(4):
                r, hf = it // 2, it % 2
                nc.vector.tensor_copy(CP[:, it, :, 0:16], CE[:, 4 * r:4 * r + 4, 16 * hf:16 * hf + 16]).then_inc(
                    sem("cpad_ready"), 1)
            dve.wait_ge(sem("imp_done"), 1)
            nc.vector.tensor_copy(IMP[:], X[0:32, 1, 0:32]).then_inc(sem("imp_copied"), 1)
            dve.wait_ge(sem("cpt_turned"), 1)
            nc.vector.tensor_copy(CPT[:].rearrange("p i n -> p (i n)"), X[:, 2, :]).then_inc(sem("cpt_ready"), 1)
            dve.wait_ge(sem("imp_copied"), 1)
            dve.wait_ge(sem("cmp_consts"), 64)
            v_j = IMP[:, 1:31].unsqueeze(1).to_broadcast([32, 30, 30])
            v_i = IMP[:, 1:31].unsqueeze(2).to_broadcast([32, 30, 30])
            bef = BEF[0:32].rearrange("p (i j) -> p i j", j=30)
            seq2.do(nc.vector.memset(LOW[:], 0.0))
            seq2.do(nc.vector.tensor_tensor(RK1[:], v_j, v_i, ALU.is_gt))
            seq2.do(nc.vector.tensor_tensor(RK2[:], v_j, v_i, ALU.is_equal))
            seq2.do(nc.vector.tensor_tensor(RK2[:], RK2[:], bef, ALU.mult))
            seq2.do(nc.vector.tensor_tensor(RK1[:], RK1[:], RK2[:], ALU.add))
            seq2.do(nc.vector.tensor_reduce(RNK[:], RK1[:], AX.X, ALU.add))
            nc.vector.tensor_scalar(LOW[:, 1:31], RNK[:], NSEL_FREE - 0.5, None, ALU.is_ge).then_inc(
                sem("low_ready"), 1)
            dve.wait_ge(sem("oc_done"), 1)
            dve.wait_ge(sem("gates_copied"), 2)
            for s4 in range(4):
                nc.vector.tensor_tensor(OC[:, s4::4, :], X[:, s4, 0:2 * P].rearrange("p (r n) -> p r n", r=2),
                                        over(GS[:, 0, s4::4], P), ALU.mult).then_inc(sem("oc_ready"), 1)
            dve.wait_ge(sem("low_spread"), 1)
            seq2.do(nc.vector.tensor_scalar(SBIAS[:].rearrange("p s n -> p (s n)"), X[:, 0, 0:NS * 32], NEG, None,
                                            ALU.mult))
            dve.sem_inc(sem("bias_ready"), 1)

            dve.sem_inc(sem("sel_read"), 4)
            dve.sem_inc(sem("os_done"), 1)
            dve.sem_inc(sem("o_rows"), 1)
            seq4 = Seq(dve, "dve_step", 0)
            SEQ4 = 16 * PG + 1 + 10

            def sample_softmax(i, first):
                s_i = slice(i, i + 1) if isinstance(i, int) else bass.ds(i, 1)
                nc.vector.tensor_copy(QS[:], QP[:, s_i].rearrange("p a g n -> p (a g) n")).then_inc(
                    sem("q_static"), 1)
                wait(dve, sem("new_scored"), i + 2)
                if not first:
                    wait(dve, sem("p_turned"), 6 * i)
                seq4.do(nc.vector.tensor_copy(SC[:, PAGES * P:PAGES * P + 1], MP[:, 0, 1, 8:9]))
                wait(dve, sem("sc_done"), 5 * i + 2)
                nc.vector.tensor_reduce(SST[:, 0:1], X[:, 2, :], AX.X, ALU.max, negate=True).then_inc(
                    sem("win_max"), 1)
                for b in range(1, 5):
                    wait(dve, sem("sc_done"), 5 * i + b + 2)
                    sb_ = SBIAS[:, s_i, 8 * (b - 1):8 * b].rearrange("p a n -> p (a n)")
                    nc.vector.tensor_tensor(SC[:, (b - 1) * 512:b * 512].rearrange("p (n t) -> p n t", t=64),
                                            X[:, 2 + b % 2, :].rearrange("p (n t) -> p n t", t=64),
                                            over(sb_, 64), ALU.add).then_inc(sem("sel_read"), 1)
                wait(dve, sem("sel_read"), 4 * i + 8)
                nc.vector.tensor_reduce(SST[:, 2:3], SC[:], AX.X, ALU.max, negate=True).then_inc(sem("sel_max"), 1)

            def sample_rows(i, i1):
                s_1 = slice(i1, i1 + 1) if isinstance(i1, int) else bass.ds(i1, 1)
                wait(dve, sem("pv_done"), i + 1)
                seq4.do(nc.vector.scalar_tensor_tensor(out=OSM[:, 0], in0=MP[:, 0, 0, 0:P], scalar=SST[:, 7:8],
                                                       in1=OC[:, s_1, :].rearrange("p a n -> p (a n)"),
                                                       op0=ALU.mult, op1=ALU.add))
                nc.vector.scalar_tensor_tensor(out=OSM[:, 1], in0=MP[:, 0, 0, P:2 * P], scalar=SST[:, 6:7],
                                               in1=OSM[:, 0], op0=ALU.mult, op1=ALU.add).then_inc(sem("o_rows"), 1)

            def sample_weights(i):
                s_i = slice(i, i + 1) if isinstance(i, int) else bass.ds(i, 1)
                for q in range(6):
                    wait(dve, sem("p_turned"), 6 * i + q + 1)
                    if q == 0:
                        ins = nc.vector.tensor_copy(WPT[:].rearrange("p t n -> p (t n)"), MP[:, 1, 0, :])
                    elif q < 5:
                        ins = nc.vector.tensor_copy(SPT[:, 4 * (q - 1):4 * q, :].rearrange("p t n -> p (t n)"),
                                                    MP[:, 1, q % 2, :])
                    else:
                        ins = nc.vector.tensor_copy(SPT[0:1, PAGES, :], MP[0:1, 0, 1, P:2 * P])
                    ins.then_inc(sem("p_evac"), 1)
                wait(dve, sem("sel_exp"), i + 1)
                seq4.do(nc.vector.reciprocal(SST[:, 4:6], SST[:, 1:4:2]))
                seq4.do(nc.vector.tensor_tensor(SST[:, 6:7], SST[:, 4:5], GS[:, 2, s_i], ALU.mult))
                seq4.do(nc.vector.tensor_tensor(SST[:, 7:8], SST[:, 5:6], GS[:, 1, s_i], ALU.mult))

            def sample_store(i, i1):
                wait(dve, sem("o_turned"), i)
                nc.vector.tensor_copy(A[:, :, bass.ds(SEQ + i1, 1)].rearrange("p (g h) a -> p g (h a)", g=KV),
                                      MP[:, 0, 1, 2 * P:3 * P].rearrange("p (g n) -> p g n", g=KV)[:, :, 0:REP]
                                      ).then_inc(sem("os_done"), 1)

            seq4.base = SEQ4
            sample_softmax(0, True)
            sample_weights(0)
            with dve.Fori(1, NS) as i:
                seq4.loop(i, 5, SEQ4 - 1)
                sample_softmax(i, False)
                sample_rows(i, i - 1)
                sample_weights(i)
                sample_store(i, i - 1)
            seq4.base, seq4.n = SEQ4 + 4 + 5 * (NS - 1), 0
            sample_rows(NS, NS - 1)
            sample_store(NS, NS - 1)

            dve.wait_ge(sem("os_done"), NS + 1)
            dve.wait_ge(sem("attn_consts"), 48)
            nc.vector.tensor_copy(CAB[:], CAU[:]).then_inc(sem("attn_ready"), 1)
            nc.vector.tensor_copy(IDB[:], ident[:]).then_inc(sem("attn_ready"), 1)
            seq5 = Seq(dve, "dve_step", SEQ4 + 5 * NS)
            seq5.do(nc.vector.memset(CPP[:], 0.0))
            dve.sem_inc(sem("p4_scaled"), 8)
            dve.sem_inc(sem("o_used"), 2)
            with dve.Fori(0, KV) as i:
                seq5.loop(i, 7 + 32 + 4, SEQ4 + 5 * NS + 1)
                wait(dve, sem("pv4"), 8 * i + 2)
                nc.vector.tensor_scalar(QC[:], A[:, bass.ds(4 * i, REP), 0:SEQ], SCALE, None, ALU.mult).then_inc(
                    sem("qc_ready"), 1)
                wait(dve, sem("c4_scored"), i + 1)
                nc.vector.tensor_copy(CS[:], X[:, 0, :]).then_inc(sem("c4_rows"), 1)
                wait(dve, sem("c4_turned"), i + 1)
                cx = CX[:].rearrange("p j e n -> p (j e) n")
                x1 = X[:, 1, :].rearrange("p (q n) -> p q n", n=32)[:, :, 0:8]
                seq5.do(nc.vector.tensor_tensor(cx, x1, CBI[:].rearrange("p j e n -> p (j e) n"), ALU.add))
                cm, cs_ = CMX[:].rearrange("p j e -> p (j e)"), CSM[:].rearrange("p j e -> p (j e)")
                seq5.do(nc.vector.tensor_reduce(cm, cx, AX.X, ALU.max))
                nc.vector.tensor_tensor(cx, cx, over(cm, 8), ALU.subtract).then_inc(sem("c4_shifted"), 1)
                wait(dve, sem("c4_exp"), i + 1)
                seq5.do(nc.vector.tensor_reduce(cs_, cx, AX.X, ALU.add))
                seq5.do(nc.vector.reciprocal(cs_, cs_))
                g0 = GT[:, :, bass.ds(12 * i, 12)].rearrange("p j (e b) -> p j e b", b=3)[:, :, :, 0]
                seq5.do(nc.vector.tensor_tensor(CSM[:], CSM[:], g0, ALU.mult))
                seq5.do(nc.vector.tensor_tensor(cx, cx, over(cs_, 8), ALU.mult))
                nc.vector.tensor_tensor(CPP[:].rearrange("p j e n -> p (j e) n")[:, :, 0:8], cx,
                                        COK[:].rearrange("p j e n -> p (j e) n"), ALU.mult).then_inc(
                    sem("c4_probs"), 1)
                wait(dve, sem("c4_back"), i + 1)
                seq5.do(nc.vector.tensor_copy(CPX[:], X[:, 0, :]))
                dve.sem_inc(sem("c4_probs_t"), 1)

                def max4(w):
                    j = w % 4
                    wait(dve, sem("s4_done"), 32 * i + w + 1)
                    nc.vector.tensor_reduce(AMX[:, w % 8:w % 8 + 1], X[:, w % 4, 0:(j + 1) * P], AX.X, ALU.max,
                                            negate=True).then_inc(sem("max4"), 1)

                max4(0)
                max4(1)
                for w in range(32):
                    e, br, j = w // 8, (w // 4) % 2, w % 4
                    if w + 2 < 32:
                        max4(w + 2)
                    wait(dve, sem("p4_exp"), 32 * i + w + 5)
                    seq5.do(nc.vector.reciprocal(AW[:, w % 8:w % 8 + 1], ASM[:, w % 8:w % 8 + 1]))
                    nc.vector.tensor_scalar(PR[:, w % 4, 0:(j + 1) * P], PR[:, w % 4, 0:(j + 1) * P],
                                            AW[:, w % 8:w % 8 + 1], GT[:, j, bass.ds(12 * i + 3 * e + 1 + br, 1)],
                                            ALU.mult, ALU.mult).then_inc(sem("p4_scaled"), 1)
                    for e2 in ([e - 1] if w % 8 == 4 and e >= 1 else []) + ([3] if w == 31 else []):
                        wait(dve, sem("pv4"), 8 * i + 2 * e2 + 4)
                        wait(dve, sem(f"sz_landed{e2 % 2}"), 32 * i + 16 * (e2 // 2) + 16)
                        a = A[:, bass.ds(4 * i + e2, 1), :].rearrange("p a t -> p (a t)")
                        seq5.do(nc.vector.tensor_tensor(a[:, SEQ:T], a[:, SEQ:T], SZH[:, e2 % 2, SEQ:T], ALU.mult))
                        nc.vector.tensor_tensor(a[:, 0:SEQ], MP[:, 1, e2 % 2, :], SZH[:, e2 % 2, 0:SEQ],
                                                ALU.mult).then_inc(sem("o_used"), 1)
                assert seq5.n == 43, seq5.n

            dve.sem_inc(held, 1)
            split_lo(dve, N_ODD_OUT, (N_ODD_OUT // 2, N_ODD_OUT % 2))
            split_act_dve(dve, 3)

            def out_dve(i, last):
                for c in range(2):
                    n, (h, slot) = tile_no(N_ODD_OUT, 2, i, c)
                    nn, nhalf = tile_no(N_ODD_OUT, 2, i, c + 1)
                    if not (last and c == 1):
                        split_lo(dve, nn, nhalf)
                    wait(dve, mm_done, n + 3)
                    wait(dve, sem(f"res_landed{slot}"), 128 + 16 * i + 16)
                    wait(dve, sem("y_turned"), 2 * i + c + 1)
                    nc.vector.tensor_tensor(two(YT[:, slot]), mp(slot), two(XR[:, slot]), ALU.add).then_inc(
                        evac[slot], 1)

            with dve.Fori(0, 7) as i:
                out_dve(i, False)
            out_dve(7, True)

        @block.gpsimd
        def _(pool):
            pseq = Seq(pool, "pool_step")
            nc.gpsimd.memset(eps_t[:], EPS).then_inc(sem("setup_set"), 1)
            nc.gpsimd.memset(mhalf[:], -0.5).then_inc(sem("setup_set"), 1)
            nc.gpsimd.dma_start(STR[:], I["state_pool"].rearrange("s r c -> (s r) c")).then_inc(
                sem("raw_landed"), 16)
            nc.gpsimd.dma_start(WSR[:], I["w_spatial"].rearrange("h i j -> i h j")).then_inc(
                sem("raw_landed"), 16)
            loads = [(ones[:], cst("ones")), (TRIL[:], cst("tril_t")), (DI8[:], cst("diag8")),
                     (PAR[:], cst("pool").rearrange("p (g n) -> p g n", g=PG)),
                     (g_even[:], I["norm_even"].rearrange("(k p) -> p k", p=P)),
                     (g_odd[:], I["norm_odd"].rearrange("(k p) -> p k", p=P)),
                     (VG[:], I["v_norm"].partition_broadcast(P)),
                     (BS[:], I["b_spatial"].rearrange("h i -> (h i)").partition_broadcast(P)),
                     (W00[:], I["w_spatial"][:, 0, 0].partition_broadcast(P)),
                     (PSC[:], I["pool_scale"].rearrange("(g e p) -> p g e", g=PG, p=P))]
            loads += [(WP[:, g], I["w_pool"][g].rearrange("(c p) e -> p c e", p=P)) for g in range(PG)]
            with nc.allow_non_contiguous_dma(reason="a few parameters, one element per row"):
                for dst, src in loads:
                    nc.gpsimd.dma_start(dst, src).then_inc(sem("setup"), 16)
            assert SETUP == 16 * len(loads)
            for lo, hi, s_ in ((0, 2, "gv_out"), (2, 5, "tail_out"), (5, 8, "tail_out")):
                nc.gpsimd.dma_start(O["pool_sample"][lo:hi, 0:PAD - 1, :], I["state_pool"][lo:hi, 1:PAD, :]).then_inc(
                    sem(s_), 16)
            pool.wait_ge(sem("x_evac0"), 9)
            pool.wait_ge(sem("x_evac1"), 9)
            nc.gpsimd.dma_start(xT_scr.rearrange("k p t -> p k t"), A[:]).then_inc(sem("xT_out"), 16)
            pool.wait_ge(sem("lo_done"), KT)
            pool.wait_ge(sem("x_evac0"), 12)
            nc.gpsimd.memset(VT[:, T:TP], 0.0).then_inc(sem("pads"), 1)
            for e in range(2):
                nc.gpsimd.memset(EX[e][:, 0:PAD], 0.0).then_inc(sem("pads"), 1)
            pool.wait_ge(sem("pads"), 3)

            with pool.Fori(0, PG) as i:
                pseq.loop(i, 2, 0)
                wait(pool, sem("y_ready"), 2 * i + 1)
                wait(pool, sem("y_used"), 2 * i + 1)
                wait(pool, sem("pool_d"), 2 * i + 2)
                nc.gpsimd.tensor_copy(PARG[:], PAR[:, bass.ds(i, 1), :].rearrange("p a n -> p (a n)")).then_inc(
                    sem("group_ready"), 1)
                nc.gpsimd.tensor_copy(PSG[:], PSC[:, bass.ds(i, 1), :].rearrange("p a n -> p (a n)")).then_inc(
                    sem("group_ready"), 1)
                nc.gpsimd.tensor_copy(WPG[:], WP[:, bass.ds(i, 1)].rearrange("p a c e -> p (a c) e")).then_inc(
                    sem("group_ready"), 1)
                for e in range(2):
                    wait(pool, sem("tail_turned"), 2 * i + e + 1)
                    hist = EX[e][:, PAD + SEQ:EXT].rearrange("p (s r) -> p s r", r=16)[:, :, 0:PAD]
                    nc.gpsimd.tensor_copy(hist, STP[:, bass.ds(2 * i + e, 1), :].rearrange(
                        "p a (s r) -> p (a s) r", r=PAD)).then_inc(sem("hist_ready"), 1)
                for e in range(2):
                    wait(pool, sem("v_ss"), 2 * i + e + 2)
                    pseq.do(nc.gpsimd.tensor_scalar(SR[:], SS[:], 1.0 / P, EPS, ALU.mult, ALU.add))
                    nc.gpsimd.tensor_tensor(SR[:], SR[:], mhalf[:, 0:5], ALU.pow).then_inc(sem("v_rstd"), 1)
                    wait(pool, sem("v_mul"), 2 * i + e + 1)
                    vg = VG[:, bass.ds((2 * i + e) * P, P)].unsqueeze(1).to_broadcast([P, 5, P])
                    nc.gpsimd.tensor_tensor(VN[:], VN[:], vg, ALU.mult).then_inc(sem("v_ready"), 1)
                    col = nc.gpsimd.snap((2 * i + e) * P, min_val=0, max_val=1024 - P)
                    wait(pool, sem("v_ready"), 2 * i + e + 1)
                    nc.gpsimd.dma_start(O["gmlp_v_sample"][:, bass.ds(col, P)], VN[0:NS, 4, :]).then_inc(
                        sem("gv_out"), 16)
                for e in range(2):
                    col = nc.gpsimd.snap((2 * i + e) * P, min_val=0, max_val=1024 - P)
                    wait(pool, sem("tail_copied"), 2 * i + e + 2)
                    wait(pool, sem("tail_first"), 2 * i + e + 1)
                    nc.gpsimd.dma_start(O["pool_prompt"][:, bass.ds(col, P)], TLP[:]).then_inc(sem("tail_out"), 16)
                    nc.gpsimd.dma_start(O["pool_sample"][:, PAD - 1, bass.ds(col, P)], TLS[:]).then_inc(
                        sem("tail_out"), 16)
            with pool.Fori(0, 8) as i:
                for c in range(2):
                    n, (h, slot) = tile_no(N_EVEN_OUT, 2, i, c)
                    kt = nc.gpsimd.snap(2 * i + c, min_val=0, max_val=KT - 1)
                    wait(pool, evac[slot], h + 2)
                    nc.gpsimd.dma_start(x1_scr[bass.ds(kt, 1)].rearrange("a p t -> p (a t)"),
                                        act_tile(2 * i + c)).then_inc(sem("x1_out"), 16)

            pool.wait_ge(sem("y_used"), 9)
            pool.wait_ge(sem("tail_out"), 32 + 32 * AH)
            pool.wait_ge(evac[0], 29)
            nc.gpsimd.dma_start(GQ[:, 0], I["q_norm"][0].partition_broadcast(P)).then_inc(sem("rows_out0"), 16)
            nc.gpsimd.dma_start(GQ[:, 1:4].rearrange("p a n -> p (a n)"), I["k_norm"].rearrange(
                "a n -> (a n)").partition_broadcast(P)).then_inc(sem("rows_out0"), 16)
            nc.gpsimd.dma_start(COS[:].rearrange("p j n -> p (j n)"), cst("cos")).then_inc(sem("rows_out1"), 16)
            nc.gpsimd.dma_start(SIN[:].rearrange("p j n -> p (j n)"), cst("sin")).then_inc(sem("rows_out1"), 16)
            pool.wait_ge(sem("lo_done"), 3 * KT)
            nc.gpsimd.dma_start(VMASK[:].rearrange("p j n -> p (j n)"), cst("prompt_blocks")).then_inc(
                sem("setup"), 16)
            nc.gpsimd.memset(KTT[:, :, T:TP], 0.0).then_inc(sem("head_pads"), 1)
            nc.gpsimd.memset(KM[:], 0.0).then_inc(sem("head_pads"), 1)
            nc.gpsimd.memset(QP[:], 0.0).then_inc(sem("head_pads"), 1)
            pool.wait_ge(sem("setup"), SETUP + 16)
            for b in range(2):
                pool.wait_ge(sem(f"rows_out{b}"), 32)
            pool.sem_inc(sem("head_pads"), 1)
            pool.sem_inc(sem("v_copied"), 2)
            pseq2 = Seq(pool, "pool_step", 0)

            def finish_head(kq, slot, gain):
                wait(pool, sem("h_ss"), kq + 2)
                pseq2.do(nc.gpsimd.tensor_scalar(HR[:], HS[:], 1.0 / P, EPS, ALU.mult, ALU.add))
                nc.gpsimd.tensor_tensor(HR[:], HR[:], mhalf[:, 0:5], ALU.pow).then_inc(sem("h_rstd"), 1)

            def rotate(m, kq, slot, gain):
                wait(pool, sem("rows_read"), m + 2)
                kn = KN[:, slot]
                pseq2.do(nc.gpsimd.tensor_tensor(kn, kn, GQ[:, gain].unsqueeze(1).to_broadcast([P, 5, P]), ALU.mult))
                x1, x2 = kn[:, :, 0:16], kn[:, :, 16:32]
                pseq2.do(nc.gpsimd.tensor_tensor(RA[:, :, 0:16], x1, COS[:], ALU.mult))
                pseq2.do(nc.gpsimd.tensor_tensor(RA[:, :, 16:32], x2, COS[:], ALU.mult))
                pseq2.do(nc.gpsimd.tensor_tensor(RB[:, :, 0:16], x2, SIN[:], ALU.mult))
                pseq2.do(nc.gpsimd.tensor_tensor(RB[:, :, 16:32], x1, SIN[:], ALU.mult))
                pseq2.do(nc.gpsimd.tensor_tensor(x1, RA[:, :, 0:16], RB[:, :, 0:16], ALU.subtract))
                pseq2.do(nc.gpsimd.tensor_tensor(x2, RA[:, :, 16:32], RB[:, :, 16:32], ALU.add))
                pool.sem_inc(sem("rows_ready"), 1)

            with pool.Fori(0, KV) as i:
                pseq2.loop(i, 8 * 3, 8)
                for c, (kind, col0, br) in enumerate(KVT):
                    slot = c % 2
                    if c < 3:
                        finish_head(3 * i + c, slot, 1 + br)
                        rotate(6 * i + c, 3 * i + c, slot, 1 + br)
                    else:
                        wait(pool, sem("rows_read"), 6 * i + c + 2)
                        if c > 3:
                            nc.gpsimd.tensor_copy(VS[:, br - 1, bass.ds(i, 1)].rearrange("p a j n -> p (a j) n"),
                                                  KN[:, slot, 0:TT, :]).then_inc(sem("v_copied"), 1)
                    col = nc.gpsimd.snap((0 if c < 3 else 512) + i * P, min_val=0, max_val=1024 - P)
                    nc.gpsimd.dma_start(kv_p[br].rearrange("(j p) c -> p j c", p=P)[:, :, bass.ds(col, P)],
                                        KN[:, slot, 0:TT, :]).then_inc(sem(f"rows_out{slot}"), 16)
                    dst = kv_s[br] if br < 2 else kv_s[2][:, 511, :]
                    nc.gpsimd.dma_start(dst[:, bass.ds(col, P)], KN[0:NS, slot, 4, :]).then_inc(
                        sem(f"rows_out{slot}"), 16)
            with pool.Fori(0, KV) as i:
                pseq2.loop(i, 8 * 4, 104)
                for e in range(REP):
                    finish_head(12 + 4 * i + e, e % 2, 0)
                    rotate(24 + 4 * i + e, 12 + 4 * i + e, e % 2, 0)

            pool.wait_ge(sem("bias_ready"), 1)
            pool.wait_ge(sem("table_landed"), 16)
            for b in range(2):
                pool.wait_ge(sem(f"rows_out{b}"), 32 * 12 + 32)
            with pool.Fori(0, NS) as i:
                smp = nc.gpsimd.snap(i, min_val=0, max_val=NS - 1)
                wait(pool, sem("pv_done"), i + 1)
                nc.gpsimd.dma_start(NRV[:], O["sel_kv_sample"][bass.ds(smp, 1), 512:1024]).then_inc(
                    sem("vals_landed"), 16)
                window_half(nc.gpsimd, smp, KWV, 512, sem("vals_landed"))
                for j in range(PAGES):
                    page = page_at(nc.gpsimd, "cache_sel_kv", PAGES * i + j)
                    nc.gpsimd.dma_start(SV[:, j], page[:, 512:1024]).then_inc(sem("vals_landed"), 16)

            pool.wait_ge(sem("os_done"), NS + 1)
            with pool.Fori(0, KV) as i:
                wait(pool, sem("pv4"), 8 * i + 2)
                for br in range(2):
                    nc.gpsimd.tensor_copy(VB[:, br], VS[:, br, bass.ds(i, 1)].rearrange("p a j n -> p (a j) n")
                                          ).then_inc(sem("static_copied"), 1)
                nc.gpsimd.tensor_copy(KMG[:], KM[:, bass.ds(i, 1), :].rearrange("p a n -> p (a n)")).then_inc(
                    sem("static_copied"), 1)
                nc.gpsimd.tensor_copy(VMG[:], VM4[:, bass.ds(i, 1), :].rearrange("p a n -> p (a n)")).then_inc(
                    sem("static_copied"), 1)
                wait(pool, sem("static_copied"), 4 * i + 4)
                pool.sem_inc(sem("group_static"), 1)

NPHYS = 160
SETUP = 16 * 14


def kernel(**inputs):
    import concourse.bacc as bacc
    from concourse.bass_utils import run_bass_kernel_spmd

    nc = bacc.Bacc("TRN2", target_bir_lowering=False, num_devices=1)
    views = {
        "x_prompt": (SEQ, D), "x_sample": (NS, D), "cache_cmp_kv": (-1, P, 1024), "cache_sel_kv": (-1, P, 1024),
        "state_win_kv": (NS, 512, 1024), "state_pool": (NS, PAD, 1024), "page_table": (1, NS * PAGES),
        "norm_even": (D,), "w_in_even": (D, 5120), "v_norm": (1024,), "w_spatial": (AH, P, P),
        "b_spatial": (AH, P), "w_pool": (PG, 256, 256), "pool_scale": (1024,), "w_out_even": (D, D),
        "norm_odd": (D,), "w_in_odd": (D, 7216), "q_norm": (1, P), "k_norm": (3, P), "w_out_odd": (D, D),
    }
    arrays = {name: np.ascontiguousarray(inputs[name]).reshape(shape) for name, shape in views.items()}
    arrays["consts"] = _lay_consts()
    I = {name: nc.dram_tensor(name, a.shape, mybir.dt.from_np(a.dtype), kind="ExternalInput").ap()
         for name, a in arrays.items()}
    outs = [("y_prompt", (SEQ, D)), ("y_sample", (NS, D)),
            ("cmp_kv_prompt", (SEQ, 1024)), ("cmp_kv_sample", (NS, 1024)),
            ("sel_kv_prompt", (SEQ, 1024)), ("sel_kv_sample", (NS, 1024)),
            ("win_kv_prompt", (SEQ, 1024)), ("win_kv_sample", (NS, 512, 1024)),
            ("pool_prompt", (PAD, 1024)), ("pool_sample", (NS, PAD, 1024)), ("gmlp_v_sample", (NS, 1024))]
    O = {name: nc.dram_tensor(name + "_out", shape, F32, kind="ExternalOutput").ap() for name, shape in outs}
    xT_scr = nc.dram_tensor("xT_scr", (KT, P, T), F32, kind="Internal").ap()
    x1_scr = nc.dram_tensor("x1_scr", (KT, P, T), F32, kind="Internal").ap()
    szT_scr = nc.dram_tensor("szT_scr", (KT, P, T), F32, kind="Internal").ap()
    build(nc, I, O, xT_scr, x1_scr, szT_scr)
    r = run_bass_kernel_spmd(nc, [arrays], core_ids=[0]).results[0]
    shapes = {"y_prompt": (1, SEQ, D), "y_sample": (NS, 1, D), "pool_prompt": (1, 1, PAD, 1024),
              "pool_sample": (1, NS, PAD, 1024), "gmlp_v_sample": (1, NS, 1, 1024),
              "cmp_kv_prompt": (1, 1, SEQ, 2, KV, HD), "cmp_kv_sample": (1, NS, 1, 2, KV, HD),
              "sel_kv_prompt": (1, 1, SEQ, 2, KV, HD), "sel_kv_sample": (1, NS, 1, 2, KV, HD),
              "win_kv_prompt": (1, 1, SEQ, 2, KV, HD), "win_kv_sample": (1, NS, 512, 2, KV, HD)}
    return tuple(r[name + "_out"].reshape(shapes[name]) if name in shapes else r[name + "_out"] for name, _ in outs)
```

```python
from contextlib import ExitStack

import numpy as np
import concourse.bass as bass
from concourse import mybir

F32 = mybir.dt.float32
F32R = mybir.dt.float32r
BF16 = mybir.dt.bfloat16
I32 = mybir.dt.int32
ALU = mybir.AluOpType
ACT = mybir.ActivationFunctionType
AX = mybir.AxisListType

P = 128
D = 2048
KT = D // P
SEQ = 512
NS = 8
T = SEQ + NS
HALF = T // 2
TT = SEQ // P
TP = 5 * P
EPS = 1e-6
AH = 8
PG = 4
PAD = 15
HEADS = 16
KV = 4
REP = HEADS // KV
HD = 128
PAGES = 16
NBLK = 32
NSEL_FREE = 13
NEG = -1e30
SCALE = HD ** -0.5
PAST = 2048
EXT = PAD + SEQ + NS * 16

N_EVEN_IN, N_EVEN_OUT, N_KV, N_Q, N_Z, N_GATE, N_ODD_OUT = 0, 40, 56, 80, 96, 112, 113

CONSTS = {}


def _lay_consts():
    parts, at = [], 0

    def put(name, a):
        nonlocal at
        a = np.asarray(a, np.float32).reshape(P, -1)
        CONSTS[name] = (at, a.shape[1])
        parts.append(a)
        at += a.shape[1]

    p = np.arange(P)
    put("ident", np.eye(P))
    put("ones", np.ones((P, P)))
    put("tril_t", p[:, None] <= p[None, :])
    put("diag8", np.eye(P)[:, :NS])
    pos = np.zeros((P, 5), np.float32)
    pos[:, :TT] = p[:, None] + P * np.arange(TT)[None, :]
    pos[:, TT] = PAST
    inv_freq = np.float32(500000.0) ** (-np.arange(16, dtype=np.float32) * np.float32(2.0 / 32))
    ang = (pos[:, :, None] * inv_freq[None, None, :]).astype(np.float32).astype(np.float64)
    cos, sin = np.cos(ang), np.sin(ang)
    put("cos", cos)
    put("sin", sin)
    par = np.zeros((P, PG, 4 + PAD))
    for g, w in enumerate((2, 4, 8, 16)):
        par[:, g, 0:3] = [w >= 4, w >= 8, w >= 16]
        par[:, g, 3] = 1.0 / w
        par[:, g, 4:] = 1.0 / np.minimum(np.arange(PAD) + 1, w)
    put("pool", par)
    bm = np.zeros((P, 8, 32))
    for c in range(8):
        bm[p, c, 2 * c + p // 64] = 1.0 / 64
    put("page_blocks", bm)
    vm = np.zeros((P, TT, REP, 32))
    for j in range(TT):
        vm[p, j, :, 0] = 0
        for h in range(REP):
            vm[p, j, h, 2 * j + p // 64] = 1.0 / 64
    put("prompt_blocks", vm)
    t = p[:, None] + P * np.arange(TT)[None, :]
    ok = ((np.arange(8) + 1) * 64 - 1)[None, None, :] <= t[:, :, None]
    ok4 = np.repeat(ok[:, :, None, :], REP, 2)
    put("cmp_ok", ok4)
    put("cmp_bias", np.where(ok4, 0.0, NEG))
    put("causal", np.where(p[None, :] <= p[:, None], 0.0, NEG))
    rows = np.zeros((P, NS, 32))
    spread = np.zeros((P, NS, P))
    for smp in range(NS):
        for g in range(KV):
            rows[32 * g:32 * g + REP, smp, KV * smp + g] = 1.0
            spread[KV * smp + g, smp, 32 * g:32 * g + 32] = 1.0
    put("imp_rows", rows)
    put("imp_spread", spread)
    i30 = np.arange(30)
    put("before", np.broadcast_to((i30[None, :] < i30[:, None]).reshape(1, -1), (P, 900)))
    return np.ascontiguousarray(np.concatenate(parts, 1))


def build(nc, I, O, xT_scr, x1_scr, szT_scr, means_scr):
    ctx = ExitStack()
    with ctx:
        base = nc.sbuf_base
        base = (base + 127) // 128 * 128
        LIMIT = nc.sbuf_usable_end

        def at(name, off, shape, dt=F32):
            size = int(np.prod(shape[1:])) * (2 if dt == BF16 else 4)
            assert base + off + size <= LIMIT, (name, base + off + size, LIMIT)
            t_ = nc.alloc_sbuf_tensor_at(name, shape, dt, offset=base + off)
            return t_, off + (size + 31) // 32 * 32

        o = 0
        H_OFF = o
        HH, o = at("act_hi", o, [P, KT, T], F32R)
        HL, o = at("act_lo", o, [P, KT, T], F32R)
        WHL_OFF = o
        WH, o = at("w_hi", o, [P, 2, KT, P], F32R)
        WL, o = at("w_lo", o, [P, 2, KT, P], F32R)
        RAW_OFF = o
        RAW, o = at("w_raw", o, [P, 2, KT, P])
        A, o = at("act", o, [P, KT, T])
        ident, o = at("ident", o, [P, P])
        PTAB, _ = at("page_table", o, [1, P], I32)
        ones, o = at("ones", o, [P, P])
        g_even, o = at("gain_even", o, [P, KT])
        g_odd, o = at("gain_odd", o, [P, KT])
        eps_t, o = at("eps", o, [P, 1])
        mhalf, o = at("minus_half", o, [P, 8])
        R_OFF = o

        o = R_OFF
        VG, o = at("v_gain", o, [P, AH * P])
        BS, o = at("b_spatial", o, [P, AH * P])
        WST, o = at("w_spatial_t", o, [P, AH, P])
        DG, o = at("w00_diag", o, [P, AH, NS])
        W00, o = at("w00", o, [P, AH])
        WP, o = at("w_pool", o, [P, PG, 2, 256])
        WPG, o = at("w_pool_group", o, [P, 2, 256])
        PSC, o = at("pool_scale", o, [P, PG, 2])
        PAR, o = at("pool_par", o, [P, PG, 4 + PAD])
        PARG, o = at("pool_par_group", o, [P, 4 + PAD])
        PSG, o = at("pool_scale_group", o, [P, 2])
        STP, o = at("pool_state_t", o, [P, AH, NS * PAD])
        E_OFF = o
        VT, o = at("v_t", o, [P, TP])
        VN, o = at("v_norm", o, [P, 5, P])
        C1, o = at("chain1", o, [P, EXT])
        C2, o = at("chain2", o, [P, EXT])
        UT, o = at("u_t", o, [P, T])
        SZ, o = at("silu_z", o, [P, T])
        EX0, o = at("pool_in0", o, [P, EXT])
        EX1, o = at("pool_in1", o, [P, EXT])
        PD, o = at("pool_diff", o, [P, 2, T])
        TLP, o = at("pool_tail", o, [PAD, P])
        TLS, o = at("pool_tail_s", o, [NS, P])
        SS, o = at("v_sumsq", o, [P, 5])
        SR, o = at("v_rstd", o, [P, 5])
        FIX, o = at("pool_fix", o, [P, PAD])
        EX = [EX0, EX1]
        o = E_OFF
        XS, o = at("x_stage", o, [P, 2, D])
        WSR, o = at("w_spatial_raw", o, [P, AH, P])
        STR, o = at("pool_state_raw", o, [NS * PAD, AH * P])
        TRIL, o = at("tril_t", o, [P, P])
        DI8, o = at("diag8", o, [P, NS])
        o = E_OFF
        SQ, o = at("sq", o, [P, 2, T])
        RS, o = at("rstd", o, [P, T])
        TM, o = at("norm_tmp", o, [P, 2, T])
        o = R_OFF
        XR, o = at("residual", o, [P, 2, T])
        YT, o = at("y_t", o, [P, 2, T])
        YS, o = at("y_rows", o, [P, 2, 5, P])

        o = R_OFF
        KTS, o = at("k_t", o, [P, 2, KV, SEQ])
        PGT0, o = at("cmp_pages0", o, [P, 2, 4, 512])
        VM4, o = at("v_cmp_mean", o, [P, KV, P])
        KM, o = at("k_cmp_mean", o, [P, KV, 32])
        BM, _ = at("page_blocks", o, [P, 8, 32])
        GT, o = at("gate_rows", o, [P, TT, P])
        GS, o = at("gate_sample", o, [P, 3, NS])
        QP, o = at("q_sample", o, [P, NS, KV, 32])
        L1_OFF = o
        KTT, o = at("head_t", o, [P, 2, TP])
        KN, o = at("head_rows", o, [P, 2, 5, P])
        SQ1, o = at("head_sq", o, [P, 5, P])
        GQ, o = at("qk_gain", o, [P, 4, P])
        COS, o = at("cos", o, [P, 5, 16])
        SIN, o = at("sin", o, [P, 5, 16])
        RA, o = at("rope_a", o, [P, 5, 32])
        RB, o = at("rope_b", o, [P, 5, 32])
        HS, o = at("head_ss", o, [P, 5])
        HR, o = at("head_rstd", o, [P, 5])
        VMASK, _ = at("prompt_blocks", o, [P, TT, P])
        ZT, o = at("z_t", o, [P, T])
        STG, o = at("means_stage", o, [P, 512])
        KSUM, o = at("k_block_sum", o, [P, 8])
        PGT1, o = at("cmp_pages1", L1_OFF, [P, 2, 4, 512])
        PGT = [PGT0, PGT1]
        o = L1_OFF
        SBIAS, o = at("sel_bias", o, [P, NS, NBLK])
        OC, o = at("o_cmp", o, [P, NS, P])
        o = H_OFF
        KMS, o = at("cmp_means", o, [P, 4, 1024])
        KMT, o = at("cmp_k_t", o, [P, KV, NS, 32])
        o2 = WHL_OFF
        CE, o2 = at("cmp_e", o2, [P, NS, 32])
        CP, o2 = at("cmp_p_pad", o2, [P, 4, 4, 32])
        CPT, o2 = at("cmp_p_t", o2, [P, 4, P])
        CM, o2 = at("cmp_max", o2, [P, NS])
        CR, o2 = at("cmp_sum", o2, [P, NS])
        GROWS, o2 = at("imp_rows", o2, [P, NS, 32])
        GSPR, o2 = at("imp_spread", o2, [P, NS, P])
        IMP, o2 = at("importance", o2, [32, 32])
        LOW, o2 = at("not_selected", o2, [32, 32])
        BEF, o2 = at("before", o2, [P, 900])
        RK1, o2 = at("rank1", o2, [32, 30, 30])
        RK2, o2 = at("rank2", o2, [32, 30, 30])
        RNK, o2 = at("rank", o2, [32, 30])
        GTT, o2 = at("gate_t", o2, [P, T])
        G8, o2 = at("gate8", o2, [NS, 3, P])
        assert o2 <= WHL_OFF + 28672
        o = H_OFF
        SV, o = at("sel_v", o, [P, PAGES, 512])
        SK, o = at("sel_k", o, [P, 8, 512])
        KWK, o = at("win_k", o, [P, 4, 512])
        KWV, o = at("win_v", o, [P, 4, 512])
        assert o <= WHL_OFF
        o = WHL_OFF
        SC, o = at("scores", o, [P, PAGES * P + 1])
        SPT, o = at("p_t", o, [P, 17, P])
        QS, o = at("q_static", o, [P, KV, 32])
        KNT, o = at("new_k_t", o, [P, KV])
        SWP, o = at("win_p", o, [P, SEQ])
        assert o <= WHL_OFF + 28672
        NRK, o = at("new_k", WHL_OFF + 28672, [1, 512])
        NRV, o = at("new_v", o, [1, 512])
        SKT, o = at("sel_k_t", RAW_OFF, [P, 2, KV, 512])
        o = L1_OFF + 8 * 1024
        WPT, o = at("win_p_t", o, [P, 4, P])
        SST, o = at("s_stat", o, [P, 8])
        OSM, o = at("o_sample", o, [P, 2, P])
        o = H_OFF
        VB, o = at("v_static", o, [P, 2, TT, P])
        QC, o = at("q_cmp", o, [P, REP, SEQ])
        PR, o = at("probs", o, [P, 4, SEQ])
        PT_, o = at("probs_t", o, [P, 2, TT, SEQ])
        CS, o = at("cmp_s_t", o, [P, SEQ])
        KMG, o = at("k_mean_static", o, [P, 32])
        VMG, o = at("v_mean_static", o, [P, P])
        o = WHL_OFF
        CPP, o = at("cmp_probs", o, [P, TT, REP, 32])
        CPX, o = at("cmp_probs_t", o, [P, SEQ])
        COK, o = at("cmp_ok", o, [P, TT, REP, 8])
        CBI, o = at("cmp_bias", o, [P, TT, REP, 8])
        CX, o = at("cmp_x", o, [P, TT, REP, 8])
        CMX, o = at("cmp_mx", o, [P, TT, REP])
        CSM, o = at("cmp_sm", o, [P, TT, REP])
        CAU, o = at("causal", o, [P, P])
        CAB, o = at("causal_bf", o, [P, P], BF16)
        IDB, o = at("ident_bf", o, [P, P], BF16)
        AMX, o = at("a_max", o, [P, 8])
        ASM, o = at("a_sum", o, [P, 8])
        AW, o = at("a_w", o, [P, 8])
        SZH, o = at("sz_head", o, [P, 2, T])
        assert o <= WHL_OFF + 32768

        MP = ctx.enter_context(nc.psum_tensor("main", [P, 2, 2, 512], F32))
        X = ctx.enter_context(nc.psum_tensor("aux", [P, 4, 512], F32))

        sems = {}

        def sem(name):
            if name not in sems:
                sems[name] = ctx.enter_context(nc.semaphore(name))
            return sems[name]

        w_landed = [sem("w_landed0"), sem("w_landed1")]
        w_hi, w_split, mm_done = sem("w_hi"), sem("w_split"), sem("mm_done")
        evac = [sem("evac0"), sem("evac1")]
        held = sem("held")

        def wait(eng, s, v):
            eng.wait_ge(s, v)
            if not isinstance(v, int):
                eng.sem_inc(held, 1)

        class Seq:

            def __init__(self, eng, name, base=0):
                self.eng, self.s, self.n, self.base = eng, sem(name), 0, base

            def loop(self, i, per, start):
                self.base, self.n = start + per * i, 0

            def do(self, ins):
                self.n += 1
                ins.then_inc(self.s, 1)
                wait(self.eng, self.s, self.base + self.n)

        def load_w(sp, n, half, src, width=P):
            slot = half[1]
            wait(sp, w_split, n + 1)
            nc.sync.dma_start(RAW[:, slot, :, 0:width], src).then_inc(w_landed[slot], 16)

        def split_hi(act, n, half):
            h, slot = half
            wait(act, w_landed[slot], 16 * h + 16)
            wait(act, mm_done, n + 1)
            nc.scalar.copy(WH[:, slot], RAW[:, slot]).then_inc(w_hi, 1)

        def split_lo(dve, n, half):
            slot = half[1]
            wait(dve, w_hi, n + 1)
            nc.vector.tensor_tensor(WL[:, slot], RAW[:, slot], WH[:, slot].bitcast(F32),
                                    ALU.subtract).then_inc(w_split, 1)

        def main(pe, n, half, between=None):
            h, slot = half
            wait(pe, w_split, n + 3)
            wait(pe, evac[slot], h + 1)
            for k in range(KT):
                for q, (w_, x_) in enumerate(((WH, HH), (WH, HL), (WL, HH))):
                    for b in range(2):
                        ins = nc.tensor.matmul(MP[:, slot, b, 0:HALF], w_[:, slot, k, :],
                                               x_[:, k, b * HALF:(b + 1) * HALF],
                                               start=(k == 0 and q == 0), stop=(k == KT - 1 and q == 2))
                if k == KT - 1:
                    ins.then_inc(mm_done, 1)
                if between:
                    between(k)

        Z_FIRST = 4
        VALS_LANDED = 16 * (20 * NS - PAGES // 2)
        HALF_QUADS = [(0, 6), (6, 11), (11, 16)]

        def quads_of(c, kv):
            return [u // 2 for u in range(*HALF_QUADS[c % 3]) if u % 2 == kv]

        def tile_no(n0, per, i, c):
            return n0 + per * i + c, ((n0 + c) // 2 + (per // 2) * i, (n0 + c) % 2)

        def mp(slot):
            return MP[:, slot, :, 0:HALF]

        def two(ap):
            return ap.rearrange("p (b t) -> p b t", b=2)

        w_even = I["w_in_even"].rearrange("(k p) n -> p k n", p=P)
        w_eout = I["w_out_even"].rearrange("(k p) n -> p k n", p=P)
        w_odd = I["w_in_odd"].rearrange("(k p) n -> p k n", p=P)
        w_oout = I["w_out_odd"].rearrange("(k p) n -> p k n", p=P)

        EV = [("v", 0), ("u", 0), ("za", 0), ("v", 1), ("u", 1), ("za", 1), ("p", 0), ("p", 1), ("zb", 0), ("zb", 1)]
        EV_COL = {"u": 0, "v": 1024, "za": 2048, "p": 3072, "zb": 4096}
        KVT = [("k", 2048, 0), ("k", 3072, 1), ("k", 4096, 2), ("v", 2560, 0), ("v", 3584, 1), ("v", 4608, 2)]
        kv_p = [O.get(b + "_kv_prompt") for b in ("cmp", "sel", "win")]
        kv_s = [O.get(b + "_kv_sample") for b in ("cmp", "sel", "win")]
        QKV_Z, QKV_G = 5168, 5120

        def cst(name):
            a, n_ = CONSTS[name]
            return I["consts"][:, a:a + n_]

        block = ctx.enter_context(nc.Block())

        def pad5(bank):
            return X[:, bank:bank + 2, :].rearrange("p b n -> p (b n)")[:, 0:TP].rearrange("p (j d) -> p j d", d=P)

        def over(ap, n):
            return ap.unsqueeze(2).to_broadcast([ap.shape[0], ap.shape[1], n])

        def window_half(queue, smp, dst, col0, s_):
            cols = slice(col0, col0 + 512)
            win = I["state_win_kv"][bass.ds(smp, 1), :, cols].rearrange("a (p j) c -> p (a j) c", j=4)
            queue.dma_start(dst[1:P], win[1:P]).then_inc(s_, 16)
            queue.dma_start(dst[0:1, 1:4], win[0:1, 1:4]).then_inc(s_, 16)
            queue.dma_start(dst[0:1, 0, :], O["win_kv_sample"][bass.ds(smp, 1), 511, cols]).then_inc(s_, 16)

        def page_at(queue, cache, idx):
            pg = queue.value_load(PTAB[0:1, idx:idx + 1] if isinstance(idx, int) else PTAB[0:1, bass.ds(idx, 1)],
                                  min_val=0, max_val=NPHYS - 1)
            return I[cache][bass.ds(pg, 1)].rearrange("a t c -> t (a c)")

        def act_tile(idx):
            if isinstance(idx, int):
                return A[:, idx, :]
            return A[:, bass.ds(idx, 1), :].rearrange("p a t -> p (a t)")

        @block.sync
        def _(sp):
            nc.sync.dma_start(ident[:], cst("ident")).then_inc(sem("ident_landed"), 16)
            xp = I["x_prompt"].rearrange("(j p) d -> j p d", p=P)
            for j in range(2):
                nc.sync.dma_start(XS[:, j], xp[j]).then_inc(sem(f"x_landed{j}"), 16)
            for j in range(2, 5):
                sp.wait_ge(sem("x_turned"), 4 * (j - 1))
                if j < 4:
                    nc.sync.dma_start(XS[:, j % 2], xp[j]).then_inc(sem(f"x_landed{j % 2}"), 16)
                else:
                    nc.sync.dma_start(XS[0:NS, 0], I["x_sample"]).then_inc(sem("x_landed0"), 16)
            with sp.Fori(0, PG) as i:
                for c, (kind, e) in enumerate(EV):
                    n, half = tile_no(N_EVEN_IN, 10, i, c)
                    col = nc.sync.snap(EV_COL[kind] + (2 * i + e) * P, min_val=0, max_val=4992)
                    load_w(sp, n, half, w_even[:, :, bass.ds(col, P)])
            sp.wait_ge(sem("xT_out"), 16)
            with sp.Fori(0, 8) as i:
                for c in range(2):
                    n, half = tile_no(N_EVEN_OUT, 2, i, c)
                    col = nc.sync.snap((2 * i + c) * P, min_val=0, max_val=D - P)
                    kt = nc.sync.snap(2 * i + c, min_val=0, max_val=KT - 1)
                    load_w(sp, n, half, w_eout[:, :, bass.ds(col, P)])
                    wait(sp, evac[c], half[0] + 1)
                    nc.sync.dma_start(XR[:, c], xT_scr[bass.ds(kt, 1)].rearrange("a p t -> p (a t)")).then_inc(
                        sem(f"res_landed{c}"), 16)
            with sp.Fori(0, KV) as i:
                for c, (kind, col0, br) in enumerate(KVT):
                    n, half = tile_no(N_KV, 6, i, c)
                    col = nc.sync.snap(col0 + i * P, min_val=0, max_val=7216 - P)
                    load_w(sp, n, half, w_odd[:, :, bass.ds(col, P)])
                    if c in (1, 4):
                        smp = nc.sync.snap(2 * i + c // 4, min_val=0, max_val=NS - 1)
                        nc.sync.dma_start(O["win_kv_sample"][bass.ds(smp, 1), 0:511, :].rearrange("a r c -> a (r c)"),
                                          I["state_win_kv"][bass.ds(smp, 1), 1:512, :].rearrange("a r c -> a (r c)")
                                          ).then_inc(sem("win_moved"), 16)
            with sp.Fori(0, KV) as i:
                for c in range(REP):
                    n, half = tile_no(N_Q, REP, i, c)
                    col = nc.sync.snap((4 * i + c) * P, min_val=0, max_val=7216 - P)
                    load_w(sp, n, half, w_odd[:, :, bass.ds(col, P)])

            def load_z(t_):
                if t_ < HEADS:
                    load_w(sp, N_Z + t_, ((N_Z + t_) // 2, t_ % 2), w_odd[:, :, QKV_Z + t_ * P:QKV_Z + (t_ + 1) * P])
                elif t_ == HEADS:
                    load_w(sp, N_GATE, (N_GATE // 2, 0), w_odd[:, :, QKV_G:QKV_G + 48], 48)

            sp.wait_ge(sem("lo_done"), 3 * KT)
            nc.sync.dma_start(PTAB[:], I["page_table"]).then_inc(sem("table_landed"), 16)
            nc.sync.dma_start(BM[:].rearrange("p c n -> p (c n)"), cst("page_blocks")).then_inc(
                sem("cmp_consts"), 16)
            for t_ in range(Z_FIRST + 2):
                load_z(t_)
            sp.wait_ge(sem("table_landed"), 16)
            sp.wait_ge(sem("back_used"), 29)
            for t_ in range(12):
                load_z(Z_FIRST + t_ + 2)
                for c in quads_of(t_, 0):
                    quarter = t_ // 3
                    sp.wait_ge(sem("pages_used"), 16 * quarter + 2 * c + 1)
                    for s4 in range(4):
                        at_ = 64 * (quarter // 2) + 16 * s4 + 8 * (quarter % 2) + c
                        nc.sync.dma_start(PGT[c % 2][:, 0, s4], page_at(nc.sync, "cache_cmp_kv", at_)[:, 0:512]
                                          ).then_inc(sem(f"keys_landed{c % 2}"), 16)

            sp.wait_ge(mm_done, N_GATE + 3)
            sp.wait_ge(sem("means_out"), 16 * 8 + 16)
            nc.sync.dma_start(KMS[:], means_scr.rearrange("q p n -> p q n")).then_inc(sem("means_landed"), 16)
            for dst, name in ((GROWS[:].rearrange("p s n -> p (s n)"), "imp_rows"),
                              (GSPR[:].rearrange("p s n -> p (s n)"), "imp_spread"), (BEF[:], "before")):
                nc.sync.dma_start(dst, cst(name)).then_inc(sem("cmp_consts"), 16)

            for b in range(2):
                sp.wait_ge(sem(f"rows_out{b}"), 32 * 12 + 32)

            def key_loads(i, first):
                if not first:
                    wait(sp, sem("k_turned"), 20 * i - 15)
                    wait(sp, sem("new_turned"), i)
                smp = i if first else nc.sync.snap(i, min_val=0, max_val=NS - 1)
                nc.sync.dma_start(NRK[:], O["sel_kv_sample"][bass.ds(smp, 1), 0:512]).then_inc(sem("win_landed"), 16)
                window_half(nc.sync, smp, KWK, 0, sem("win_landed"))
                for j in range(PAGES):
                    page = page_at(nc.sync, "cache_sel_kv", PAGES * i + j)
                    if j >= 8:
                        wait(sp, sem("k_turned"), 20 * i + j - 2)
                    elif not first:
                        wait(sp, sem("k_turned"), 20 * i + j - 6)
                    nc.sync.dma_start(SK[:, j % 8], page[:, 0:512]).then_inc(sem(f"sk_landed{j % 8}"), 16)

            key_loads(0, True)
            with sp.Fori(1, NS) as i:
                key_loads(i, False)
            for j in range(PAGES // 2, PAGES):
                if j % 4 == 0:
                    sp.wait_ge(sem("pv_done"), 4 * (NS - 1) + j // 4 + 1)
                page = page_at(nc.sync, "cache_sel_kv", PAGES * (NS - 1) + j)
                nc.sync.dma_start(SV[:, j], page[:, 512:1024]).then_inc(sem("win_landed"), 16)

            sp.wait_ge(sem("os_done"), NS + 1)
            for dst, name in ((COK[:], "cmp_ok"), (CBI[:], "cmp_bias")):
                nc.sync.dma_start(dst.rearrange("p j e n -> p (j e n)"), cst(name)).then_inc(sem("attn_consts"), 16)
            nc.sync.dma_start(CAU[:], cst("causal")).then_inc(sem("attn_consts"), 16)
            sp.wait_ge(sem("z_out"), 16 * HEADS + 16)
            with sp.Fori(0, KV) as i:
                for e in range(REP):
                    head = nc.sync.snap(4 * i + e, min_val=0, max_val=HEADS - 1)
                    wait(sp, sem("o_used"), 4 * i + e + 1)
                    nc.sync.dma_start(SZH[:, e % 2], szT_scr[bass.ds(head, 1)].rearrange("a p t -> p (a t)")).then_inc(
                        sem(f"sz_landed{e % 2}"), 16)

            sp.wait_ge(sem("x1_out"), 256)
            with sp.Fori(0, 8) as i:
                for c in range(2):
                    n, half = tile_no(N_ODD_OUT, 2, i, c)
                    h, slot = half
                    col = nc.sync.snap((2 * i + c) * P, min_val=0, max_val=D - P)
                    kt = nc.sync.snap(2 * i + c, min_val=0, max_val=KT - 1)
                    load_w(sp, n, half, w_oout[:, :, bass.ds(col, P)])
                    wait(sp, evac[slot], h + 1)
                    nc.sync.dma_start(XR[:, slot], x1_scr[bass.ds(kt, 1)].rearrange("a p t -> p (a t)")).then_inc(
                        sem(f"res_landed{slot}"), 16)
            for b in range(2):
                sp.wait_ge(sem(f"y_out{b}"), 32 * 8 + 32)
            sp.wait_ge(sem("win_moved"), 16 * NS)
            sp.wait_ge(sem("gv_out"), 16 + 16 * AH)
            sp.wait_ge(sem("tail_out"), 32 + 32 * AH)

        def norm_act(act, r):
            for k in range(KT if r == 0 else 0):
                if k >= 2:
                    act.wait_ge(sem("norm_summed"), k - 1)
                nc.scalar.activation(SQ[:, k % 2], A[:, k, :], ACT.Square).then_inc(sem("norm_sq"), 1)
            act.wait_ge(sem("norm_summed"), KT * (r + 1))
            nc.scalar.activation(two(RS[:]), X[:, 2:4, 0:HALF], ACT.Sqrt, bias=eps_t[:, 0:1],
                                 scale=1.0 / D).then_inc(sem("norm_root"), 1)
            if r == 0:
                split_hi(act, 0, (0, 0))
            for k in range(KT):
                act.wait_ge(sem("norm_scaled"), KT * r + k + 1)
                nc.scalar.copy(HH[:, k], TM[:, k % 2]).then_inc(sem("hi_done"), 1)

        def norm_dve(dve, r, gain, q):
            dve.wait_ge(sem("norm_root"), r + 1)
            nc.vector.reciprocal(RS[:], RS[:]).then_inc(sem("norm_rstd"), 1)
            dve.wait_ge(sem("norm_rstd"), r + 1)

            def scaled(k):
                if k >= 2:
                    dve.wait_ge(sem("lo_done"), KT * q + k - 1)
                nc.vector.scalar_tensor_tensor(out=TM[:, k % 2], in0=A[:, k, :], scalar=gain[:, k:k + 1],
                                               in1=RS[:], op0=ALU.mult, op1=ALU.mult).then_inc(sem("norm_scaled"), 1)

            scaled(0)
            for k in range(KT):
                if k + 1 < KT:
                    scaled(k + 1)
                dve.wait_ge(sem("norm_scaled"), KT * r + k + 1)
                dve.wait_ge(sem("hi_done"), KT * q + k + 1)
                nc.vector.tensor_tensor(HL[:, k], TM[:, k % 2], HH[:, k].bitcast(F32),
                                        ALU.subtract).then_inc(sem("lo_done"), 1)
                if r == 0 and k == 2:
                    split_lo(dve, 0, (0, 0))

        def norm_pe(pe, r):
            for k in range(KT):
                sum_squares(pe, r, k, k % 2, k == 0, k == KT - 1)

        def sum_squares(pe, r, k, slot, start, stop):
            wait(pe, sem("norm_sq"), KT * r + k + 1)
            for b in range(2):
                ins = nc.tensor.matmul(X[:, 2 + b, 0:HALF], ones[:], SQ[:, slot, b * HALF:(b + 1) * HALF],
                                       start=start, stop=stop)
            ins.then_inc(sem("norm_summed"), 1)

        def split_act_act(act, q):
            for k in range(KT):
                nc.scalar.copy(HH[:, k], A[:, k, :]).then_inc(sem("hi_done"), 1)

        def split_act_dve(dve, q):
            for k in range(KT):
                dve.wait_ge(sem("hi_done"), KT * q + k + 1)
                nc.vector.tensor_tensor(HL[:, k], A[:, k, :], HH[:, k].bitcast(F32),
                                        ALU.subtract).then_inc(sem("lo_done"), 1)

        @block.tensor
        def _(pe):
            pe.sem_inc(mm_done, 2)
            pe.sem_inc(sem("v_turned"), 1)
            pe.sem_inc(sem("s_ready"), 1)
            pe.sem_inc(sem("y_ready"), 1)
            pe.sem_inc(sem("tail_turned"), 2)

            def main_split(pe, n, half, q):
                h, slot = half
                wait(pe, w_split, n + 3)
                wait(pe, evac[slot], h + 1)
                for k in range(KT):
                    pe.wait_ge(sem("lo_done"), KT * q + k + 1)
                    for qq, (w_, x_) in enumerate(((WH, HH), (WH, HL), (WL, HH))):
                        for b in range(2):
                            ins = nc.tensor.matmul(MP[:, slot, b, 0:HALF], w_[:, slot, k, :],
                                                   x_[:, k, b * HALF:(b + 1) * HALF],
                                                   start=(k == 0 and qq == 0), stop=(k == KT - 1 and qq == 2))
                ins.then_inc(mm_done, 1)

            x_ev = [sem("x_evac0"), sem("x_evac1")]
            pe.wait_ge(sem("ident_landed"), 16)
            for j in range(4):
                pe.wait_ge(sem(f"x_landed{j % 2}"), 16 * (j // 2) + 16)
                for c in range(4):
                    q = 4 * j + c
                    if q >= 4:
                        pe.wait_ge(x_ev[q % 2], (q - 4) // 2 + 1)
                    for kk in range(4):
                        ins = nc.tensor.transpose(X[:, q % 4, kk * P:(kk + 1) * P],
                                                  XS[:, j % 2, (4 * c + kk) * P:(4 * c + kk + 1) * P], ident[:])
                    ins.then_inc(sem("x_turned"), 1)
            pe.wait_ge(sem("x_landed0"), 48)
            pe.wait_ge(x_ev[0], 7)
            for k in range(KT):
                ins = nc.tensor.transpose(X[:, 0, k * NS:(k + 1) * NS], XS[0:NS, 0, k * P:(k + 1) * P],
                                          ident[0:NS, 0:NS])
            ins.then_inc(sem("x_turned"), 1)
            pe.wait_ge(sem("raw_landed"), 32)
            for b in range(2):
                pe.wait_ge(x_ev[1 - b], 7 + b)
                for t_ in range(4):
                    ins = nc.tensor.transpose(X[:, 1 + b, t_ * 120:(t_ + 1) * 120],
                                              STR[:, (4 * b + t_) * P:(4 * b + t_ + 1) * P], ident[0:120, 0:120])
                ins.then_inc(sem("x_turned"), 1)
            pe.wait_ge(sem("raw_landed"), 32)
            for b in range(2):
                pe.wait_ge(x_ev[1 - b], 8 + b)
                for t_ in range(4):
                    ins = nc.tensor.transpose(X[:, 3 * (1 - b), t_ * P:(t_ + 1) * P], WSR[:, 4 * b + t_, :], ident[:])
                ins.then_inc(sem("x_turned"), 1)
            pe.wait_ge(sem("setup"), SETUP)
            pe.wait_ge(x_ev[0], 12)
            norm_pe(pe, 0)
            pe.wait_ge(sem("diag_ready"), 1)

            def turn_v(i, e):
                n, (h, slot) = tile_no(N_EVEN_IN, 10, i, 3 * e)
                wait(pe, evac[slot], h + 2)
                if e == 0:
                    wait(pe, sem("tail_copied"), 2 * i + 1)
                else:
                    wait(pe, sem("v_mul"), 2 * i + 1)
                pe.wait_ge(sem("pads"), 5)
                for j in range(5):
                    ins = nc.tensor.transpose(pad5(0)[:, j, :], VT[:, j * P:(j + 1) * P], ident[:])
                ins.then_inc(sem("v_turned"), 1)

            def spatial(i, e):
                wait(pe, sem("v_ready"), 2 * i + e + 1)
                if e == 0:
                    wait(pe, sem("y_used"), 2 * i + 1)
                else:
                    wait(pe, sem("s_used"), 2 * i + 1)
                wst = WST[:, bass.ds(2 * i + e, 1), :].rearrange("p a t -> p (a t)")
                dg = DG[:, bass.ds(2 * i + e, 1), :].rearrange("p a t -> p (a t)")
                for j in range(TT):
                    nc.tensor.matmul(X[:, 2, j * P:(j + 1) * P], VN[:, j, :], wst, start=True, stop=True)
                nc.tensor.matmul(X[:, 3, 0:NS], VN[:, 4, :], dg, start=True, stop=True).then_inc(sem("s_ready"), 1)

            def turn_tail(i, e):
                n, (h, slot) = tile_no(N_EVEN_IN, 10, i, 6 + e)
                wait(pe, evac[slot], h + 2)
                if e == 0:
                    wait(pe, sem("v_mul"), 2 * i + 2)
                else:
                    wait(pe, sem("tail_copied"), 2 * i + 2)
                nc.tensor.transpose(X[0:PAD, 0, 0:P], EX[e][:, SEQ:SEQ + PAD], ident[:])
                nc.tensor.transpose(X[0:NS, 1, 0:P], EX[e][:, PAD + SEQ + 15::16], ident[:]).then_inc(
                    sem("tail_turned"), 1)

            def pool_y(i, e):
                wait(pe, sem("pool_d"), 2 * i + 4)
                wait(pe, sem("group_ready"), 3 * i + 3)
                if e == 0:
                    wait(pe, sem("s_used"), 2 * i + 2)
                else:
                    wait(pe, sem("y_used"), 2 * i + 2)
                for b in range(2):
                    for c in range(2):
                        ins = nc.tensor.matmul(X[:, 2 + b, 0:HALF], WPG[:, c, e * P:(e + 1) * P],
                                               PD[:, c, b * HALF:(b + 1) * HALF], start=(c == 0), stop=(c == 1))
                ins.then_inc(sem("y_ready"), 1)

            with pe.Fori(0, PG) as i:
                for c, (kind, e) in enumerate(EV):
                    n, half = tile_no(N_EVEN_IN, 10, i, c)
                    if c == 0:
                        main_split(pe, n, half, 0)
                    else:
                        main(pe, n, half)
                    if kind == "u":
                        turn_v(i, e)
                    if kind == "za":
                        spatial(i, e)
                    if c == 7:
                        turn_tail(i, 0)
                    if c == 8:
                        turn_tail(i, 1)
                        pool_y(i, 0)
                    if c == 9:
                        pool_y(i, 1)
            def out_even(i, first):
                for c in range(2):
                    n, half = tile_no(N_EVEN_OUT, 2, i, c)
                    if first and c == 0:
                        pe.wait_ge(sem("y_used"), 9)
                        main_split(pe, n, half, 1)
                    else:
                        main(pe, n, half)
                        if first:
                            sum_squares(pe, 1, 0, 0, True, False)
                        else:
                            sum_squares(pe, 1, 2 * i + c - 1, 1 - c, False, False)

            out_even(0, True)
            with pe.Fori(1, 8) as i:
                out_even(i, False)
            sum_squares(pe, 1, KT - 1, 1, False, True)

            pe.sem_inc(sem("head_turned"), 2)
            pe.wait_ge(sem("tail_copied"), 9)

            def turn_head(i, m, n, h, slot):
                wait(pe, evac[slot], h + 2)
                wait(pe, sem("rows_read"), m + 1)
                pe.wait_ge(sem("head_pads"), 4)
                for j in range(5):
                    ins = nc.tensor.transpose(pad5(0)[:, j, :], KTT[:, slot, j * P:(j + 1) * P], ident[:])
                ins.then_inc(sem("head_turned"), 1)

            def turn_back(kq, slot, tiles):
                wait(pe, sem("rows_ready"), kq + 1)
                wait(pe, sem("back_used"), kq + 1)
                for j in range(tiles):
                    ins = nc.tensor.transpose(pad5(2)[:, j, :], KN[:, slot, j, :], ident[:])
                ins.then_inc(sem("back_turned"), 1)

            with pe.Fori(0, KV) as i:
                for c, (kind, col0, br) in enumerate(KVT):
                    n, half = tile_no(N_KV, 6, i, c)
                    if c == 0:
                        main_split(pe, n, half, 2)
                    else:
                        main(pe, n, half)
                    for t_ in ([c - 1, 5] if c == 5 else [c - 1] if c else []):
                        m_n, (mh, ms) = tile_no(N_KV, 6, i, t_)
                        turn_head(i, 6 * i + t_, m_n, mh, ms)
                        if t_ == 4:
                            wait(pe, sem("vc_rows"), i + 1)
                            wait(pe, sem("vm_used"), i + 1)
                            for j in range(TT):
                                ins = nc.tensor.matmul(X[:, 3, 0:P], VMASK[:, j, :], KN[:, 1, j, :],
                                                       start=(j == 0), stop=(j == TT - 1))
                            ins.then_inc(sem("vm_done"), 1)
                    if 2 <= c <= 4:
                        turn_back(3 * i + c - 2, (c - 2) % 2, TT)
            def q_turns(i, c, head, back):
                if head:
                    m_n, (mh, ms) = tile_no(N_Q, REP, i, c - 1)
                    turn_head(i, 24 + 4 * i + c - 1, m_n, mh, ms)
                if back:
                    turn_back(12 + 4 * i + c - 2, c % 2, 5)

            def q_pass(i, first):
                for c in range(REP):
                    n, half = tile_no(N_Q, REP, i, c)
                    main(pe, n, half)
                    q_turns(i, c, not first or c >= 1, not first or c >= 2)

            q_pass(0, True)
            with pe.Fori(1, KV) as i:
                q_pass(i, False)
            for t_ in range(Z_FIRST):
                n = N_Z + t_
                main(pe, n, (n // 2, n % 2))
                q_turns(KV, t_, t_ == 0, t_ <= 1)
            pe.wait_ge(sem("cmp_consts"), 16)
            pe.wait_ge(sem("back_used"), 29)
            pe.sem_inc(sem("pages_used"), 4)
            with pe.Fori(0, 2) as r:
                def page_sums(hf, u):
                    c, kv = u // 2, u % 2
                    if u == 0:
                        wait(pe, sem("means_used_a" if hf == 0 else "means_used_b"), r + 1)
                    wait(pe, sem(f"values_landed{c % 2}" if kv else f"keys_landed{c % 2}"),
                         512 * r + 256 * hf + 64 * (c // 2) + 64)
                    for s4 in range(4):
                        ins = nc.tensor.matmul(X[32 * s4:32 * s4 + 32, 2 * hf + kv, :], BM[:, c, :],
                                               PGT[c % 2][:, kv, s4, :], start=(c == 0), stop=(c == 7))
                    ins.then_inc(sem("pages_used"), 1)

                for c in range(6):
                    n, half = tile_no(N_Z + Z_FIRST, 6, r, c)
                    lo, hi = HALF_QUADS[c % 3]

                    def between(k):
                        for u in range(lo, hi):
                            if (u - lo + 1) * KT // (hi - lo) - 1 == k:
                                page_sums(c // 3, u)

                    main(pe, n, half, between)
            main(pe, N_GATE, (N_GATE // 2, 0))
            pe.wait_ge(evac[0], N_GATE // 2 + 2)
            pe.wait_ge(sem("rows_read"), 41)
            pe.wait_ge(sem("means_used_a"), 3)
            pe.wait_ge(sem("means_used_b"), 3)
            for j in range(TT):
                nc.tensor.transpose(X[:, 0, j * P:(j + 1) * P], GTT[:, j * P:(j + 1) * P], ident[:])
            nc.tensor.transpose(X[0:NS, 1, 0:P], GTT[:, SEQ:T], ident[:]).then_inc(sem("gates_turned"), 1)
            pe.wait_ge(sem("gate8_ready"), 3)
            for b in range(3):
                ins = nc.tensor.transpose(X[:, 1, P + b * NS:P + (b + 1) * NS], G8[:, b, :], ident[0:NS, 0:NS])
            ins.then_inc(sem("gates_turned"), 1)

            pe.wait_ge(sem("cmp_consts"), 64)
            pe.wait_ge(sem("gates_copied"), 2)
            pe.wait_ge(sem("means_landed"), 16)
            for it in range(4):
                for g in range(KV):
                    ins = nc.tensor.transpose(X[:, it, g * P:(g + 1) * P], KMS[:, it, g * P:(g + 1) * P], ident[:])
                ins.then_inc(sem("km_turned"), 1)
            pe.wait_ge(sem("kmt_ready"), 4)
            pe.wait_ge(sem("qp_ready"), 1)
            for s_ in range(NS):
                for g in range(KV):
                    ins = nc.tensor.matmul(X[32 * g:32 * g + 32, 0, s_ * 32:(s_ + 1) * 32], QP[:, s_, g, :],
                                           KMT[:, g, s_, :], start=True, stop=True)
            ins.then_inc(sem("cs_done"), 1)
            pe.wait_ge(sem("cp_ready"), 1)
            for s_ in range(NS):
                ins = nc.tensor.matmul(X[0:32, 1, 0:32], GROWS[:, s_, :], CE[:, s_, :], start=(s_ == 0),
                                       stop=(s_ == NS - 1))
            ins.then_inc(sem("imp_done"), 1)
            pe.wait_ge(sem("cpad_ready"), 5)
            for it in range(4):
                ins = nc.tensor.transpose(X[:, 2, it * P:(it + 1) * P], CP[:, it].rearrange("p s n -> p (s n)"),
                                          ident[:])
            ins.then_inc(sem("cpt_turned"), 1)
            pe.wait_ge(sem("cpt_ready"), 1)
            pe.wait_ge(sem("imp_copied"), 1)
            for s4 in range(4):
                for r in range(2):
                    for g in range(KV):
                        for hf in range(2):
                            ins = nc.tensor.matmul(
                                X[32 * g:32 * g + 32, s4, r * P:(r + 1) * P],
                                CPT[32 * s4:32 * s4 + 32, 2 * r + hf, 32 * g:32 * g + 32],
                                KMS[32 * s4:32 * s4 + 32, 2 * r + hf, 512 + g * P:512 + (g + 1) * P],
                                start=(hf == 0), stop=(hf == 1))
            ins.then_inc(sem("oc_done"), 1)
            pe.wait_ge(sem("low_ready"), 1)
            pe.wait_ge(sem("oc_ready"), 4)
            for s_ in range(NS):
                ins = nc.tensor.matmul(X[:, 0, s_ * 32:(s_ + 1) * 32], GSPR[0:32, s_, :], LOW[:], start=True,
                                       stop=True)
            ins.then_inc(sem("low_spread"), 1)

            pe.wait_ge(sem("bias_ready"), 1)
            pe.sem_inc(sem("k_turned"), 1)
            pe.sem_inc(sem("sc_done"), 1)
            pe.sem_inc(sem("pv_done"), 4)
            pe.sem_inc(sem("new_scored"), 1)
            new = MP[:, 0, 1, :]

            def sample_scores(i):
                def turn_k(t_):
                    if t_ >= 4:
                        j = t_ - 4
                        wait(pe, sem(f"sk_landed{j % 8}"), 32 * i + 16 * (j // 8) + 16)
                    wait(pe, sem("k_evac"), 20 * i + t_ + 1)
                    src = KWK[:, t_] if t_ < 4 else SK[:, (t_ - 4) % 8]
                    for g in range(KV):
                        ins = nc.tensor.transpose(X[:, t_ % 2, g * P:(g + 1) * P], src[:, g * P:(g + 1) * P],
                                                  ident[:])
                    ins.then_inc(sem("k_turned"), 1)

                def score_block(b):
                    wait(pe, sem("k_evac"), 20 * i + 4 * b + 6)
                    if b == 2:
                        wait(pe, sem("win_exp"), i + 1)
                    else:
                        wait(pe, sem("sel_read"), 4 * i + 4 if b < 2 else 4 * i + 2 + b)
                    for g in range(KV):
                        ins = nc.tensor.matmul(X[32 * g:32 * g + 32, 2 + b % 2, :], QS[:, g, :],
                                               SKT[:, b % 2, g, :], start=True, stop=True)
                    ins.then_inc(sem("sc_done"), 1)

                wait(pe, sem("win_landed"), 64 * i + 64)
                for t_ in range(20):
                    turn_k(t_)
                    if t_ == 3:
                        if not isinstance(i, int):
                            wait(pe, sem("os_done"), i)
                            wait(pe, sem("p_evac"), 6 * i)
                        for g in range(KV):
                            ins = nc.tensor.transpose(new[:, g:g + 1], NRK[0:1, g * P:(g + 1) * P], ident[0:1, 0:1])
                        ins.then_inc(sem("new_turned"), 1)
                    if t_ == 5:
                        wait(pe, sem("q_static"), i + 1)
                        wait(pe, sem("new_evac"), i + 1)
                        for g in range(KV):
                            ins = nc.tensor.matmul(MP[32 * g:32 * g + 32, 0, 1, 8:9], QS[:, g, :], KNT[:, g:g + 1],
                                                   start=True, stop=True)
                        ins.then_inc(sem("new_scored"), 1)
                    if t_ % 4 == 1 and t_ > 4:
                        score_block(t_ // 4 - 1)
                score_block(4)

            def sample_values(i):
                if isinstance(i, int):
                    pe.wait_ge(sem("vals_landed"), VALS_LANDED)
                    pe.wait_ge(sem("win_landed"), 64 * NS + 16 * PAGES // 2)
                else:
                    wait(pe, sem("vals_landed"), 320 * i)
                wait(pe, sem("p_evac"), 6 * i)
                wait(pe, sem("o_rows"), i)
                for j in range(PAGES):
                    for g in range(KV):
                        ins = nc.tensor.matmul(MP[32 * g:32 * g + 32, 0, 0, 0:P], SPT[:, j, 32 * g:32 * g + 32],
                                         SV[:, j, g * P:(g + 1) * P], start=(j == 0), stop=False)
                    if j % 4 == 3 and j < PAGES - 1:
                        ins.then_inc(sem("pv_done"), 1)
                for g in range(KV):
                    nc.tensor.matmul(MP[32 * g:32 * g + 32, 0, 0, 0:P], SPT[0:1, PAGES, 32 * g:32 * g + 32],
                                     NRV[0:1, g * P:(g + 1) * P], start=False, stop=True)
                for t_ in range(4):
                    for g in range(KV):
                        ins = nc.tensor.matmul(MP[32 * g:32 * g + 32, 0, 0, P:2 * P],
                                               WPT[:, t_, 32 * g:32 * g + 32], KWV[:, t_, g * P:(g + 1) * P],
                                               start=(t_ == 0), stop=(t_ == 3))
                ins.then_inc(sem("pv_done"), 1)

            def sample_probs(i):
                wait(pe, sem("win_exp"), i + 1)
                for t_ in range(4):
                    ins = nc.tensor.transpose(MP[:, 1, 0, t_ * P:(t_ + 1) * P], SWP[:, t_ * P:(t_ + 1) * P], ident[:])
                ins.then_inc(sem("p_turned"), 1)
                wait(pe, sem("sel_exp"), i + 1)
                for q in range(1, 5):
                    if q >= 2:
                        wait(pe, sem("p_evac"), 6 * i + q - 1)
                    for t_ in range(4):
                        ins = nc.tensor.transpose(MP[:, 1, q % 2, t_ * P:(t_ + 1) * P],
                                                  SC[:, (4 * q - 4 + t_) * P:(4 * q - 3 + t_) * P], ident[:])
                    ins.then_inc(sem("p_turned"), 1)
                nc.tensor.transpose(MP[0:1, 0, 1, P:2 * P], SC[:, PAGES * P:PAGES * P + 1], ident[:]).then_inc(
                    sem("p_turned"), 1)

            def sample_out(i):
                wait(pe, sem("o_rows"), i + 1)
                wait(pe, sem("p_evac"), 6 * i + (0 if isinstance(i, int) else 6))
                nc.tensor.transpose(new[:, 2 * P:3 * P], OSM[:, 1, :], ident[:]).then_inc(sem("o_turned"), 1)

            sample_scores(0)
            sample_probs(0)
            with pe.Fori(1, NS) as i:
                sample_scores(i)
                sample_values(i)
                sample_probs(i)
                sample_out(i)
            sample_values(NS)
            sample_out(NS)

            pe.wait_ge(sem("os_done"), NS + 1)
            pe.wait_ge(sem("attn_ready"), 2)
            pe.sem_inc(sem("p4_turned"), 4)
            pe.sem_inc(sem("pv4"), 2)
            pe.sem_inc(sem("o_done"), 1)

            def unit(w):
                return w // 8, (w // 4) % 2, w % 4

            with pe.Fori(0, KV) as i:
                def score(w):
                    e, br, j = unit(w)
                    wait(pe, sem("p4_exp"), 32 * i + w + 1)
                    nc.tensor.matmul(X[:, w % 4, 0:(j + 1) * P], QC[:, e, j * P:(j + 1) * P],
                                     KTS[:, br, bass.ds(i, 1), 0:(j + 1) * P].rearrange("p a t -> p (a t)"),
                                     start=True, stop=False)
                    nc.tensor.matmul(X[:, w % 4, j * P:(j + 1) * P], IDB[:], CAB[:], start=False,
                                     stop=True).then_inc(sem("s4_done"), 1)

                cmp_bank = MP[:, 1, 1, :]

                def cmp_scores():
                    wait(pe, sem("group_static"), 2 * i + 2)
                    wait(pe, sem("qc_ready"), 4 * i + 4)
                    wait(pe, sem("o_used"), 4 * i + 2)
                    for e in range(REP):
                        ins = nc.tensor.matmul(MP[32 * e:32 * e + 32, 1, 1, :], KMG[:], QC[:, e, :], start=True,
                                               stop=True)
                    ins.then_inc(sem("c4_scored"), 1)

                def cmp_turn():
                    wait(pe, sem("c4_rows"), i + 1)
                    for j in range(TT):
                        ins = nc.tensor.transpose(cmp_bank[:, j * P:(j + 1) * P], CS[:, j * P:(j + 1) * P], ident[:])
                    ins.then_inc(sem("c4_turned"), 1)

                def cmp_turn_back():
                    wait(pe, sem("c4_probs"), i + 1)
                    for j in range(TT):
                        ins = nc.tensor.transpose(cmp_bank[:, j * P:(j + 1) * P],
                                                  CPP[:, j].rearrange("p e n -> p (e n)"), ident[:])
                    ins.then_inc(sem("c4_back"), 1)

                def values(w, m):
                    e, br, j = unit(w)
                    o_ = MP[:, 1, e % 2, :]
                    if w == 3 and m == 0:
                        wait(pe, sem("vals_landed"), VALS_LANDED + 32 * i + 32)
                    if m == 0:
                        if br == 0:
                            wait(pe, sem("o_used"), 4 * i + e + 1)
                        wait(pe, sem("pt4_evac"), 32 * i + w + 3)
                    ins = nc.tensor.matmul(o_[:, m * P:SEQ], VB[:, br, m, :], PT_[:, br, m, m * P:SEQ],
                                           start=(br == 0 and m == 0), stop=False)
                    if m == TT - 1:
                        ins.then_inc(sem("pv4"), 1)

                def finish(e):
                    if e == 0:
                        wait(pe, sem("c4_probs_t"), i + 1)
                    nc.tensor.matmul(MP[:, 1, e % 2, :], VMG[32 * e:32 * e + 32, :], CPX[32 * e:32 * e + 32, :],
                                     start=False, stop=True).then_inc(sem("o_done"), 1)

                wait(pe, sem("qc_ready"), 4 * i + 1)
                for w in range(3):
                    score(w)
                for w in range(32):
                    e, br, j = unit(w)
                    if w + 3 < 32:
                        if w + 3 == 8:
                            wait(pe, sem("qc_ready"), 4 * i + 4)
                        score(w + 3)
                    wait(pe, sem("p4_scaled"), 32 * i + w + 9)
                    wait(pe, sem("pt4_evac"), 32 * i + w + 1)
                    for m in range(j + 1):
                        ins = nc.tensor.transpose(MP[:, 0, w % 2, m * P:(m + 1) * P],
                                                  PR[:, w % 4, m * P:(m + 1) * P], ident[:])
                    ins.then_inc(sem("p4_turned"), 1)
                    if w % 8 == 4 and w >= 12:
                        finish(w // 8 - 1)
                    if w >= 4:
                        values(w // 4 * 4 - 1, w % 4)
                    if w == 3:
                        cmp_scores()
                    if w == 5:
                        cmp_turn()
                    if w == 10:
                        cmp_turn_back()
                for m in range(TT):
                    values(31, m)
                finish(3)

            pe.wait_ge(sem("o_used"), HEADS + 2)
            pe.wait_ge(sem("c4_probs_t"), KV)

            def turn_y(k, slot, n, h):
                bank = 2 * (1 - slot)
                wait(pe, evac[slot], h + 2)
                wait(pe, sem("y_read"), k + 1)
                for j in range(TT):
                    nc.tensor.transpose(pad5(bank)[:, j, :], YT[:, slot, j * P:(j + 1) * P], ident[:])
                nc.tensor.transpose(X[0:NS, bank + 1, 0:P], YT[:, slot, SEQ:T], ident[:]).then_inc(sem("y_turned"), 1)

            pe.sem_inc(sem("y_turned"), 2)

            def out_pass(i, first):
                for c in range(2):
                    n, half = tile_no(N_ODD_OUT, 2, i, c)
                    if first and c == 0:
                        main_split(pe, n, half, 3)
                    else:
                        main(pe, n, half)
                    if not (first and c == 0):
                        pn, (ph, ps_) = tile_no(N_ODD_OUT - 1, 2, i, c)
                        turn_y(2 * i + c - 1, ps_, pn, ph)

            out_pass(0, True)
            with pe.Fori(1, 8) as i:
                out_pass(i, False)
            turn_y(15, (N_ODD_OUT + 15) % 2, N_ODD_OUT + 15, (N_ODD_OUT + 15) // 2)

        @block.scalar
        def _(act):
            act.sem_inc(sem("tail_copied"), 1)
            for q in range(1, 16, 2):
                act.wait_ge(sem("x_turned"), q + 1)
                j, c = q // 4, q % 4
                nc.scalar.copy(A[:, 4 * c:4 * c + 4, j * P:(j + 1) * P],
                               X[:, q % 4, :].rearrange("p (k t) -> p k t", k=4)).then_inc(sem("x_evac1"), 1)
            act.wait_ge(sem("x_turned"), 18)
            nc.scalar.copy(STP[:, 0:4, :], X[:, 1, 0:480].rearrange("p (k t) -> p k t", k=4)).then_inc(
                sem("x_evac1"), 1)
            act.wait_ge(sem("x_evac0"), 9)
            act.wait_ge(sem("x_evac1"), 9)
            act.wait_ge(sem("setup"), SETUP)
            act.wait_ge(sem("pads"), 2)
            norm_act(act, 0)

            def evac_p(i, e, slot):
                wait(act, sem("pool_d"), 2 * i + e + 1)
                wait(act, sem("tail_turned"), 2 * i + e + 1)
                nc.scalar.copy(EX[e][:, PAD:PAD + HALF], MP[:, slot, 0, 0:HALF])
                nc.scalar.copy(EX[e][:, PAD + HALF:PAD + SEQ], MP[:, slot, 1, 0:SEQ - HALF])
                nc.scalar.copy(EX[e][:, PAD + SEQ + 15::16], MP[:, slot, 1, SEQ - HALF:HALF]).then_inc(evac[slot], 1)

            def square_v(i, e):
                wait(act, sem("v_turned"), 2 * i + e + 2)
                wait(act, sem("v_ss"), 2 * i + e + 1)
                wait(act, sem("pool_d"), 2 * i + 2)
                nc.scalar.activation(C1[:, 0:TP].rearrange("p (j d) -> p j d", d=P), pad5(0),
                                     ACT.Square).then_inc(sem("v_sq"), 1)

            def copy_tail(i, e):
                wait(act, sem("tail_turned"), 2 * i + e + 3)
                wait(act, sem("tail_out"), 32 * (2 * i + e) + 32)
                nc.scalar.copy(TLP[:], X[0:PAD, 0, 0:P]).then_inc(sem("tail_first"), 1)
                nc.scalar.copy(TLS[:], X[0:NS, 1, 0:P]).then_inc(sem("tail_copied"), 1)

            with act.Fori(0, PG) as i:
                for c, (kind, e) in enumerate(EV):
                    n, half = tile_no(N_EVEN_IN, 10, i, c)
                    nn, nhalf = tile_no(N_EVEN_IN, 10, i, c + 1)
                    slot = half[1]
                    split_hi(act, nn, nhalf)
                    wait(act, mm_done, n + 3)
                    if kind == "v":
                        wait(act, sem("v_turned"), 2 * i + e + 1)
                        nc.scalar.copy(two(VT[:, 0:T]), mp(slot)).then_inc(evac[slot], 1)
                    elif kind == "u":
                        wait(act, sem("u_used"), 2 * i + e + 1)
                        nc.scalar.copy(two(UT[:]), mp(slot)).then_inc(evac[slot], 1)
                        square_v(i, e)
                    elif kind in ("za", "zb"):
                        wait(act, sem("z_used"), 4 * i + (0 if kind == "za" else 2) + e + 1)
                        nc.scalar.activation(two(SZ[:]), mp(slot), ACT.Silu).then_inc(evac[slot], 1)
                    else:
                        evac_p(i, e, slot)
                    if c == 7:
                        copy_tail(i, 0)
                    if c == 8:
                        copy_tail(i, 1)
            act.wait_ge(sem("z_used"), 17)
            act.wait_ge(mm_done, N_EVEN_OUT + 2)
            split_act_act(act, 1)
            with act.Fori(0, 8) as i:
                for c in range(2):
                    n, half = tile_no(N_EVEN_OUT, 2, i, c + 1)
                    split_hi(act, n, half)
                    n, (h, slot) = tile_no(N_EVEN_OUT, 2, i, c)
                    wait(act, evac[slot], h + 2)
                    wait(act, sem("norm_summed"), KT + 2 * i + c - 1)
                    nc.scalar.activation(SQ[:, c], act_tile(2 * i + c), ACT.Square).then_inc(sem("norm_sq"), 1)

            act.wait_ge(evac[0], 29)
            act.wait_ge(evac[1], 29)
            norm_act(act, 1)
            act.sem_inc(sem("z_out"), 16)
            act.sem_inc(sem("back_used"), 1)

            def square_head(m, kq):
                wait(act, sem("head_turned"), m + 3)
                wait(act, sem("h_ss"), kq + 1)
                nc.scalar.activation(SQ1[:], pad5(0), ACT.Square).then_inc(sem("h_sq"), 1)

            with act.Fori(0, KV) as i:
                for c, (kind, col0, br) in enumerate(KVT):
                    n, (h, slot) = tile_no(N_KV, 6, i, c)
                    nn, nhalf = tile_no(N_KV, 6, i, c + 1)
                    split_hi(act, nn, nhalf)
                    wait(act, mm_done, n + 3)
                    wait(act, sem("head_turned"), 6 * i + c + 1)
                    act.wait_ge(sem("head_pads"), 4)
                    nc.scalar.copy(two(KTT[:, slot, 0:T]), mp(slot)).then_inc(evac[slot], 1)
                    if 1 <= c <= 3:
                        square_head(6 * i + c - 1, 3 * i + c - 1)
                    if c in (3, 4):
                        wait(act, sem("back_turned"), 3 * i + c - 1)
                        nc.scalar.copy(KTS[:, c - 3, bass.ds(i, 1), :].rearrange("p a t -> p (a t)"),
                                       X[:, 2, :]).then_inc(sem("back_used"), 1)
            act.wait_ge(sem("x1_out"), 256)
            def q_follow(i, c, head, back):
                if head:
                    square_head(24 + 4 * i + c - 1, 12 + 4 * i + c - 1)
                if back:
                    wait(act, sem("back_turned"), 12 + 4 * i + c - 1)
                    nc.scalar.copy(act_tile(4 * i + c - 2), X[:, 2:4, :].rearrange("p b n -> p (b n)")[:, 0:T]
                                   ).then_inc(sem("back_used"), 1)

            def q_act(i, first):
                for c in range(REP):
                    n, (h, slot) = tile_no(N_Q, REP, i, c)
                    nn, nhalf = tile_no(N_Q, REP, i, c + 1)
                    split_hi(act, nn, nhalf)
                    wait(act, mm_done, n + 3)
                    wait(act, sem("head_turned"), 24 + 4 * i + c + 1)
                    nc.scalar.copy(two(KTT[:, slot, 0:T]), mp(slot)).then_inc(evac[slot], 1)
                    q_follow(i, c, not first or c >= 1, not first or c >= 2)

            def z_act(t_, n, h, slot, nhalf):
                head = t_ if isinstance(t_, int) else nc.scalar.snap(t_, min_val=0, max_val=HEADS - 1)
                split_hi(act, n + 1, nhalf)
                wait(act, mm_done, n + 3)
                wait(act, sem("z_out"), 16 * t_ + 16)
                nc.scalar.activation(two(ZT[:]), mp(slot), ACT.Silu).then_inc(evac[slot], 1)
                wait(act, evac[slot], h + 2)
                nc.scalar.dma_start(szT_scr[bass.ds(head, 1)].rearrange("a p t -> p (a t)"), ZT[:]).then_inc(
                    sem("z_out"), 16)

            q_act(0, True)
            with act.Fori(1, KV) as i:
                q_act(i, False)
            for t_ in range(Z_FIRST):
                n = N_Z + t_
                z_act(t_, n, n // 2, n % 2, ((n + 1) // 2, (n + 1) % 2))
                q_follow(KV, t_, t_ == 0, t_ <= 1)
            act.sem_inc(sem("means_used_a"), 1)
            act.sem_inc(sem("means_used_b"), 1)
            act.sem_inc(sem("means_out"), 16)
            with act.Fori(0, 2) as r:
                for c in range(6):
                    n, (h, slot) = tile_no(N_Z + Z_FIRST, 6, r, c)
                    z_act(Z_FIRST + 6 * r + c, n, h, slot, tile_no(N_Z + Z_FIRST, 6, r, c + 1)[1])
                    if c % 3 == 2:
                        hf = c // 3
                        quarter = nc.scalar.snap(2 * r + hf, min_val=0, max_val=3)
                        wait(act, sem("pages_used"), 32 * r + 16 * hf + 16 + 4)
                        for kv in range(2):
                            step = 4 * r + 2 * hf + kv
                            wait(act, sem("means_out"), 16 * step + 16)
                            nc.scalar.copy(STG[:], X[:, 2 * hf + kv, :]).then_inc(sem("means_staged"), 1)
                            wait(act, sem("means_staged"), step + 1)
                            nc.scalar.dma_start(means_scr[bass.ds(quarter, 1), :, kv * 512:(kv + 1) * 512].rearrange(
                                "a p n -> p (a n)"), STG[:]).then_inc(sem("means_out"), 16)
                        act.sem_inc(sem("means_used_a" if hf == 0 else "means_used_b"), 1)
            act.wait_ge(mm_done, N_GATE + 3)
            nc.scalar.activation(two(GTT[:]), mp(0), ACT.Sigmoid).then_inc(evac[0], 1)
            act.wait_ge(sem("gates_turned"), 1)
            nc.scalar.copy(GT[:].rearrange("p j n -> p (j n)"), X[:, 0, :]).then_inc(sem("gates_copied"), 1)

            for it in range(4):
                r, hf = it // 2, it % 2
                act.wait_ge(sem("km_turned"), it + 1)
                nc.scalar.copy(KMT[:, :, 4 * r:4 * r + 4, 16 * hf:16 * hf + 16],
                               X[:, it, :].rearrange("p (g s n) -> p g s n", g=KV, s=4)[:, :, :, 0:16]).then_inc(
                    sem("kmt_ready"), 1)
            act.wait_ge(sem("cs_shifted"), 1)
            nc.scalar.activation(CE[:], CE[:], ACT.Exp).then_inc(sem("cs_exp"), 1)

            act.wait_ge(sem("bias_ready"), 1)
            act.sem_inc(sem("k_evac"), 2)

            def sample_act(i, first):
                for t_ in range(20):
                    b = t_ // 4
                    if t_ % 4 == 0:
                        wait(act, sem("sc_done"), 5 * i + 1 if b < 2 else 5 * i + b)
                    wait(act, sem("k_turned"), 20 * i + t_ + 2)
                    nc.scalar.copy(SKT[:, b % 2, :, (t_ % 4) * P:(t_ % 4 + 1) * P],
                                   X[:, t_ % 2, :].rearrange("p (g t) -> p g t", g=KV)).then_inc(sem("k_evac"), 1)
                    if t_ == 3:
                        wait(act, sem("new_scored"), i + 1)
                        wait(act, sem("new_turned"), i + 1)
                        nc.scalar.copy(KNT[:], MP[:, 0, 1, 0:KV]).then_inc(sem("new_evac"), 1)
                    if t_ == 9:
                        if not first:
                            wait(act, sem("p_turned"), 6 * i)
                        wait(act, sem("win_max"), i + 1)
                        nc.scalar.activation(SWP[:], X[:, 2, :], ACT.Exp, bias=SST[:, 0:1],
                                             accum_out=SST[:, 1:2]).then_inc(sem("win_exp"), 1)
                wait(act, sem("sel_max"), i + 1)
                nc.scalar.activation(SC[:], SC[:], ACT.Exp, bias=SST[:, 2:3], accum_out=SST[:, 3:4]).then_inc(
                    sem("sel_exp"), 1)

            sample_act(0, True)
            with act.Fori(1, NS) as i:
                sample_act(i, False)

            act.wait_ge(sem("os_done"), NS + 1)
            act.sem_inc(sem("p4_exp"), 4)
            act.sem_inc(sem("pt4_evac"), 2)
            with act.Fori(0, KV) as i:
                def exp4(w):
                    j = w % 4
                    wait(act, sem("max4"), 32 * i + w + 1)
                    wait(act, sem("p4_turned"), 32 * i + w + 1)
                    wait(act, sem("p4_scaled"), 32 * i + w + 1)
                    nc.scalar.activation(PR[:, w % 4, 0:(j + 1) * P], X[:, w % 4, 0:(j + 1) * P], ACT.Exp,
                                         bias=AMX[:, w % 8:w % 8 + 1], accum_out=ASM[:, w % 8:w % 8 + 1]).then_inc(
                        sem("p4_exp"), 1)

                exp4(0)
                exp4(1)
                for w in range(32):
                    e, br, j = w // 8, (w // 4) % 2, w % 4
                    if w + 2 < 32:
                        exp4(w + 2)
                    wait(act, sem("p4_turned"), 32 * i + w + 5)
                    if j == 0:
                        wait(act, sem("pv4"), 8 * i + 2 * e + br + 1)
                    nc.scalar.copy(PT_[:, br, 0:j + 1, j * P:(j + 1) * P],
                                   MP[:, 0, w % 2, 0:(j + 1) * P].rearrange("p (m t) -> p m t", t=P)).then_inc(
                        sem("pt4_evac"), 1)
                    if w == 7:
                        wait(act, sem("c4_shifted"), i + 1)
                        nc.scalar.activation(CX[:], CX[:], ACT.Exp).then_inc(sem("c4_exp"), 1)

            act.wait_ge(sem("o_used"), HEADS + 2)
            for b in range(2):
                act.sem_inc(sem(f"y_out{b}"), 32)
            split_hi(act, N_ODD_OUT, (N_ODD_OUT // 2, N_ODD_OUT % 2))
            split_act_act(act, 3)
            act.sem_inc(sem("y_read"), 2)
            y_p = O["y_prompt"].rearrange("(j p) c -> p j c", p=P)

            def rows_y(k, slot, uses):
                bank = 2 * (1 - slot)
                wait(act, sem("y_turned"), k + 3)
                wait(act, sem(f"y_out{slot}"), 32 * uses + 32)
                nc.scalar.copy(YS[:, slot, 0:TT, :], pad5(bank)[:, 0:TT, :]).then_inc(sem("y_rows"), 1)
                nc.scalar.copy(YS[0:NS, slot, 4, :], X[0:NS, bank + 1, 0:P]).then_inc(sem("y_read"), 1)
                col = k * P if isinstance(k, int) else nc.scalar.snap(k * P, min_val=0, max_val=D - P)
                wait(act, sem("y_rows"), k + 1)
                wait(act, sem("y_read"), k + 3)
                cols = bass.ds(col, P)
                nc.scalar.dma_start(y_p[:, :, cols], YS[:, slot, 0:TT, :]).then_inc(sem(f"y_out{slot}"), 16)
                nc.scalar.dma_start(O["y_sample"][:, cols], YS[0:NS, slot, 4, :]).then_inc(sem(f"y_out{slot}"), 16)

            def out_act(i, first, last):
                for c in range(2):
                    nn, nhalf = tile_no(N_ODD_OUT, 2, i, c + 1)
                    if not (last and c == 1):
                        split_hi(act, nn, nhalf)
                    if not (first and c == 0):
                        rows_y(2 * i + c - 1, (N_ODD_OUT + c - 1) % 2, i - 1 if c == 0 else i)

            out_act(0, True, False)
            with act.Fori(1, 7) as i:
                out_act(i, False, False)
            out_act(7, False, True)
            rows_y(15, (N_ODD_OUT + 15) % 2, 7)

        @block.vector
        def _(dve):
            dve.sem_inc(w_split, 2)
            dve.sem_inc(evac[0], 1)
            dve.sem_inc(evac[1], 1)
            for name, k in (("v_ss", 1), ("s_used", 0), ("u_used", 1), ("z_used", 1), ("y_used", 1), ("pool_d", 2),
                            ("v_mul", 0)):
                if k:
                    dve.sem_inc(sem(name), k)
            seq = Seq(dve, "dve_step")
            for q in range(0, 16, 2):
                dve.wait_ge(sem("x_turned"), q + 1)
                j, c = q // 4, q % 4
                nc.vector.tensor_copy(A[:, 4 * c:4 * c + 4, j * P:(j + 1) * P],
                                      X[:, q % 4, :].rearrange("p (k t) -> p k t", k=4)).then_inc(sem("x_evac0"), 1)
            dve.wait_ge(sem("x_turned"), 17)
            nc.vector.tensor_copy(A[:, :, SEQ:T], X[:, 0, 0:KT * NS].rearrange("p (k t) -> p k t", k=KT)).then_inc(
                sem("x_evac0"), 1)
            dve.wait_ge(sem("x_turned"), 19)
            nc.vector.tensor_copy(STP[:, 4:8, :], X[:, 2, 0:480].rearrange("p (k t) -> p k t", k=4)).then_inc(
                sem("x_evac0"), 1)
            dve.wait_ge(sem("setup"), SETUP)
            for b in range(2):
                dve.wait_ge(sem("x_turned"), 20 + b)
                nc.vector.tensor_tensor(WST[:, 4 * b:4 * b + 4, :],
                                        X[:, 3 * (1 - b), :].rearrange("p (k t) -> p k t", k=4),
                                        TRIL[:].unsqueeze(1).to_broadcast([P, 4, P]), ALU.mult).then_inc(
                    sem("x_evac0"), 1)
            nc.vector.tensor_tensor(DG[:], DI8[:].unsqueeze(1).to_broadcast([P, AH, NS]), over(W00[:], NS),
                                    ALU.mult).then_inc(sem("diag_ready"), 1)
            norm_dve(dve, 0, g_even, 0)

            def norm_v(i, e):
                wait(dve, sem("v_sq"), 2 * i + e + 1)
                nc.vector.tensor_reduce(SS[:], C1[:, 0:TP].rearrange("p (j d) -> p j d", d=P), AX.X,
                                        ALU.add).then_inc(sem("v_ss"), 1)
                wait(dve, sem("v_rstd"), 2 * i + e + 1)
                wait(dve, sem("s_ready"), 2 * i + e + 1)
                wait(dve, sem("gv_out"), 16 * (2 * i + e) + 16)
                nc.vector.tensor_tensor(VN[:], pad5(0), over(SR[:], P), ALU.mult).then_inc(sem("v_mul"), 1)

            def add_bias(i, e):
                wait(dve, sem("s_ready"), 2 * i + e + 2)
                bs = BS[:, bass.ds((2 * i + e) * P, P)]
                dst = A[:, bass.ds(2 * i + e, 1), :]
                seq.do(nc.vector.tensor_tensor(dst[:, :, 0:SEQ].rearrange("p a (j t) -> p (a j) t", j=TT),
                                               X[:, 2, :].rearrange("p (j t) -> p j t", j=TT),
                                               bs.unsqueeze(1).to_broadcast([P, TT, P]), ALU.add))
                nc.vector.tensor_tensor(dst[:, :, SEQ:T].rearrange("p a t -> p (a t)"), X[:, 3, 0:NS],
                                        BS[:, bass.ds((2 * i + e) * P, 1)].to_broadcast([P, NS]),
                                        ALU.add).then_inc(sem("s_used"), 1)
                wait(dve, sem("s_used"), 2 * i + e + 1)

            def gate_a(i, e):
                n, (h, slot) = tile_no(N_EVEN_IN, 10, i, 3 * e + 2)
                wait(dve, evac[slot], h + 2)
                nc.vector.tensor_tensor(UT[:], UT[:], SZ[:], ALU.mult).then_inc(sem("z_used"), 1)
                wait(dve, sem("z_used"), 4 * i + e + 2)
                a = act_tile(2 * i + e)
                nc.vector.tensor_tensor(a, a, UT[:], ALU.mult).then_inc(sem("u_used"), 1)

            def pool_chain(i, e):
                n, (h, slot) = tile_no(N_EVEN_IN, 10, i, 6 + e)
                wait(dve, evac[slot], h + 2)
                dve.wait_ge(sem("pads"), 5)
                wait(dve, sem("hist_ready"), 2 * i + e + 1)
                wait(dve, sem("group_ready"), 3 * i + 3)
                wait(dve, sem("y_ready"), 2 * i + 1)
                ex = EX[e]
                seq.do(nc.vector.tensor_tensor(C2[:, 1:EXT], ex[:, 1:EXT], ex[:, 0:EXT - 1], ALU.add))
                src, dst = C2, C1
                lo = 1
                for k, s_ in enumerate((2, 4, 8)):
                    a0 = lo + s_
                    seq.do(nc.vector.scalar_tensor_tensor(out=dst[:, a0:EXT], in0=src[:, a0 - s_:EXT - s_],
                                                          scalar=PARG[:, k:k + 1], in1=src[:, a0:EXT],
                                                          op0=ALU.mult, op1=ALU.add))
                    src, dst, lo = dst, src, a0
                s0 = PAD + SEQ + 15
                seq.do(nc.vector.scalar_tensor_tensor(out=PD[:, e, 0:SEQ], in0=src[:, PAD:PAD + SEQ],
                                                      scalar=PARG[:, 3:4], in1=ex[:, PAD:PAD + SEQ],
                                                      op0=ALU.mult, op1=ALU.subtract))
                seq.do(nc.vector.scalar_tensor_tensor(out=PD[:, e, SEQ:T], in0=src[:, s0::16],
                                                      scalar=PARG[:, 3:4], in1=ex[:, s0::16],
                                                      op0=ALU.mult, op1=ALU.subtract))
                seq.do(nc.vector.tensor_tensor(FIX[:], src[:, PAD:2 * PAD], PARG[:, 4:4 + PAD], ALU.mult))
                nc.vector.tensor_tensor(PD[:, e, 0:PAD], FIX[:], ex[:, PAD:2 * PAD],
                                        ALU.subtract).then_inc(sem("pool_d"), 1)

            def gate_m(i, e):
                wait(dve, sem("y_ready"), 2 * i + e + 2)
                n, (h, slot) = tile_no(N_EVEN_IN, 10, i, 8 + e)
                a = A[:, bass.ds(AH + 2 * i + e, 1), :].rearrange("p a (b t) -> p (a b) t", b=2)
                nc.vector.tensor_scalar(a, X[:, 2:4, 0:HALF], PSG[:, e:e + 1], None, ALU.mult).then_inc(
                    sem("y_used"), 1)
                wait(dve, sem("y_used"), 2 * i + e + 2)
                wait(dve, evac[slot], h + 2)
                a = act_tile(AH + 2 * i + e)
                nc.vector.tensor_tensor(a, a, SZ[:], ALU.mult).then_inc(sem("z_used"), 1)

            dve.wait_ge(sem("xT_out"), 16)
            with dve.Fori(0, PG) as i:
                seq.loop(i, 2 + 14, 0)
                for c, (kind, e) in enumerate(EV):
                    nn, nhalf = tile_no(N_EVEN_IN, 10, i, c + 1)
                    split_lo(dve, nn, nhalf)
                    if kind == "u":
                        norm_v(i, e)
                    if kind == "za":
                        add_bias(i, e)
                        gate_a(i, e)
                    if kind == "p":
                        pool_chain(i, e)
                    if kind == "zb":
                        gate_m(i, e)
            assert seq.n == 16, seq.n
            split_act_dve(dve, 1)
            with dve.Fori(0, 8) as i:
                for c in range(2):
                    nn, nhalf = tile_no(N_EVEN_OUT, 2, i, c + 1)
                    n, (h, slot) = tile_no(N_EVEN_OUT, 2, i, c)
                    split_lo(dve, nn, nhalf)
                    wait(dve, mm_done, n + 3)
                    wait(dve, sem(f"res_landed{c}"), 16 * i + 16)
                    a = A[:, bass.ds(2 * i + c, 1), :].rearrange("p a (b t) -> p (a b) t", b=2)
                    nc.vector.tensor_tensor(a, mp(slot), two(XR[:, slot]), ALU.add).then_inc(evac[slot], 1)

            norm_dve(dve, 1, g_odd, 2)
            dve.sem_inc(sem("rows_read"), 1)
            dve.sem_inc(sem("h_ss"), 1)
            dve.sem_inc(sem("vm_used"), 1)

            def norm_head(m, kq, slot):
                wait(dve, sem("h_sq"), kq + 1)
                nc.vector.tensor_reduce(HS[:], SQ1[:], AX.X, ALU.add).then_inc(sem("h_ss"), 1)
                wait(dve, sem("h_rstd"), kq + 1)
                nc.vector.tensor_tensor(KN[:, slot], pad5(0), over(HR[:], P), ALU.mult).then_inc(
                    sem("rows_read"), 1)

            with dve.Fori(0, KV) as i:
                for c, (kind, col0, br) in enumerate(KVT):
                    nn, nhalf = tile_no(N_KV, 6, i, c + 1)
                    split_lo(dve, nn, nhalf)
                    for t_ in ([4, 5] if c == 5 else [c - 1] if c else []):
                        slot = t_ % 2
                        dve.wait_ge(sem("head_pads"), 4)
                        wait(dve, sem(f"rows_out{slot}"), 32 * (3 * i + t_ // 2) + 32)
                        if 2 <= t_ < 5:
                            wait(dve, sem("back_turned"), 3 * i + t_ - 1)
                        elif t_ == 5:
                            wait(dve, sem("vm_done"), i + 1)
                        if t_ < 3:
                            norm_head(6 * i + t_, 3 * i + t_, slot)
                        else:
                            wait(dve, sem("head_turned"), 6 * i + t_ + 3)
                            nc.vector.tensor_copy(KN[:, slot], pad5(0)).then_inc(sem("rows_read"), 1)
                            if t_ == 3:
                                wait(dve, sem("rows_read"), 6 * i + 5)
                                dve.sem_inc(sem("vc_rows"), 1)
                    if c == 2:
                        wait(dve, sem("back_turned"), 3 * i + 1)
                        nc.vector.tensor_reduce(KSUM[:], X[:, 2, :].rearrange("p (b t) -> p b t", t=64), AX.X,
                                                ALU.add).then_inc(sem("ksum"), 1)
                        wait(dve, sem("ksum"), i + 1)
                        dve.sem_inc(sem("back_used"), 1)
                        nc.vector.tensor_scalar(KM[:, bass.ds(i, 1), 0:8].rearrange("p a n -> p (a n)"), KSUM[:],
                                                1.0 / 64, None, ALU.mult).then_inc(sem("km_ready"), 1)
                wait(dve, sem("vm_done"), i + 1)
                nc.vector.tensor_copy(VM4[:, bass.ds(i, 1), :].rearrange("p a n -> p (a n)"), X[:, 3, 0:P]).then_inc(
                    sem("vm_used"), 1)
            for b in range(2):
                dve.wait_ge(sem(f"rows_out{b}"), 32 * 12 + 32)
            def q_norm(i, c):
                kq = 12 + 4 * i + c - 1
                wait(dve, sem("back_turned"), kq - 1)
                norm_head(24 + 4 * i + c - 1, kq, (c - 1) % 2)

            def q_dve(i, first):
                for c in range(REP):
                    nn, nhalf = tile_no(N_Q, REP, i, c + 1)
                    split_lo(dve, nn, nhalf)
                    if not first or c >= 1:
                        q_norm(i, c)

            q_dve(0, True)
            with dve.Fori(1, KV) as i:
                q_dve(i, False)
            split_lo(dve, N_Z + 1, ((N_Z + 1) // 2, 1))
            q_norm(KV, 0)
            split_lo(dve, N_Z + 2, ((N_Z + 2) // 2, 0))
            split_lo(dve, N_Z + 3, ((N_Z + 3) // 2, 1))
            split_lo(dve, N_Z + 4, ((N_Z + 4) // 2, 0))
            with dve.Fori(0, 2) as r:
                for c in range(6):
                    nn, nhalf = tile_no(N_Z + Z_FIRST, 6, r, c + 1)
                    split_lo(dve, nn, nhalf)
            dve.wait_ge(sem("back_used"), 29)
            nc.vector.tensor_scalar(QP[:, :, :, 0:REP],
                                    A[:, :, SEQ:T].rearrange("p (g h) s -> p s g h", g=KV), SCALE, None,
                                    ALU.mult).then_inc(sem("qp_ready"), 1)
            dve.wait_ge(sem("gates_turned"), 1)
            seq.base, seq.n = 16 * PG, 0
            dve.wait_ge(mm_done, N_GATE + 3)
            seq.do(nc.vector.memset(G8[:], 0.0))
            for b in range(3):
                nc.vector.tensor_copy(G8[:, b].rearrange("s (g n) -> s g n", g=KV)[:, :, 0:REP],
                                      X[0:NS, 1, 0:48].rearrange("s (g h b) -> s g h b", g=KV, h=REP)[:, :, :, b]
                                      ).then_inc(sem("gate8_ready"), 1)
            dve.wait_ge(sem("gates_turned"), 2)
            nc.vector.tensor_copy(GS[:], X[:, 1, P:P + 3 * NS].rearrange("p (b s) -> p b s", b=3)).then_inc(
                sem("gates_copied"), 1)

            xs = X[:, 0, 0:NS * 32].rearrange("p (s n) -> p s n", n=32)
            seq2 = Seq(dve, "dve_step", 16 * PG + 1)
            dve.wait_ge(sem("cs_done"), 1)
            seq2.do(nc.vector.tensor_reduce(CM[:], xs, AX.X, ALU.max))
            nc.vector.tensor_tensor(CE[:], xs, over(CM[:], 32), ALU.subtract).then_inc(sem("cs_shifted"), 1)
            dve.wait_ge(sem("cs_exp"), 1)
            seq2.do(nc.vector.tensor_reduce(CR[:], CE[:], AX.X, ALU.add))
            seq2.do(nc.vector.reciprocal(CR[:], CR[:]))
            nc.vector.tensor_tensor(CE[:], CE[:], over(CR[:], 32), ALU.mult).then_inc(sem("cp_ready"), 1)
            dve.wait_ge(sem("cp_ready"), 1)
            nc.vector.memset(CP[:], 0.0).then_inc(sem("cpad_ready"), 1)
            dve.wait_ge(sem("cpad_ready"), 1)
            for it in range(4):
                r, hf = it // 2, it % 2
                nc.vector.tensor_copy(CP[:, it, :, 0:16], CE[:, 4 * r:4 * r + 4, 16 * hf:16 * hf + 16]).then_inc(
                    sem("cpad_ready"), 1)
            dve.wait_ge(sem("imp_done"), 1)
            nc.vector.tensor_copy(IMP[:], X[0:32, 1, 0:32]).then_inc(sem("imp_copied"), 1)
            dve.wait_ge(sem("cpt_turned"), 1)
            nc.vector.tensor_copy(CPT[:].rearrange("p i n -> p (i n)"), X[:, 2, :]).then_inc(sem("cpt_ready"), 1)
            dve.wait_ge(sem("imp_copied"), 1)
            dve.wait_ge(sem("cmp_consts"), 64)
            v_j = IMP[:, 1:31].unsqueeze(1).to_broadcast([32, 30, 30])
            v_i = IMP[:, 1:31].unsqueeze(2).to_broadcast([32, 30, 30])
            bef = BEF[0:32].rearrange("p (i j) -> p i j", j=30)
            seq2.do(nc.vector.memset(LOW[:], 0.0))
            seq2.do(nc.vector.tensor_tensor(RK1[:], v_j, v_i, ALU.is_gt))
            seq2.do(nc.vector.tensor_tensor(RK2[:], v_j, v_i, ALU.is_equal))
            seq2.do(nc.vector.tensor_tensor(RK2[:], RK2[:], bef, ALU.mult))
            seq2.do(nc.vector.tensor_tensor(RK1[:], RK1[:], RK2[:], ALU.add))
            seq2.do(nc.vector.tensor_reduce(RNK[:], RK1[:], AX.X, ALU.add))
            nc.vector.tensor_scalar(LOW[:, 1:31], RNK[:], NSEL_FREE - 0.5, None, ALU.is_ge).then_inc(
                sem("low_ready"), 1)
            dve.wait_ge(sem("oc_done"), 1)
            dve.wait_ge(sem("gates_copied"), 2)
            for s4 in range(4):
                nc.vector.tensor_tensor(OC[:, s4::4, :], X[:, s4, 0:2 * P].rearrange("p (r n) -> p r n", r=2),
                                        over(GS[:, 0, s4::4], P), ALU.mult).then_inc(sem("oc_ready"), 1)
            dve.wait_ge(sem("low_spread"), 1)
            seq2.do(nc.vector.tensor_scalar(SBIAS[:].rearrange("p s n -> p (s n)"), X[:, 0, 0:NS * 32], NEG, None,
                                            ALU.mult))
            dve.sem_inc(sem("bias_ready"), 1)

            dve.sem_inc(sem("sel_read"), 4)
            dve.sem_inc(sem("os_done"), 1)
            dve.sem_inc(sem("o_rows"), 1)
            seq4 = Seq(dve, "dve_step", 0)
            SEQ4 = 16 * PG + 1 + 10

            def sample_softmax(i, first):
                s_i = slice(i, i + 1) if isinstance(i, int) else bass.ds(i, 1)
                nc.vector.tensor_copy(QS[:], QP[:, s_i].rearrange("p a g n -> p (a g) n")).then_inc(
                    sem("q_static"), 1)
                wait(dve, sem("new_scored"), i + 2)
                if not first:
                    wait(dve, sem("p_turned"), 6 * i)
                seq4.do(nc.vector.tensor_copy(SC[:, PAGES * P:PAGES * P + 1], MP[:, 0, 1, 8:9]))
                wait(dve, sem("sc_done"), 5 * i + 2)
                nc.vector.tensor_reduce(SST[:, 0:1], X[:, 2, :], AX.X, ALU.max, negate=True).then_inc(
                    sem("win_max"), 1)
                for b in range(1, 5):
                    wait(dve, sem("sc_done"), 5 * i + b + 2)
                    sb_ = SBIAS[:, s_i, 8 * (b - 1):8 * b].rearrange("p a n -> p (a n)")
                    nc.vector.tensor_tensor(SC[:, (b - 1) * 512:b * 512].rearrange("p (n t) -> p n t", t=64),
                                            X[:, 2 + b % 2, :].rearrange("p (n t) -> p n t", t=64),
                                            over(sb_, 64), ALU.add).then_inc(sem("sel_read"), 1)
                wait(dve, sem("sel_read"), 4 * i + 8)
                nc.vector.tensor_reduce(SST[:, 2:3], SC[:], AX.X, ALU.max, negate=True).then_inc(sem("sel_max"), 1)

            def sample_rows(i, i1):
                s_1 = slice(i1, i1 + 1) if isinstance(i1, int) else bass.ds(i1, 1)
                wait(dve, sem("pv_done"), 4 * i + 4)
                seq4.do(nc.vector.scalar_tensor_tensor(out=OSM[:, 0], in0=MP[:, 0, 0, 0:P], scalar=SST[:, 7:8],
                                                       in1=OC[:, s_1, :].rearrange("p a n -> p (a n)"),
                                                       op0=ALU.mult, op1=ALU.add))
                nc.vector.scalar_tensor_tensor(out=OSM[:, 1], in0=MP[:, 0, 0, P:2 * P], scalar=SST[:, 6:7],
                                               in1=OSM[:, 0], op0=ALU.mult, op1=ALU.add).then_inc(sem("o_rows"), 1)

            def sample_weights(i):
                s_i = slice(i, i + 1) if isinstance(i, int) else bass.ds(i, 1)
                for q in range(6):
                    wait(dve, sem("p_turned"), 6 * i + q + 1)
                    if q == 0:
                        ins = nc.vector.tensor_copy(WPT[:].rearrange("p t n -> p (t n)"), MP[:, 1, 0, :])
                    elif q < 5:
                        ins = nc.vector.tensor_copy(SPT[:, 4 * (q - 1):4 * q, :].rearrange("p t n -> p (t n)"),
                                                    MP[:, 1, q % 2, :])
                    else:
                        ins = nc.vector.tensor_copy(SPT[0:1, PAGES, :], MP[0:1, 0, 1, P:2 * P])
                    ins.then_inc(sem("p_evac"), 1)
                wait(dve, sem("sel_exp"), i + 1)
                seq4.do(nc.vector.reciprocal(SST[:, 4:6], SST[:, 1:4:2]))
                seq4.do(nc.vector.tensor_tensor(SST[:, 6:7], SST[:, 4:5], GS[:, 2, s_i], ALU.mult))
                seq4.do(nc.vector.tensor_tensor(SST[:, 7:8], SST[:, 5:6], GS[:, 1, s_i], ALU.mult))

            def sample_store(i, i1):
                wait(dve, sem("o_turned"), i)
                nc.vector.tensor_copy(A[:, :, bass.ds(SEQ + i1, 1)].rearrange("p (g h) a -> p g (h a)", g=KV),
                                      MP[:, 0, 1, 2 * P:3 * P].rearrange("p (g n) -> p g n", g=KV)[:, :, 0:REP]
                                      ).then_inc(sem("os_done"), 1)

            seq4.base = SEQ4
            sample_softmax(0, True)
            sample_weights(0)
            with dve.Fori(1, NS) as i:
                seq4.loop(i, 5, SEQ4 - 1)
                sample_softmax(i, False)
                sample_rows(i, i - 1)
                sample_weights(i)
                sample_store(i, i - 1)
            seq4.base, seq4.n = SEQ4 + 4 + 5 * (NS - 1), 0
            sample_rows(NS, NS - 1)
            sample_store(NS, NS - 1)

            dve.wait_ge(sem("os_done"), NS + 1)
            dve.wait_ge(sem("attn_consts"), 48)
            nc.vector.tensor_copy(CAB[:], CAU[:]).then_inc(sem("attn_ready"), 1)
            nc.vector.tensor_copy(IDB[:], ident[:]).then_inc(sem("attn_ready"), 1)
            seq5 = Seq(dve, "dve_step", SEQ4 + 5 * NS)
            seq5.do(nc.vector.memset(CPP[:], 0.0))
            dve.sem_inc(sem("p4_scaled"), 8)
            dve.sem_inc(sem("o_used"), 2)
            with dve.Fori(0, KV) as i:
                seq5.loop(i, 7 + 31 + 4, SEQ4 + 5 * NS + 1)
                wait(dve, sem("pv4"), 8 * i + 2)

                def queries(e):
                    nc.vector.tensor_scalar(QC[:, e], act_tile(4 * i + e)[:, 0:SEQ], SCALE, None, ALU.mult).then_inc(
                        sem("qc_ready"), 1)

                cx = CX[:].rearrange("p j e n -> p (j e) n")
                cm, cs_ = CMX[:].rearrange("p j e -> p (j e)"), CSM[:].rearrange("p j e -> p (j e)")

                def cmp_rows():
                    wait(dve, sem("c4_scored"), i + 1)
                    nc.vector.tensor_copy(CS[:], MP[:, 1, 1, :]).then_inc(sem("c4_rows"), 1)

                def cmp_shift():
                    wait(dve, sem("c4_turned"), i + 1)
                    x1 = MP[:, 1, 1, :].rearrange("p (q n) -> p q n", n=32)[:, :, 0:8]
                    seq5.do(nc.vector.tensor_tensor(cx, x1, CBI[:].rearrange("p j e n -> p (j e) n"), ALU.add))
                    seq5.do(nc.vector.tensor_reduce(cm, cx, AX.X, ALU.max))
                    nc.vector.tensor_tensor(cx, cx, over(cm, 8), ALU.subtract).then_inc(sem("c4_shifted"), 1)

                def cmp_probs():
                    wait(dve, sem("c4_exp"), i + 1)
                    seq5.do(nc.vector.tensor_reduce(cs_, cx, AX.X, ALU.add))
                    seq5.do(nc.vector.reciprocal(cs_, cs_))
                    g0 = GT[:, :, bass.ds(12 * i, 12)].rearrange("p j (e b) -> p j e b", b=3)[:, :, :, 0]
                    seq5.do(nc.vector.tensor_tensor(CSM[:], CSM[:], g0, ALU.mult))
                    seq5.do(nc.vector.tensor_tensor(cx, cx, over(cs_, 8), ALU.mult))
                    nc.vector.tensor_tensor(CPP[:].rearrange("p j e n -> p (j e) n")[:, :, 0:8], cx,
                                            COK[:].rearrange("p j e n -> p (j e) n"), ALU.mult).then_inc(
                        sem("c4_probs"), 1)

                def cmp_back():
                    wait(dve, sem("c4_back"), i + 1)
                    nc.vector.tensor_copy(CPX[:], MP[:, 1, 1, :]).then_inc(sem("c4_probs_t"), 1)

                queries(0)

                def max4(w):
                    j = w % 4
                    wait(dve, sem("s4_done"), 32 * i + w + 1)
                    nc.vector.tensor_reduce(AMX[:, w % 8:w % 8 + 1], X[:, w % 4, 0:(j + 1) * P], AX.X, ALU.max,
                                            negate=True).then_inc(sem("max4"), 1)

                max4(0)
                max4(1)
                for w in range(32):
                    e, br, j = w // 8, (w // 4) % 2, w % 4
                    if w + 2 < 32:
                        max4(w + 2)
                    wait(dve, sem("p4_exp"), 32 * i + w + 5)
                    seq5.do(nc.vector.reciprocal(AW[:, w % 8:w % 8 + 1], ASM[:, w % 8:w % 8 + 1]))
                    nc.vector.tensor_scalar(PR[:, w % 4, 0:(j + 1) * P], PR[:, w % 4, 0:(j + 1) * P],
                                            AW[:, w % 8:w % 8 + 1], GT[:, j, bass.ds(12 * i + 3 * e + 1 + br, 1)],
                                            ALU.mult, ALU.mult).then_inc(sem("p4_scaled"), 1)
                    if w < 3:
                        queries(w + 1)
                    if w == 4:
                        cmp_rows()
                    if w == 7:
                        cmp_shift()
                    if w == 9:
                        cmp_probs()
                    if w == 11:
                        cmp_back()
                    for e2 in ([e - 1] if w % 8 == 5 and e >= 1 else []) + ([3] if w == 31 else []):
                        wait(dve, sem("o_done"), 4 * i + e2 + 2)
                        wait(dve, sem(f"sz_landed{e2 % 2}"), 32 * i + 16 * (e2 // 2) + 16)
                        a = A[:, bass.ds(4 * i + e2, 1), :].rearrange("p a t -> p (a t)")
                        seq5.do(nc.vector.tensor_tensor(a[:, SEQ:T], a[:, SEQ:T], SZH[:, e2 % 2, SEQ:T], ALU.mult))
                        nc.vector.tensor_tensor(a[:, 0:SEQ], MP[:, 1, e2 % 2, :], SZH[:, e2 % 2, 0:SEQ],
                                                ALU.mult).then_inc(sem("o_used"), 1)
                assert seq5.n == 42, seq5.n

            dve.sem_inc(held, 1)
            split_lo(dve, N_ODD_OUT, (N_ODD_OUT // 2, N_ODD_OUT % 2))
            split_act_dve(dve, 3)

            def out_dve(i, last):
                for c in range(2):
                    n, (h, slot) = tile_no(N_ODD_OUT, 2, i, c)
                    nn, nhalf = tile_no(N_ODD_OUT, 2, i, c + 1)
                    if not (last and c == 1):
                        split_lo(dve, nn, nhalf)
                    wait(dve, mm_done, n + 3)
                    wait(dve, sem(f"res_landed{slot}"), 128 + 16 * i + 16)
                    wait(dve, sem("y_turned"), 2 * i + c + 1)
                    nc.vector.tensor_tensor(two(YT[:, slot]), mp(slot), two(XR[:, slot]), ALU.add).then_inc(
                        evac[slot], 1)

            with dve.Fori(0, 7) as i:
                out_dve(i, False)
            out_dve(7, True)

        @block.gpsimd
        def _(pool):
            pseq = Seq(pool, "pool_step")
            nc.gpsimd.memset(eps_t[:], EPS).then_inc(sem("pads"), 1)
            nc.gpsimd.memset(mhalf[:], -0.5).then_inc(sem("pads"), 1)
            nc.gpsimd.dma_start(STR[:], I["state_pool"].rearrange("s r c -> (s r) c")).then_inc(
                sem("raw_landed"), 16)
            nc.gpsimd.dma_start(WSR[:], I["w_spatial"].rearrange("h i j -> i h j")).then_inc(
                sem("raw_landed"), 16)
            loads = [(ones[:], cst("ones")), (TRIL[:], cst("tril_t")), (DI8[:], cst("diag8")),
                     (PAR[:], cst("pool").rearrange("p (g n) -> p g n", g=PG)),
                     (g_even[:], I["norm_even"].rearrange("(k p) -> p k", p=P)),
                     (g_odd[:], I["norm_odd"].rearrange("(k p) -> p k", p=P)),
                     (VG[:], I["v_norm"].partition_broadcast(P)),
                     (BS[:], I["b_spatial"].rearrange("h i -> (h i)").partition_broadcast(P)),
                     (W00[:], I["w_spatial"][:, 0, 0].partition_broadcast(P)),
                     (PSC[:], I["pool_scale"].rearrange("(g e p) -> p g e", g=PG, p=P))]
            loads += [(WP[:, g], I["w_pool"][g].rearrange("(c p) e -> p c e", p=P)) for g in range(PG)]
            with nc.allow_non_contiguous_dma(reason="a few parameters, one element per row"):
                for dst, src in loads:
                    nc.gpsimd.dma_start(dst, src).then_inc(sem("setup"), 16)
            assert SETUP == 16 * len(loads)
            for lo, hi, s_ in ((0, 2, "gv_out"), (2, 5, "tail_out"), (5, 8, "tail_out")):
                nc.gpsimd.dma_start(O["pool_sample"][lo:hi, 0:PAD - 1, :], I["state_pool"][lo:hi, 1:PAD, :]).then_inc(
                    sem(s_), 16)
            pool.wait_ge(sem("x_evac0"), 9)
            pool.wait_ge(sem("x_evac1"), 9)
            nc.gpsimd.dma_start(xT_scr.rearrange("k p t -> p k t"), A[:]).then_inc(sem("xT_out"), 16)
            pool.wait_ge(sem("lo_done"), KT)
            pool.wait_ge(sem("x_evac0"), 12)
            nc.gpsimd.memset(VT[:, T:TP], 0.0).then_inc(sem("pads"), 1)
            for e in range(2):
                nc.gpsimd.memset(EX[e][:, 0:PAD], 0.0).then_inc(sem("pads"), 1)
            pool.wait_ge(sem("pads"), 5)

            with pool.Fori(0, PG) as i:
                pseq.loop(i, 2, 0)
                wait(pool, sem("y_ready"), 2 * i + 1)
                wait(pool, sem("y_used"), 2 * i + 1)
                wait(pool, sem("pool_d"), 2 * i + 2)
                nc.gpsimd.tensor_copy(PARG[:], PAR[:, bass.ds(i, 1), :].rearrange("p a n -> p (a n)")).then_inc(
                    sem("group_ready"), 1)
                nc.gpsimd.tensor_copy(PSG[:], PSC[:, bass.ds(i, 1), :].rearrange("p a n -> p (a n)")).then_inc(
                    sem("group_ready"), 1)
                nc.gpsimd.tensor_copy(WPG[:], WP[:, bass.ds(i, 1)].rearrange("p a c e -> p (a c) e")).then_inc(
                    sem("group_ready"), 1)
                for e in range(2):
                    wait(pool, sem("tail_turned"), 2 * i + e + 1)
                    hist = EX[e][:, PAD + SEQ:EXT].rearrange("p (s r) -> p s r", r=16)[:, :, 0:PAD]
                    nc.gpsimd.tensor_copy(hist, STP[:, bass.ds(2 * i + e, 1), :].rearrange(
                        "p a (s r) -> p (a s) r", r=PAD)).then_inc(sem("hist_ready"), 1)
                for e in range(2):
                    wait(pool, sem("v_ss"), 2 * i + e + 2)
                    pseq.do(nc.gpsimd.tensor_scalar(SR[:], SS[:], 1.0 / P, EPS, ALU.mult, ALU.add))
                    nc.gpsimd.tensor_tensor(SR[:], SR[:], mhalf[:, 0:5], ALU.pow).then_inc(sem("v_rstd"), 1)
                    wait(pool, sem("v_mul"), 2 * i + e + 1)
                    vg = VG[:, bass.ds((2 * i + e) * P, P)].unsqueeze(1).to_broadcast([P, 5, P])
                    nc.gpsimd.tensor_tensor(VN[:], VN[:], vg, ALU.mult).then_inc(sem("v_ready"), 1)
                    col = nc.gpsimd.snap((2 * i + e) * P, min_val=0, max_val=1024 - P)
                    wait(pool, sem("v_ready"), 2 * i + e + 1)
                    nc.gpsimd.dma_start(O["gmlp_v_sample"][:, bass.ds(col, P)], VN[0:NS, 4, :]).then_inc(
                        sem("gv_out"), 16)
                for e in range(2):
                    col = nc.gpsimd.snap((2 * i + e) * P, min_val=0, max_val=1024 - P)
                    wait(pool, sem("tail_copied"), 2 * i + e + 2)
                    wait(pool, sem("tail_first"), 2 * i + e + 1)
                    nc.gpsimd.dma_start(O["pool_prompt"][:, bass.ds(col, P)], TLP[:]).then_inc(sem("tail_out"), 16)
                    nc.gpsimd.dma_start(O["pool_sample"][:, PAD - 1, bass.ds(col, P)], TLS[:]).then_inc(
                        sem("tail_out"), 16)
            with pool.Fori(0, 8) as i:
                for c in range(2):
                    n, (h, slot) = tile_no(N_EVEN_OUT, 2, i, c)
                    kt = nc.gpsimd.snap(2 * i + c, min_val=0, max_val=KT - 1)
                    wait(pool, evac[slot], h + 2)
                    nc.gpsimd.dma_start(x1_scr[bass.ds(kt, 1)].rearrange("a p t -> p (a t)"),
                                        act_tile(2 * i + c)).then_inc(sem("x1_out"), 16)

            pool.wait_ge(sem("y_used"), 9)
            pool.wait_ge(sem("tail_out"), 32 + 32 * AH)
            pool.wait_ge(evac[0], 29)
            nc.gpsimd.dma_start(GQ[:, 0], I["q_norm"][0].partition_broadcast(P)).then_inc(sem("rows_out0"), 16)
            nc.gpsimd.dma_start(GQ[:, 1:4].rearrange("p a n -> p (a n)"), I["k_norm"].rearrange(
                "a n -> (a n)").partition_broadcast(P)).then_inc(sem("rows_out0"), 16)
            nc.gpsimd.dma_start(COS[:].rearrange("p j n -> p (j n)"), cst("cos")).then_inc(sem("rows_out1"), 16)
            nc.gpsimd.dma_start(SIN[:].rearrange("p j n -> p (j n)"), cst("sin")).then_inc(sem("rows_out1"), 16)
            pool.wait_ge(sem("lo_done"), 3 * KT)
            nc.gpsimd.dma_start(VMASK[:].rearrange("p j n -> p (j n)"), cst("prompt_blocks")).then_inc(
                sem("setup"), 16)
            nc.gpsimd.memset(KTT[:, :, T:TP], 0.0).then_inc(sem("head_pads"), 1)
            nc.gpsimd.memset(KM[:], 0.0).then_inc(sem("head_pads"), 1)
            nc.gpsimd.memset(QP[:], 0.0).then_inc(sem("head_pads"), 1)
            pool.wait_ge(sem("setup"), SETUP + 16)
            for b in range(2):
                pool.wait_ge(sem(f"rows_out{b}"), 32)
            pool.sem_inc(sem("head_pads"), 1)
            pseq2 = Seq(pool, "pool_step", 0)

            def finish_head(kq, slot, gain):
                wait(pool, sem("h_ss"), kq + 2)
                pseq2.do(nc.gpsimd.tensor_scalar(HR[:], HS[:], 1.0 / P, EPS, ALU.mult, ALU.add))
                nc.gpsimd.tensor_tensor(HR[:], HR[:], mhalf[:, 0:5], ALU.pow).then_inc(sem("h_rstd"), 1)

            def rotate(m, kq, slot, gain):
                wait(pool, sem("rows_read"), m + 2)
                kn = KN[:, slot]
                pseq2.do(nc.gpsimd.tensor_tensor(kn, kn, GQ[:, gain].unsqueeze(1).to_broadcast([P, 5, P]), ALU.mult))
                x1, x2 = kn[:, :, 0:16], kn[:, :, 16:32]
                pseq2.do(nc.gpsimd.tensor_tensor(RA[:, :, 0:16], x1, COS[:], ALU.mult))
                pseq2.do(nc.gpsimd.tensor_tensor(RA[:, :, 16:32], x2, COS[:], ALU.mult))
                pseq2.do(nc.gpsimd.tensor_tensor(RB[:, :, 0:16], x2, SIN[:], ALU.mult))
                pseq2.do(nc.gpsimd.tensor_tensor(RB[:, :, 16:32], x1, SIN[:], ALU.mult))
                pseq2.do(nc.gpsimd.tensor_tensor(x1, RA[:, :, 0:16], RB[:, :, 0:16], ALU.subtract))
                pseq2.do(nc.gpsimd.tensor_tensor(x2, RA[:, :, 16:32], RB[:, :, 16:32], ALU.add))
                pool.sem_inc(sem("rows_ready"), 1)

            with pool.Fori(0, KV) as i:
                pseq2.loop(i, 8 * 3, 8)
                for c, (kind, col0, br) in enumerate(KVT):
                    slot = c % 2
                    if c < 3:
                        finish_head(3 * i + c, slot, 1 + br)
                        rotate(6 * i + c, 3 * i + c, slot, 1 + br)
                    else:
                        wait(pool, sem("rows_read"), 6 * i + c + 2)
                    col = nc.gpsimd.snap((0 if c < 3 else 512) + i * P, min_val=0, max_val=1024 - P)
                    nc.gpsimd.dma_start(kv_p[br].rearrange("(j p) c -> p j c", p=P)[:, :, bass.ds(col, P)],
                                        KN[:, slot, 0:TT, :]).then_inc(sem(f"rows_out{slot}"), 16)
                    dst = kv_s[br] if br < 2 else kv_s[2][:, 511, :]
                    nc.gpsimd.dma_start(dst[:, bass.ds(col, P)], KN[0:NS, slot, 4, :]).then_inc(
                        sem(f"rows_out{slot}"), 16)
            with pool.Fori(0, KV) as i:
                pseq2.loop(i, 8 * 4, 104)
                for e in range(REP):
                    finish_head(12 + 4 * i + e, e % 2, 0)
                    rotate(24 + 4 * i + e, 12 + 4 * i + e, e % 2, 0)

            pool.wait_ge(sem("table_landed"), 16)
            pool.wait_ge(sem("back_used"), 29)
            with pool.Fori(0, 2) as r:
                for hf in range(2):
                    for c in range(8):
                        wait(pool, sem("pages_used"), 32 * r + 16 * hf + 2 * c + 2)
                        for s4 in range(4):
                            page = page_at(nc.gpsimd, "cache_cmp_kv", 64 * r + 16 * s4 + 8 * hf + c)
                            nc.gpsimd.dma_start(PGT[c % 2][:, 1, s4], page[:, 512:1024]).then_inc(
                                sem(f"values_landed{c % 2}"), 16)

            pool.wait_ge(sem("bias_ready"), 1)
            pool.wait_ge(sem("table_landed"), 16)
            for b in range(2):
                pool.wait_ge(sem(f"rows_out{b}"), 32 * 12 + 32)

            def value_loads(i, pages):
                smp = i if isinstance(i, int) else nc.gpsimd.snap(i, min_val=0, max_val=NS - 1)
                for j in range(pages):
                    page = page_at(nc.gpsimd, "cache_sel_kv", PAGES * i + j)
                    if j % 4 == 0:
                        wait(pool, sem("pv_done"), 4 * i + j // 4 + 1)
                    nc.gpsimd.dma_start(SV[:, j], page[:, 512:1024]).then_inc(sem("vals_landed"), 16)
                wait(pool, sem("pv_done"), 4 * i + 4)
                nc.gpsimd.dma_start(NRV[:], O["sel_kv_sample"][bass.ds(smp, 1), 512:1024]).then_inc(
                    sem("vals_landed"), 16)
                window_half(nc.gpsimd, smp, KWV, 512, sem("vals_landed"))

            with pool.Fori(0, NS - 1) as i:
                value_loads(i, PAGES)
            value_loads(NS - 1, PAGES // 2)

            pool.wait_ge(sem("os_done"), NS + 1)
            with pool.Fori(0, KV) as i:
                vcol = nc.gpsimd.snap(512 + i * P, min_val=512, max_val=1024 - P)
                wait(pool, sem("o_done"), 4 * i + 1)
                for br in range(2):
                    nc.gpsimd.dma_start(VB[:, br], kv_p[1 + br].rearrange("(j p) c -> p j c", p=P)[
                        :, :, bass.ds(vcol, P)]).then_inc(sem("vals_landed"), 16)
                nc.gpsimd.tensor_copy(KMG[:], KM[:, bass.ds(i, 1), :].rearrange("p a n -> p (a n)")).then_inc(
                    sem("group_static"), 1)
                nc.gpsimd.tensor_copy(VMG[:], VM4[:, bass.ds(i, 1), :].rearrange("p a n -> p (a n)")).then_inc(
                    sem("group_static"), 1)
                pool.sem_inc(held, 1)

NPHYS = 160
SETUP = 16 * 14


def kernel(**inputs):
    import concourse.bacc as bacc
    from concourse.bass_utils import run_bass_kernel_spmd

    nc = bacc.Bacc("TRN2", target_bir_lowering=False, num_devices=1)
    views = {
        "x_prompt": (SEQ, D), "x_sample": (NS, D), "cache_cmp_kv": (-1, P, 1024), "cache_sel_kv": (-1, P, 1024),
        "state_win_kv": (NS, 512, 1024), "state_pool": (NS, PAD, 1024), "page_table": (1, NS * PAGES),
        "norm_even": (D,), "w_in_even": (D, 5120), "v_norm": (1024,), "w_spatial": (AH, P, P),
        "b_spatial": (AH, P), "w_pool": (PG, 256, 256), "pool_scale": (1024,), "w_out_even": (D, D),
        "norm_odd": (D,), "w_in_odd": (D, 7216), "q_norm": (1, P), "k_norm": (3, P), "w_out_odd": (D, D),
    }
    arrays = {name: np.ascontiguousarray(inputs[name]).reshape(shape) for name, shape in views.items()}
    arrays["consts"] = _lay_consts()
    I = {name: nc.dram_tensor(name, a.shape, mybir.dt.from_np(a.dtype), kind="ExternalInput").ap()
         for name, a in arrays.items()}
    outs = [("y_prompt", (SEQ, D)), ("y_sample", (NS, D)),
            ("cmp_kv_prompt", (SEQ, 1024)), ("cmp_kv_sample", (NS, 1024)),
            ("sel_kv_prompt", (SEQ, 1024)), ("sel_kv_sample", (NS, 1024)),
            ("win_kv_prompt", (SEQ, 1024)), ("win_kv_sample", (NS, 512, 1024)),
            ("pool_prompt", (PAD, 1024)), ("pool_sample", (NS, PAD, 1024)), ("gmlp_v_sample", (NS, 1024))]
    O = {name: nc.dram_tensor(name + "_out", shape, F32, kind="ExternalOutput").ap() for name, shape in outs}
    xT_scr = nc.dram_tensor("xT_scr", (KT, P, T), F32, kind="Internal").ap()
    x1_scr = nc.dram_tensor("x1_scr", (KT, P, T), F32, kind="Internal").ap()
    szT_scr = nc.dram_tensor("szT_scr", (KT, P, T), F32, kind="Internal").ap()
    means_scr = nc.dram_tensor("means_scr", (4, P, 1024), F32, kind="Internal").ap()
    build(nc, I, O, xT_scr, x1_scr, szT_scr, means_scr)
    r = run_bass_kernel_spmd(nc, [arrays], core_ids=[0]).results[0]
    shapes = {"y_prompt": (1, SEQ, D), "y_sample": (NS, 1, D), "pool_prompt": (1, 1, PAD, 1024),
              "pool_sample": (1, NS, PAD, 1024), "gmlp_v_sample": (1, NS, 1, 1024),
              "cmp_kv_prompt": (1, 1, SEQ, 2, KV, HD), "cmp_kv_sample": (1, NS, 1, 2, KV, HD),
              "sel_kv_prompt": (1, 1, SEQ, 2, KV, HD), "sel_kv_sample": (1, NS, 1, 2, KV, HD),
              "win_kv_prompt": (1, 1, SEQ, 2, KV, HD), "win_kv_sample": (1, NS, 512, 2, KV, HD)}
    return tuple(r[name + "_out"].reshape(shapes[name]) if name in shapes else r[name + "_out"] for name, _ in outs)
```
